# Optimizing a Trainium2 kernel written in Bass

```python
import math
import jax, jax.numpy as jnp
from jax import lax
import numpy as np

D_MODEL = 1024
BATCH = 1
SEQ = 256
DEPTH = 2

CTX_LEN = 256
GRID_W = 64

MLA_HEADS = 8
QK_NOPE_DIM = 64
QK_ROPE_DIM = 32
QK_HEAD_DIM = QK_NOPE_DIM + QK_ROPE_DIM
V_HEAD_DIM = 64
Q_LORA_RANK = 256
KV_LORA_RANK = 128
MLA_OUT = MLA_HEADS * V_HEAD_DIM

CONV_DIM = 512
CONV_K = 3

IN_SPLITS = [Q_LORA_RANK,
             Q_LORA_RANK + KV_LORA_RANK,
             Q_LORA_RANK + KV_LORA_RANK + QK_ROPE_DIM,
             Q_LORA_RANK + KV_LORA_RANK + QK_ROPE_DIM + CONV_DIM,
             Q_LORA_RANK + KV_LORA_RANK + QK_ROPE_DIM + 2 * CONV_DIM]
D_IN = Q_LORA_RANK + KV_LORA_RANK + QK_ROPE_DIM + 3 * CONV_DIM
KV_COL_START = Q_LORA_RANK
KV_COL_END = Q_LORA_RANK + KV_LORA_RANK + QK_ROPE_DIM
MIX_WIDTH = MLA_OUT + CONV_DIM

D_FF = 2816
N_MOD = 9
ROPE_BASE = 10000.0
EPS = 1e-6
Q_BLOCK = 128
ATTN_SCALE = 1.0 / math.sqrt(QK_HEAD_DIM)


def rmsnorm(x, w):
    x32 = x.astype(jnp.float32)
    r = lax.rsqrt(jnp.mean(x32 * x32, axis=-1, keepdims=True) + EPS)
    return (x32 * r).astype(x.dtype) * w

def modulate(h, shift, scale):
    return h * (1 + scale) + shift

def swiglu(h, w_i, w_o):
    g, u = jnp.split(h @ w_i, 2, axis=-1)
    return (jax.nn.silu(g) * u) @ w_o

def axial_rope_tables(rows, dtype):
    t = jnp.arange(rows * GRID_W)
    row = (t // GRID_W).astype(jnp.float32)
    col = (t % GRID_W).astype(jnp.float32)
    d_axis = QK_ROPE_DIM // 2
    inv = ROPE_BASE ** (-jnp.arange(0, d_axis, 2, dtype=jnp.float32) / d_axis)
    ar = row[:, None] * inv
    ac = col[:, None] * inv
    return tuple(a.astype(dtype) for a in (jnp.cos(ar), jnp.sin(ar), jnp.cos(ac), jnp.sin(ac)))

def rotate(x, cos, sin):
    x1, x2 = jnp.split(x, 2, axis=-1)
    return jnp.concatenate([x1 * cos - x2 * sin, x2 * cos + x1 * sin], axis=-1)

def axial_rope(x, tabs):
    cr, sr, cc, sc = tabs
    xr, xc = jnp.split(x, 2, axis=-1)
    return jnp.concatenate([rotate(xr, cr, sr), rotate(xc, cc, sc)], axis=-1)

def attend(q, k, v):
    s = jnp.einsum('bqhd,bkhd->bhqk', q, k, preferred_element_type=jnp.float32) * ATTN_SCALE
    p = jax.nn.softmax(s, axis=-1).astype(v.dtype)
    return jnp.einsum('bhqk,bkhd->bqhd', p, v)

def blocked_attend(q, k, v):
    b, l, h, d = q.shape
    nb = l // Q_BLOCK
    qb = q.reshape(b, nb, Q_BLOCK, h, d).transpose(1, 0, 2, 3, 4)
    ob = lax.map(lambda qi: attend(qi, k, v), qb)
    return ob.transpose(1, 0, 2, 3, 4).reshape(b, l, h, v.shape[-1])

def mla_queries(cq, q_norm_w, w_uq, tabs):
    b, l, _ = cq.shape
    q = (rmsnorm(cq, q_norm_w) @ w_uq).reshape(b, l, MLA_HEADS, QK_HEAD_DIM)
    q_nope, q_pe = q[..., :QK_NOPE_DIM], q[..., QK_NOPE_DIM:]
    if tabs is not None:
        q_pe = axial_rope(q_pe, tuple(t[:, None, :] for t in tabs))
    return jnp.concatenate([q_nope, q_pe], axis=-1)

def mla_keys_values(ckv, k_pe, kv_norm_w, w_ukv, tabs):
    b, l, _ = ckv.shape
    kv = (rmsnorm(ckv, kv_norm_w) @ w_ukv).reshape(b, l, MLA_HEADS, QK_NOPE_DIM + V_HEAD_DIM)
    k_nope, v = kv[..., :QK_NOPE_DIM], kv[..., QK_NOPE_DIM:]
    if tabs is not None:
        k_pe = axial_rope(k_pe, tabs)
    k_pe = jnp.broadcast_to(k_pe[:, :, None, :], (b, l, MLA_HEADS, QK_ROPE_DIM))
    return jnp.concatenate([k_nope, k_pe], axis=-1), v

def short_conv(u, w):
    up = jnp.pad(u, ((0, 0), (1, 1), (0, 0)))
    return up[:, :-2] * w[0] + up[:, 1:-1] * w[1] + up[:, 2:] * w[2]

def token_mixer(hl, hc, w_in, q_norm_w, kv_norm_w, w_uq, w_ukv, conv_w, w_out, tabs, ctx_out):
    b, l, _ = hl.shape
    cq_l, ckv_l, kpe_l, gb_l, gc_l, xv_l = jnp.split(hl @ w_in, IN_SPLITS, axis=-1)
    if ctx_out:
        cq_c, ckv_c, kpe_c, gb_c, gc_c, xv_c = jnp.split(hc @ w_in, IN_SPLITS, axis=-1)
    else:
        ckv_c, kpe_c = jnp.split(hc @ w_in[:, KV_COL_START:KV_COL_END], [KV_LORA_RANK], axis=-1)
    k_c, v_c = mla_keys_values(ckv_c, kpe_c, kv_norm_w, w_ukv, None)
    k_l, v_l = mla_keys_values(ckv_l, kpe_l, kv_norm_w, w_ukv, tabs)
    q_l = mla_queries(cq_l, q_norm_w, w_uq, tabs)
    k_all = jnp.concatenate([k_c, k_l], axis=1)
    v_all = jnp.concatenate([v_c, v_l], axis=1)
    att_l = blocked_attend(q_l, k_all, v_all).reshape(b, l, MLA_OUT)
    conv_l = gb_l * short_conv(gc_l * xv_l, conv_w)
    out_l = jnp.concatenate([att_l, conv_l], axis=-1) @ w_out
    if not ctx_out:
        return out_l, None
    q_c = mla_queries(cq_c, q_norm_w, w_uq, None)
    att_c = attend(q_c, k_c, v_c).reshape(hc.shape[0], hc.shape[1], MLA_OUT)
    conv_c = gb_c * short_conv(gc_c * xv_c, conv_w)
    out_c = jnp.concatenate([att_c, conv_c], axis=-1) @ w_out
    return out_l, out_c

def trunk_layer(xl, xc, ml, mc, norm_w, w_ffn1_in, w_ffn1_out, w_ffn2_in, w_ffn2_out,
                w_in, q_norm_w, kv_norm_w, w_uq, w_ukv, conv_w, w_out, tabs, last):
    sh1l, sc1l, g1l, sh2l, sc2l, g2l, sh3l, sc3l, g3l = ml
    sh1c, sc1c, g1c, sh2c, sc2c, g2c, sh3c, sc3c, g3c = mc
    xl = xl + 0.5 * g1l * swiglu(modulate(rmsnorm(xl, norm_w[0]), sh1l, sc1l), w_ffn1_in, w_ffn1_out)
    xc = xc + 0.5 * g1c * swiglu(modulate(rmsnorm(xc, norm_w[0]), sh1c, sc1c), w_ffn1_in, w_ffn1_out)
    hl = modulate(rmsnorm(xl, norm_w[1]), sh2l, sc2l)
    hc = modulate(rmsnorm(xc, norm_w[1]), sh2c, sc2c)
    mix_l, mix_c = token_mixer(hl, hc, w_in, q_norm_w, kv_norm_w, w_uq, w_ukv, conv_w, w_out,
                               tabs, not last)
    xl = xl + g2l * mix_l
    xl = xl + 0.5 * g3l * swiglu(modulate(rmsnorm(xl, norm_w[2]), sh3l, sc3l), w_ffn2_in, w_ffn2_out)
    if not last:
        xc = xc + g2c * mix_c
        xc = xc + 0.5 * g3c * swiglu(modulate(rmsnorm(xc, norm_w[2]), sh3c, sc3c), w_ffn2_in, w_ffn2_out)
    return xl, xc

def first_inputs(seed: int = 0) -> dict:
    key = jax.random.key(seed)
    ks = jax.random.split(key, 20)
    f32 = jnp.float32

    def dense(k, shape, fan_in, gain=1.0):
        return jax.random.normal(k, shape, f32) * (gain * fan_in ** -0.5)

    def gains(k, shape):
        return 1.0 + 0.05 * jax.random.normal(k, shape, f32)

    return {
        "x": jax.random.normal(ks[0], (BATCH, SEQ, D_MODEL), f32),
        "c": jax.random.normal(ks[1], (BATCH, D_MODEL), f32),
        "ctx": jax.random.normal(ks[2], (BATCH, CTX_LEN, D_MODEL), f32),
        "c_ctx": jax.random.normal(ks[3], (D_MODEL,), f32),
        "w_ada": dense(ks[4], (DEPTH, D_MODEL, N_MOD * D_MODEL), D_MODEL, 0.5),
        "b_ada": 0.01 * jax.random.normal(ks[5], (DEPTH, N_MOD * D_MODEL), f32),
        "norm_w": gains(ks[6], (DEPTH, 3, D_MODEL)),
        "w_ffn1_in": dense(ks[7], (DEPTH, D_MODEL, 2 * D_FF), D_MODEL),
        "w_ffn1_out": dense(ks[8], (DEPTH, D_FF, D_MODEL), D_FF),
        "w_ffn2_in": dense(ks[9], (DEPTH, D_MODEL, 2 * D_FF), D_MODEL),
        "w_ffn2_out": dense(ks[10], (DEPTH, D_FF, D_MODEL), D_FF),
        "w_in": dense(ks[11], (DEPTH, D_MODEL, D_IN), D_MODEL),
        "q_norm_w": gains(ks[12], (DEPTH, Q_LORA_RANK)),
        "kv_norm_w": gains(ks[13], (DEPTH, KV_LORA_RANK)),
        "w_uq": dense(ks[14], (DEPTH, Q_LORA_RANK, MLA_HEADS * QK_HEAD_DIM), Q_LORA_RANK),
        "w_ukv": dense(ks[15], (DEPTH, KV_LORA_RANK, MLA_HEADS * (QK_NOPE_DIM + V_HEAD_DIM)), KV_LORA_RANK),
        "conv_w": dense(ks[16], (DEPTH, CONV_K, CONV_DIM), CONV_K),
        "w_out": dense(ks[17], (DEPTH, MIX_WIDTH, D_MODEL), MIX_WIDTH),
        "final_norm_w": gains(ks[18], (D_MODEL,)),
    }

def first_block(x, c, ctx, c_ctx, w_ada, b_ada, norm_w, w_ffn1_in, w_ffn1_out, w_ffn2_in, w_ffn2_out,
              w_in, q_norm_w, kv_norm_w, w_uq, w_ukv, conv_w, w_out, final_norm_w):
    n_tokens = x.shape[1]
    rows = n_tokens // GRID_W
    tabs = axial_rope_tables(rows, x.dtype)
    xl, xc = x, ctx
    for i in range(DEPTH):
        last = i == DEPTH - 1
        ml = jnp.split((jax.nn.silu(c) @ w_ada[i] + b_ada[i])[:, None, :], N_MOD, axis=-1)
        mc = jnp.split(jax.nn.silu(c_ctx) @ w_ada[i] + b_ada[i], N_MOD, axis=-1)
        xl, xc = trunk_layer(xl, xc, ml, mc, norm_w[i], w_ffn1_in[i], w_ffn1_out[i],
                             w_ffn2_in[i], w_ffn2_out[i], w_in[i], q_norm_w[i], kv_norm_w[i],
                             w_uq[i], w_ukv[i], conv_w[i], w_out[i], tabs, last)
    return rmsnorm(xl, final_norm_w)


DEPTH_2 = 1

D_MIX = D_MODEL
ML_HEADS = 4
ML_HEAD_DIM = 128
ML_WIDTH = ML_HEADS * ML_HEAD_DIM
HG_HEADS = 4
HG_HEAD_DIM = 128
HG_WIDTH = HG_HEADS * HG_HEAD_DIM
ML_COLS = 4 * ML_WIDTH + 4 * ML_HEADS
HG_COLS = 5 * HG_WIDTH
IN_COLS = ML_COLS + HG_COLS
CONV_W = 3
ML_CHUNK = 64
HG_CHUNK = 32
N_MOD_2 = 6


F32 = jnp.float32

def _rmsnorm(x, w):
    xf = x.astype(F32)
    y = xf * lax.rsqrt(jnp.mean(xf * xf, axis=-1, keepdims=True) + EPS)
    return (y * w.astype(F32)).astype(x.dtype)

def _modulate(h, shift, scale):
    return h * (1 + scale) + shift

def _head_rmsnorm(h, w):
    B, H, T, d = h.shape
    y = h * lax.rsqrt(jnp.mean(h * h, axis=-1, keepdims=True) + EPS)
    y = jnp.transpose(y, (0, 2, 1, 3)).reshape(B, T, H * d)
    return y * w.astype(F32)

def _to_heads(a, n_heads):
    B, T, C = a.shape
    return jnp.transpose(a.reshape(B, T, n_heads, C // n_heads), (0, 2, 1, 3)).astype(F32)

def _dwconv2d(x, w, rows, cols):
    B, T, C = x.shape
    img = x.reshape(B, rows, cols, C)
    out = lax.conv_general_dilated(img, w[:, :, None, :].astype(x.dtype), (1, 1), 'SAME',
                                   dimension_numbers=('NHWC', 'HWIO', 'NHWC'), feature_group_count=C)
    return out.reshape(B, T, C)

def _chunks(a, L):
    B, H, T = a.shape[:3]
    a = a.reshape(B, H, T // L, L, *a.shape[3:])
    return jnp.moveaxis(a, 2, 0)

def _unchunks(a):
    nc, B, H, L, d = a.shape
    return jnp.moveaxis(a, 0, 2).reshape(B, H, nc * L, d)

def _mlstm_scan(q, k, v, ig, lf, state):
    L = ML_CHUNK
    causal = jnp.tril(jnp.ones((L, L), bool))

    def step(carry, inp):
        C, n, m = carry
        qc, kc, vc, ic, fc = inp
        b = jnp.cumsum(fc, axis=-1)
        dlog = jnp.where(causal, b[..., :, None] - b[..., None, :] + ic[..., None, :], -jnp.inf)
        inter = b + m[..., None]
        mt = jnp.maximum(inter, jnp.max(dlog, axis=-1))
        w_intra = jnp.exp(dlog - mt[..., None])
        w_inter = jnp.exp(inter - mt)
        s = jnp.einsum('bhtd,bhsd->bhts', qc, kc) * w_intra
        num = jnp.einsum('bhts,bhsv->bhtv', s, vc) + w_inter[..., None] * jnp.einsum('bhtd,bhdv->bhtv', qc, C)
        den = jnp.sum(s, axis=-1) + w_inter * jnp.einsum('bhtd,bhd->bht', qc, n)
        h = num / jnp.maximum(jnp.abs(den), jnp.exp(-mt))[..., None]
        bL = b[..., -1]
        wlog = bL[..., None] - b + ic
        m_new = jnp.maximum(bL + m, jnp.max(wlog, axis=-1))
        decay = jnp.exp(bL + m - m_new)
        ws = jnp.exp(wlog - m_new[..., None])
        C_new = decay[..., None, None] * C + jnp.einsum('bhs,bhsd,bhsv->bhdv', ws, kc, vc)
        n_new = decay[..., None] * n + jnp.einsum('bhs,bhsd->bhd', ws, kc)
        return (C_new, n_new, m_new), h

    state, hs = lax.scan(step, state, tuple(_chunks(a, L) for a in (q, k, v, ig, lf)))
    return _unchunks(hs), state

def _hgrn_scan(q, k, v, lf, S):
    L = HG_CHUNK
    causal = jnp.tril(jnp.ones((L, L), bool))[:, :, None]

    def step(S, inp):
        qc, kc, vc, fc = inp
        b = jnp.cumsum(fc, axis=2)
        rel = jnp.where(causal, b[:, :, :, None, :] - b[:, :, None, :, :], -jnp.inf)
        a = jnp.einsum('bhtk,bhtsk,bhsk->bhts', qc, jnp.exp(rel), kc)
        o = jnp.einsum('bhts,bhsv->bhtv', a, vc) + jnp.einsum('bhtk,bhkv->bhtv', qc * jnp.exp(b), S)
        bL = b[:, :, -1]
        S_new = jnp.exp(bL)[..., None] * S + jnp.einsum('bhsk,bhsv->bhkv', kc * jnp.exp(bL[:, :, None] - b), vc)
        return S_new, o

    S, os_ = lax.scan(step, S, tuple(_chunks(a, L) for a in (q, k, v, lf)))
    return _unchunks(os_), S

def _bidir(scan_fn, ctx_f, ctx_b, lat_f, lat_b, init):
    flip = lambda a: jnp.flip(a, axis=2)
    hc_f, st_f = scan_fn(*ctx_f, init)
    hl_f, _ = scan_fn(*lat_f, st_f)
    hc_b, st_b = scan_fn(*(flip(a) for a in ctx_b), init)
    hl_b, _ = scan_fn(*(flip(a) for a in lat_b), st_b)
    return hl_f + flip(hl_b), hc_f + flip(hc_b)

def _mlstm_prep(p, conv_w, gate_b, rows, cols):
    W, H = ML_WIDTH, ML_HEADS
    qk = jax.nn.silu(_dwconv2d(p[..., :2 * W], conv_w, rows, cols))
    q = _to_heads(qk[..., :W], H) * (ML_HEAD_DIM ** -0.5)
    k = _to_heads(qk[..., W:], H)
    v = _to_heads(p[..., 2 * W:3 * W], H)
    o = p[..., 3 * W:4 * W]
    g = jnp.transpose(p[..., 4 * W:].astype(F32) + gate_b.astype(F32), (0, 2, 1))
    i_f, f_f, i_b, f_b = jnp.split(g, 4, axis=1)
    return q, k, v, o, (i_f, jax.nn.log_sigmoid(f_f)), (i_b, jax.nn.log_sigmoid(f_b))

def _mlstm_mixer(pl, pc, conv_w, gate_b, norm_w, rows, need_ctx):
    ql, kl, vl, ol, gfl, gbl = _mlstm_prep(pl, conv_w, gate_b, rows, GRID_W)
    qc, kc, vc, oc, gfc, gbc = _mlstm_prep(pc, conv_w, gate_b, 1, pc.shape[1])
    B = pl.shape[0]
    init = (jnp.zeros((B, ML_HEADS, ML_HEAD_DIM, ML_HEAD_DIM), F32),
            jnp.zeros((B, ML_HEADS, ML_HEAD_DIM), F32),
            jnp.zeros((B, ML_HEADS), F32))
    hl, hc = _bidir(_mlstm_scan, (qc, kc, vc) + gfc, (qc, kc, vc) + gbc,
                    (ql, kl, vl) + gfl, (ql, kl, vl) + gbl, init)
    out = lambda h, o: (_head_rmsnorm(h, norm_w) * jax.nn.sigmoid(o.astype(F32))).astype(pl.dtype)
    return out(hl, ol), (out(hc, oc) if need_ctx else None)

def _hgrn_prep(p, lb):
    W, H = HG_WIDTH, HG_HEADS
    pf = p.astype(F32)
    q = _to_heads(jax.nn.silu(pf[..., :W]), H) * (HG_HEAD_DIM ** -0.5)
    v = _to_heads(pf[..., 3 * W:4 * W], H)
    g = p[..., 4 * W:5 * W]
    dirs = []
    for j in range(2):
        z = pf[..., (1 + j) * W:(2 + j) * W]
        lbj = lb[j]
        lf = jnp.logaddexp(jnp.log(lbj), jnp.log1p(-lbj) + jax.nn.log_sigmoid(z))
        k = (1 - lbj) * jax.nn.sigmoid(-z)
        dirs.append((q, _to_heads(k, H), v, _to_heads(lf, H)))
    return dirs[0], dirs[1], g

def _hgrn_mixer(pl, pc, lb, norm_w, need_ctx):
    lat_f, lat_b, gl = _hgrn_prep(pl, lb)
    ctx_f, ctx_b, gc = _hgrn_prep(pc, lb)
    B = pl.shape[0]
    init = jnp.zeros((B, HG_HEADS, HG_HEAD_DIM, HG_HEAD_DIM), F32)
    hl, hc = _bidir(_hgrn_scan, ctx_f, ctx_b, lat_f, lat_b, init)
    out = lambda h, g: (_head_rmsnorm(h, norm_w) * jax.nn.silu(g.astype(F32))).astype(pl.dtype)
    return out(hl, gl), (out(hc, gc) if need_ctx else None)

def _conv_ffn(h, w_up, conv_w, w_down, rows, cols):
    u = _dwconv2d(h @ w_up, conv_w, rows, cols)
    a, b = jnp.split(u, 2, axis=-1)
    return (jax.nn.silu(a) * b) @ w_down

def second_inputs(seed: int = 0) -> dict:
    key = jax.random.key(seed)
    ks = jax.random.split(key, 24)
    nrm = lambda k, shape, s: jax.random.normal(k, shape, F32) * s
    L, D = DEPTH_2, D_MODEL
    gate_b = jnp.concatenate([
        nrm(ks[8], (L, ML_HEADS), 0.1),
        jnp.linspace(3.0, 6.0, ML_HEADS, dtype=F32)[None] + nrm(ks[9], (L, ML_HEADS), 0.1),
        nrm(ks[10], (L, ML_HEADS), 0.1),
        jnp.linspace(3.0, 6.0, ML_HEADS, dtype=F32)[None] + nrm(ks[11], (L, ML_HEADS), 0.1)], axis=-1)
    return {
        "x": nrm(ks[0], (BATCH, SEQ, D), 1.0),
        "c": nrm(ks[1], (BATCH, D), 1.0),
        "ctx": nrm(ks[2], (BATCH, CTX_LEN, D), 1.0),
        "c_ctx": nrm(ks[3], (D,), 1.0),
        "w_mod": nrm(ks[4], (L, D, N_MOD_2 * D), D ** -0.5),
        "b_mod": nrm(ks[5], (L, N_MOD_2 * D), 0.02),
        "norm1_w": 1.0 + nrm(ks[6], (L, D), 0.05),
        "w_in": nrm(ks[7], (L, D, IN_COLS), D ** -0.5),
        "mlstm_gate_b": gate_b,
        "mlstm_conv_w": nrm(ks[12], (L, CONV_W, CONV_W, 2 * ML_WIDTH), 1.0 / CONV_W),
        "mlstm_norm_w": 1.0 + nrm(ks[13], (L, ML_WIDTH), 0.05),
        "hgrn_lb_logits": nrm(ks[14], (2, L + 1, HG_WIDTH), 0.1),
        "hgrn_norm_w": 1.0 + nrm(ks[15], (L, HG_WIDTH), 0.05),
        "w_out": nrm(ks[16], (L, D_MIX, D), D_MIX ** -0.5),
        "norm2_w": 1.0 + nrm(ks[17], (L, D), 0.05),
        "w_up": nrm(ks[18], (L, D, 2 * D_FF), D ** -0.5),
        "ffn_conv_w": nrm(ks[19], (L, CONV_W, CONV_W, 2 * D_FF), 1.0 / CONV_W),
        "w_down": nrm(ks[20], (L, D_FF, D), D_FF ** -0.5),
        "final_norm_w": 1.0 + nrm(ks[21], (D,), 0.05),
    }

def second_block(x, c, ctx, c_ctx, w_mod, b_mod, norm1_w, w_in, mlstm_gate_b, mlstm_conv_w, mlstm_norm_w,
              hgrn_lb_logits, hgrn_norm_w, w_out, norm2_w, w_up, ffn_conv_w, w_down, final_norm_w):
    rows = x.shape[1] // GRID_W
    ctx_len = ctx.shape[1]
    lower_bounds = jnp.cumsum(jax.nn.softmax(hgrn_lb_logits.astype(F32), axis=1), axis=1)
    xl, xc = x, ctx
    for l in range(DEPTH_2):
        last = l == DEPTH_2 - 1
        mod_l = (jax.nn.silu(c) @ w_mod[l] + b_mod[l])[:, None, :]
        mod_c = (jax.nn.silu(c_ctx) @ w_mod[l] + b_mod[l])[None, None, :]
        sh1, sc1, g1, sh2, sc2, g2 = jnp.split(mod_l, N_MOD_2, axis=-1)
        sh1c, sc1c, g1c, sh2c, sc2c, g2c = jnp.split(mod_c, N_MOD_2, axis=-1)
        pl = _modulate(_rmsnorm(xl, norm1_w[l]), sh1, sc1) @ w_in[l]
        pc = _modulate(_rmsnorm(xc, norm1_w[l]), sh1c, sc1c) @ w_in[l]
        ml_l, ml_c = _mlstm_mixer(pl[..., :ML_COLS], pc[..., :ML_COLS], mlstm_conv_w[l], mlstm_gate_b[l],
                                  mlstm_norm_w[l], rows, not last)
        hg_l, hg_c = _hgrn_mixer(pl[..., ML_COLS:], pc[..., ML_COLS:], lower_bounds[:, l], hgrn_norm_w[l], not last)
        xl = xl + g1 * (jnp.concatenate([ml_l, hg_l], axis=-1) @ w_out[l])
        xl = xl + g2 * _conv_ffn(_modulate(_rmsnorm(xl, norm2_w[l]), sh2, sc2), w_up[l], ffn_conv_w[l],
                                 w_down[l], rows, GRID_W)
        if not last:
            xc = xc + g1c * (jnp.concatenate([ml_c, hg_c], axis=-1) @ w_out[l])
            xc = xc + g2c * _conv_ffn(_modulate(_rmsnorm(xc, norm2_w[l]), sh2c, sc2c), w_up[l], ffn_conv_w[l],
                                      w_down[l], 1, ctx_len)
    return _rmsnorm(xl, final_norm_w)


def setup_inputs(seed=0):
    out = dict(first_inputs(seed))
    for name, value in second_inputs(seed + 1).items():
        if name != "x":
            out[name + "_2"] = value
    return out


def reference(
    x, c, ctx, c_ctx, w_ada, b_ada, norm_w, w_ffn1_in, w_ffn1_out, w_ffn2_in, w_ffn2_out, w_in,
    q_norm_w, kv_norm_w, w_uq, w_ukv, conv_w, w_out, final_norm_w, c_2, ctx_2, c_ctx_2, w_mod_2,
    b_mod_2, norm1_w_2, w_in_2, mlstm_gate_b_2, mlstm_conv_w_2, mlstm_norm_w_2,
    hgrn_lb_logits_2, hgrn_norm_w_2, w_out_2, norm2_w_2, w_up_2, ffn_conv_w_2, w_down_2,
    final_norm_w_2,
):
    x = first_block(
        x, c, ctx, c_ctx, w_ada, b_ada, norm_w, w_ffn1_in, w_ffn1_out, w_ffn2_in, w_ffn2_out,
        w_in, q_norm_w, kv_norm_w, w_uq, w_ukv, conv_w, w_out, final_norm_w,
    )
    return second_block(
        x, c_2, ctx_2, c_ctx_2, w_mod_2, b_mod_2, norm1_w_2, w_in_2, mlstm_gate_b_2,
        mlstm_conv_w_2, mlstm_norm_w_2, hgrn_lb_logits_2, hgrn_norm_w_2, w_out_2, norm2_w_2,
        w_up_2, ffn_conv_w_2, w_down_2, final_norm_w_2,
    )


_drawn_inputs = setup_inputs


def setup_inputs(seed=0):
    import zlib

    import numpy as np

    out = dict(_drawn_inputs(seed))
    spreads = {}
    factors = {'ctx': 3.245,
     'b_ada': 3.037,
     'q_norm_w': 8.0,
     'kv_norm_w': 8.0,
     'norm1_w_2': 2.976,
     'mlstm_norm_w_2': 14.704,
     'hgrn_lb_logits_2': 8.0,
     'hgrn_norm_w_2': 3.113,
     'norm2_w_2': 6.541}
    for name, (base, spread) in spreads.items():
        noise = np.random.default_rng([zlib.crc32(name.encode()), seed]).standard_normal(out[name].shape)
        drawn = base * np.exp(spread * noise) if base else spread * noise
        out[name] = __import__('jax').numpy.asarray(drawn.astype(out[name].dtype))
    for name, factor in factors.items():
        out[name] = (out[name] * factor).astype(out[name].dtype)
    return out
```

```python
from contextlib import ExitStack

import numpy as np

import concourse.bass as bass
from concourse import mybir

F32 = mybir.dt.float32
U32 = mybir.dt.uint32
ACT = mybir.ActivationFunctionType
ALU = mybir.AluOpType
AX_X = mybir.AxisListType.X

P = 128
D = 1024
KC = D // P
CTX, LAT = 256, 256
T = CTX + LAT
FF = 2816
FC = FF // P
DEPTH = 2
N_MOD, N_MOD_2 = 9, 6
HEADS, NOPE, ROPE, VD = 8, 64, 32, 64
QK = NOPE + ROPE
QR, KVR = 256, 128
CONV = 512
GRID = 64
ROWS = LAT // GRID
EPS = 1e-6
SCALE = QK ** -0.5
ITEM = 512
RING = 3
MH = 4
MSCALE = P ** -0.5
NEG = -1.0e30



def _columns(parts):
    at, where = 0, {}
    for name, n in parts:
        where[name] = (at, n)
        at += n
    return where, at


PARAMS, N_PARAMS = _columns(
    [(f"norm{i}", 3 * KC) for i in range(DEPTH)] + [(f"b_ada{i}", N_MOD * KC) for i in range(DEPTH)]
    + [(f"q_norm{i}", QR // P) for i in range(DEPTH)] + [(f"kv_norm{i}", 1) for i in range(DEPTH)]
    + [(f"conv{i}", 3 * (CONV // P)) for i in range(DEPTH)]
    + [("final1", KC), ("c1", 2 * KC), ("c2", 2 * KC), ("b_mod", N_MOD_2 * KC), ("norm_a", KC), ("norm_b", KC),
       ("gate_b", 1), ("qk_conv", 9 * KC), ("ml_norm", MH), ("lb", 2 * 2 * MH), ("hg_norm", MH),
       ("ffn_conv", 9 * 2 * FC), ("final2", KC), ("w_gate", KC * P)])
LEVELS = 7
CONSTS, N_CONSTS = _columns(
    [("ident", P), ("ones", P), ("sum_rows", 2), ("perm", P), ("cos", LAT), ("sin", LAT), ("eps", 1),
     ("level", (LEVELS + 1) * P), ("causal", 2 * P), ("row_of", 8 * P), ("col_of", 8 * 8)])

FFN_IN = FF // (ITEM // 2)
ITEMS, at = {}, 0
for _i in range(DEPTH):
    for _name, _n in ((f"ada{_i}", N_MOD * D // ITEM), (f"up1{_i}", FFN_IN), (f"down1{_i}", 6), (f"in{_i}", 4),
                      (f"uqkv{_i}", 1), (f"out{_i}", 2), (f"up2{_i}", FFN_IN), (f"down2{_i}", 6)):
        ITEMS[_name] = at
        at += _n
for _name, _n in (("mod", N_MOD_2 * D // ITEM), ("in", 9), ("out", 2), ("up", FFN_IN), ("down", 6)):
    ITEMS[_name] = at
    at += _n
N_USED = at
N_ITEMS = -(-at // RING) * RING


PROJECTIONS = {
    "ml_q": lambda w, hg: 0, "ml_k": lambda w, hg: w, "hg_zf": lambda w, hg: hg + w, "hg_zb": lambda w, hg: hg + 2 * w,
    "hg_q": lambda w, hg: hg, "ml_v": lambda w, hg: 2 * w, "hg_v": lambda w, hg: hg + 3 * w,
    "ml_o": lambda w, hg: 3 * w, "hg_g": lambda w, hg: hg + 4 * w}



def build_program(nc, stream, x_in, ctx2_in, params_in, consts_in, out, until=None):
    with ExitStack() as stack:
        def sb(name, shape):
            return stack.enter_context(nc.sbuf_tensor(name, shape, F32))

        slots = [sb(f"slot{s}", [P, KC, ITEM]) for s in range(RING)]
        x = sb("x", [P, KC, T])
        h = sb("h", [P, KC, T])
        arena = sb("arena", [P, 44, T])
        squares = sb("squares", [P, 4, T])
        rms = sb("rms", [P, T])
        rinv = sb("rinv", [P, T])
        params = sb("params", [P, N_PARAMS])
        consts = sb("consts", [P, N_CONSTS])
        cond = sb("cond", [P, KC, 32])
        mod = sb("mod", [P, N_MOD * KC, 2])
        scales = sb("scales", [P, 3 * KC, 2])
        gates = sb("gates", [P, 3 * KC, 2])
        small = sb("small", [P, 64])
        bank = [stack.enter_context(nc.psum_tensor(f"bank{b}", [P, 512], F32)) for b in range(8)]
        sems = {}

        def sem(name):
            if name not in sems:
                sems[name] = stack.enter_context(nc.semaphore(name))
            return sems[name]

        def param(name, a=0, n=None):
            first, width = PARAMS[name]
            return params[:, first + a:first + a + (width - a if n is None else n)]

        def const(name, a=0, n=None, rows=P):
            first, width = CONSTS[name]
            return consts[0:rows, first + a:first + a + (width - a if n is None else n)]

        ident, ones = const("ident"), const("ones")

        def slot_of(item):
            return item % RING

        item_full = [sem(f"item_full{s}") for s in range(RING)]
        item_begun = sem("item_begun")
        loaded = sem("inputs_loaded")
        x_updated = sem("x_updated")

        SWIGLU = [f"ffn{n}{i}" for i in range(DEPTH) for n in (1, 2)]
        MIXERS = [f"mix{i}" for i in range(DEPTH)]
        UPDATES = [f"{s}{i}" for i in range(DEPTH) for s in ("ffn1", "mix", "ffn2")]
        BANKED = list(UPDATES) + ["mix_b", "ffn_b"]
        UPDATES += ["final1", "mix_b", "ffn_b"]
        NORMS = [(f"norm{n + 1}{i}", 3 * i + n, CTX if i == DEPTH - 1 and n == 2 else 0)
                 for i in range(DEPTH) for n in range(3)]
        NORMS += [("final1", 3 * DEPTH, CTX), ("norm_a", 3 * DEPTH + 1, 0), ("norm_b", 3 * DEPTH + 2, CTX),
                  ("final2", 3 * DEPTH + 3, CTX)]
        NORM_AT = {name: n for n, (name, _, _) in enumerate(NORMS)}
        UPDATED = {name: updates for name, updates, _ in NORMS}
        START = {name: t0 for name, _, t0 in NORMS}

        def normed(name, t0):
            return KC * sum(1 for n, (other, _, first) in enumerate(NORMS)
                            if n <= NORM_AT[name] and first <= t0 and not other.startswith("final"))

        class Chain:

            def __init__(self, engine, name):
                self.engine, self.sem, self.n = engine, sem(name), 0

            def mark(self, instruction):
                self.n += 1
                instruction.then_inc(self.sem, 1)
                return self.n

            def wait(self, n):
                self.engine.wait_ge(self.sem, n)

            def link(self, instruction):
                self.wait(self.mark(instruction))

        latent = arena[:, 0:4, :]
        conv_in = arena[:, 4:12, :]
        q_heads, k_heads = arena[:, 12:21, :], arena[:, 21:29, :]
        values = arena[:, 29:33, :]
        probs, probs_turned = arena[:, 33:36, :], arena[:, 36:38, :]
        latent_rms, latent_rinv = arena[:, 38:40, :], arena[:, 40:42, :]
        rope_tmp = arena[:, 42, :]
        mod_rows = arena[:, 22:25, :]
        SCORE_BANKS = (2, 4, 5)

        q_raw = arena[:, 0:2, :].rearrange("p a (b t) -> p (a b) t", b=2)
        k_raw = arena[:, 2:6, :]
        q_ml = arena[:, 6:8, :].rearrange("p a (b t) -> p (a b) t", b=2)
        k_ml, v_ml, v_hg = arena[:, 8:12, :], arena[:, 12:16, :], arena[:, 16:20, :]
        o_gate = arena[:, 20:22, :].rearrange("p a (b t) -> p (a b) t", b=2)
        g_gate = arena[:, 22:24, :].rearrange("p a (b t) -> p (a b) t", b=2)
        q_hg = arena[:, 24:26, :].rearrange("p a (b t) -> p (a b) t", b=2)
        k_hg = [arena[:, 26:30, :], arena[:, 30:34, :]]
        decay = [arena[:, 34:38, :], arena[:, 38:42, :]]
        hg_scores = arena[:, 0:4, :].rearrange("p h (c t) -> p h c t", c=2)
        hg_ctx_scores = arena[:, 4:6, :]
        hg_out = q_hg
        hg_factor = [[h[:, 4 * e + 2 * part:4 * e + 2 * part + 2, :].rearrange("p a (b t) -> p (a b) t", b=2)
                      for part in range(2)] for e in range(2)]
        hg_factors = [h[:, 4 * e:4 * e + 4, :] for e in range(2)]
        ml_decay = [arena[:, 26 + 2 * e:28 + 2 * e, :].rearrange("p a (b t) -> p (a b) t", b=2) for e in range(2)]
        ml_weight = [arena[:, 30 + 2 * e:32 + 2 * e, :].rearrange("p a (b t) -> p (a b) t", b=2) for e in range(2)]
        ml_num = arena[:, 34:38, :]
        ml_out = arena[:, 38:40, :].rearrange("p a (b t) -> p (a b) t", b=2)
        ml_floor, ml_den = arena[0:MH, 40, :], arena[0:MH, 41, :]
        out_squares = arena[:, 26:30, :].rearrange("p a (b t) -> p (a b) t", b=2)
        out_rms, out_rinv = arena[0:2 * MH, 30, 0:LAT], arena[0:2 * MH, 31, 0:LAT]
        u_rows = [arena[0:MH, 42, :], squares[0:MH, 0, :]]
        m_rows = [rms[0:MH, CTX:], squares[0:MH, 1, 0:LAT]]
        floor_rows = [squares[0:MH, 2, CTX:], squares[0:MH, 1, LAT:]]
        u_cols = small[:, 0:2 * 4 * MH]
        bounds = small[:, 40:56].rearrange("p (k d c) -> p k d c", k=2, d=2)
        UNITS_B = [(name, c) for name in PROJECTIONS for c in range(4)]
        WIDE = ("ml_k", "hg_zf", "hg_zb")
        HG_STAGES = ["ctx0", "ctx1"] + list(range(LEVELS + 1)) + ["diagonal"]
        N_TAPS = 2 * 8
        UP_B = 2 * FFN_IN
        raw_b = [[arena[:, 24 + e, part * LAT:(part + 1) * LAT] for part in range(2)] for e in range(2)]
        acc_b = [[arena[:, 26 + e, part * LAT:(part + 1) * LAT] for part in range(2)] for e in range(2)]

        def lat_valid(direction, c):
            if direction == 0:
                return c * P, LAT
            return 0, (c + 1) * P

        def taps(rows, cols):
            for dy in (-1, 0, 1):
                for dx in (-1, 0, 1):
                    if (dy or dx) and abs(dy) < rows:
                        r = slice(max(0, -dy), rows - max(0, dy)), slice(max(0, dy), rows - max(0, -dy))
                        c = slice(max(0, -dx), cols - max(0, dx)), slice(max(0, dx), cols - max(0, -dx))
                        yield 3 * (dy + 1) + dx + 1, (r[0], c[0]), (r[1], c[1])

        FOLLOWING = {0: "norm10", 1: "norm11", "b": "norm_a"}
        PREVIOUS = {1: (0, N_MOD * D // ITEM), "b": (1, N_MOD * D // ITEM)}

        def attention_units(t0):
            return [(hd, tc, CTX if tc * P < CTX else T) for hd in range(HEADS) for tc in range(t0 // P, T // P)]

        def h_scaled_before(name):
            return KC * sum(1 for n, (other, _, _) in enumerate(NORMS)
                            if n < NORM_AT[name] and not other.startswith("final"))

        def modulation(name, kc, which):
            if name in ("norm_a", "norm_b"):
                j = ("norm_a", "norm_b").index(name)
            else:
                j = int(name[4]) - 1
            shift = KC * 3 * j + kc
            return scales[:, KC * j + kc, which:which + 1], mod[:, shift, which:which + 1]

        n_rounds = N_ITEMS // RING if until is None else -(-ITEMS["mod"] // RING)
        block = stack.enter_context(nc.Block())

        @block.sync
        def _(sp):
            sp.dma_start(params[:, :], params_in).then_inc(loaded, 16)
            sp.dma_start(consts[:, :], consts_in).then_inc(loaded, 16)
            sp.dma_start(x[:, :, :], x_in).then_inc(loaded, 16)
            for s in range(RING):
                sp.dma_start(slots[s][:, :, :], stream[s]).then_inc(item_full[s], 16)
            with sp.Fori(1, n_rounds) as i:
                for s in range(RING):
                    sp.wait_ge(item_begun, i * RING + (s + 2 - RING))
                    sp.dma_start(slots[s][:, :, :], stream[i * RING + s]).then_inc(item_full[s], 16)
            for s in range(RING):
                sp.wait_ge(item_full[s], 16 * n_rounds)
            if until is None:
                for part in range(2):
                    sp.wait_ge(x_updated, KC * (UPDATED["final2"]) + 4 * (part + 1))
                    sp.dma_start(out[:, 4 * part:4 * part + 4, :], x[:, 4 * part:4 * part + 4, CTX:])\
                        .then_inc(sem("stored"), 16)
                sp.wait_ge(sem("stored"), 32)
            else:
                sp.wait_ge(x_updated, KC * (3 * DEPTH + 1))
                sp.dma_start(out, x[:, :, CTX:]).then_inc(sem("stored"), 16)
                sp.wait_ge(sem("stored"), 16)

        @block.tensor
        def _(pe):
            def await_item(item, rounds=0):
                pe.wait_ge(item_full[item % RING], rounds * 16 + 16 * (item // RING + 1))

            def begins(product, when=True):
                if when:
                    product.then_inc(item_begun, 1)
                return product

            def conditioning(tag, first, n):
                if tag != 0:
                    pe.wait_ge(x_updated, KC * UPDATED[FOLLOWING[tag]])
                pe.sem_inc(sem(f"mod_turned{tag}"), 3)
                pe.wait_ge(sem(f"cond_ready{tag}"), 1)
                with pe.Fori(0, n // 3) as i:
                    for j in range(3):
                        await_item(first + j, i)
                        pe.wait_ge(sem(f"mod_row{tag}"), i * 3 + (j + 1))
                        for kc in range(KC):
                            g = 32 * (kc % 4)
                            last = begins(nc.tensor.matmul(bank[4 + j][g:g + 32, :], cond[:, kc, :],
                                                           slots[(first + j) % RING][:, kc, :], start=kc < 4,
                                                           stop=kc >= 4), kc == 0)
                        last.then_inc(sem(f"mod_sum{tag}"), 1)
                    for j in range(3):
                        pe.wait_ge(sem(f"mod_row{tag}"), i * 3 + (j + 4))
                        for q in range(4):
                            last = nc.tensor.matmul(bank[7][:, bass.ds(i * 24 + (8 * j + 2 * q), 2)],
                                                    mod_rows[:, j, q * P:(q + 1) * P], const("sum_rows"),
                                                    start=True, stop=True)
                        last.then_inc(sem(f"mod_turned{tag}"), 1)

            def norm_sum(name):
                n, t0 = NORM_AT[name], START[name]
                for kc in range(KC):
                    pe.wait_ge(sem("square_ready"), KC * n + kc + 1)
                    last = nc.tensor.matmul(bank[4][:, 0:T - t0], ones, squares[:, kc % 4, t0:], start=kc == 0,
                                            stop=kc == KC - 1)
                    last.then_inc(sem("square_used"), 1)

            def await_normed(name, t0):
                if t0 == 0:
                    pe.wait_ge(sem("h_ctx_ready"), normed(name, 0))
                pe.wait_ge(sem("h_lat_ready"), normed(name, CTX))

            def swiglu(name, norm, up, down):
                f, t0 = SWIGLU.index(name), START[norm]
                await_normed(norm, t0)

                def pairs(slot, item_in_stage):
                    for sub in range(2):
                        pe.wait_ge(sem("hidden_ready"), item_in_stage * 2 + (2 * FFN_IN * f + sub + 1))
                        for gv in range(2):
                            for kc in range(KC):
                                at = gv * (ITEM // 2) + sub * P
                                last = begins(nc.tensor.matmul(bank[2 * sub + gv][:, 0:T - t0], slots[slot][:, kc, at:at + P],
                                                               h[:, kc, t0:], start=kc == 0, stop=kc == KC - 1),
                                              sub == gv == kc == 0)
                        last.then_inc(sem("pair_ready"), 1)

                looped = FFN_IN // RING
                with pe.Fori(0, looped) as i:
                    for j in range(RING):
                        await_item(up + j, i)
                        pairs((up + j) % RING, i * RING + j)
                for j in range(looped * RING, FFN_IN):
                    await_item(up + j)
                    pairs((up + j) % RING, j)
                pe.wait_ge(sem("hidden_ready"), 2 * FFN_IN * (f + 1) + 2)
                down_product(down, arena, t0)

            def down_product(down, hidden, t0):
                for half in range(2):
                    for g in range(3):
                        item, chunks = down + 3 * half + g, min(KC, FC - KC * g)
                        await_item(item)
                        for q in range(4):
                            for kc in range(chunks):
                                last = begins(nc.tensor.matmul(bank[q if half else 4 + q][:, 0:T - t0],
                                                               slots[item % RING][:, kc, q * P:(q + 1) * P],
                                                               hidden[:, KC * g + kc, t0:], start=g == 0 and kc == 0,
                                                               stop=g == 2 and kc == chunks - 1), q == kc == 0)
                            if g == 2:
                                last.then_inc(sem("acc_ready"), 1)

            def out_product(first, t0):
                for half in range(2):
                    await_item(first + half)
                    for q in range(4):
                        for kc in range(KC):
                            last = begins(nc.tensor.matmul(bank[q if half else 4 + q][:, 0:T - t0],
                                                           slots[(first + half) % RING][:, kc, q * P:(q + 1) * P],
                                                           h[:, kc, t0:], start=kc == 0, stop=kc == KC - 1), q == kc == 0)
                        last.then_inc(sem("acc_ready"), 1)

            def mla_and_conv(i):
                tag, t0 = MIXERS[i], CTX if i == DEPTH - 1 else 0
                await_normed(f"norm2{i}", 0)
                first = ITEMS[f"in{i}"]

                def product(acc, item, q, start_token):
                    for kc in range(KC):
                        last = begins(nc.tensor.matmul(acc[:, 0:T - start_token], slots[item % RING][:, kc, q * P:(q + 1) * P],
                                                       h[:, kc, start_token:], start=kc == 0, stop=kc == KC - 1), q == kc == 0)
                    return last

                await_item(first)
                for q in range(4):
                    product(bank[q], first, q, t0 if q < 2 else 0).then_inc(sem(f"latent_sum{tag}"), 1)
                for n in range(12):
                    if n % 4 == 0:
                        await_item(first + 1 + n // 4)
                    if n >= 4:
                        pe.wait_ge(sem(f"conv_moved{tag}"), n - 3)
                    product(bank[4 + n % 4], first + 1 + n // 4, n % 4, t0).then_inc(sem(f"conv_sum{tag}"), 1)
                    if n == 3:
                        pe.wait_ge(sem(f"latent_moved{tag}"), 4)
                        pe.wait_ge(sem(f"latent_square{tag}"), 3)
                        for c in range(2):
                            last = nc.tensor.matmul(bank[0][:, 0:T - t0], ones, squares[:, c, t0:], start=c == 0, stop=c == 1)
                        last.then_inc(sem(f"latent_norm_sum{tag}"), 1)
                        nc.tensor.matmul(bank[1][:, :], ones, squares[:, 2, :], start=True, stop=True)\
                            .then_inc(sem(f"latent_norm_sum{tag}"), 1)
                item = ITEMS[f"uqkv{i}"]
                await_item(item)
                flat = slots[item % RING][:, :, :].rearrange("p a b -> p (a b)")
                w_q = flat[:, 0:2 * HEADS * QK].rearrange("p (k n) -> p k n", k=2)
                w_kv = flat[:, 2 * HEADS * QK:2 * HEADS * QK + HEADS * (NOPE + VD)].rearrange("p (h n) -> p h n", h=HEADS)
                pe.wait_ge(sem(f"latent_ready{tag}"), 3)
                for n in range(20):
                    acc = bank[4 + n % 4]
                    if n < 4:
                        pe.wait_ge(sem(f"conv_u{tag}"), n + 1)
                    elif n % 2 and n < 20:
                        pe.wait_ge(sem(f"key_moved{tag}"), (n - 4) // 2 + 1)
                    else:
                        pe.wait_ge(sem(f"query_moved{tag}"), (n - 4) // 2 + 1)
                    hd = n // 2
                    if n >= 16:
                        c = n - 16
                        last = nc.tensor.matmul(acc[:, :], latent[:, 2, c * P:(c + 1) * P], w_kv[:, :, NOPE:], start=True, stop=True)
                    elif n % 2:
                        last = nc.tensor.matmul(acc[0:NOPE, :], w_kv[:, hd, 0:NOPE], latent[:, 2, :], start=True, stop=True)
                    else:
                        for c in range(2):
                            last = begins(nc.tensor.matmul(acc[0:QK, 0:T - t0], w_q[:, c, hd * QK:(hd + 1) * QK],
                                                           latent[:, c, t0:], start=c == 0, stop=c == 1), n == c == 0)
                    last.then_inc(sem(f"head_sum{tag}"), 1)
                for r in range(5):
                    if r == 4:
                        pe.wait_ge(sem(f"roped{tag}"), 1)
                    if r:
                        pe.wait_ge(sem(f"query_moved{tag}"), 2 * r)
                    src = q_heads[0:QK, 8:9, CTX:] if r == 0 else q_heads[0:QK, 2 * r - 2:2 * r, CTX:]
                    width = LAT if r == 0 else 2 * LAT
                    nc.tensor.matmul(bank[r % 4][0:QK, 0:width], const("perm", 0, QK, rows=QK), src, start=True, stop=True)\
                        .then_inc(sem(f"exchanged{tag}"), 1)
                pe.wait_ge(sem(f"roped{tag}"), 5)
                pe.wait_ge(sem(f"key_rope{tag}"), 1)
                pe.wait_ge(sem(f"key_moved{tag}"), HEADS)
                pe.wait_ge(sem(f"query_moved{tag}"), HEADS + 4)
                units = attention_units(t0)
                for n in range(len(units) + 3):
                    if n < len(units):
                        hd, tc, keys = units[n]
                        if n >= 3:
                            pe.wait_ge(sem(f"exp{tag}"), n - 2)
                        nc.tensor.matmul(bank[SCORE_BANKS[n % 3]][:, 0:keys], q_heads[0:QK, hd, tc * P:(tc + 1) * P],
                                         k_heads[0:QK, hd, 0:keys], start=True, stop=True).then_inc(sem(f"score{tag}"), 1)
                    m = n - 2
                    if 0 <= m < len(units):
                        keys = units[m][2]
                        pe.wait_ge(sem(f"prob{tag}"), m + 1)
                        if m >= 2:
                            pe.wait_ge(sem(f"prob_turned_moved{tag}"), m - 1)
                        for c in range(keys // P):
                            last = nc.tensor.transpose(bank[6 + m % 2][:, c * P:(c + 1) * P],
                                                       probs[:, m % 3, c * P:(c + 1) * P], ident)
                        last.then_inc(sem(f"prob_turned{tag}"), 1)
                    m = n - 3
                    if 0 <= m < len(units):
                        hd, tc, keys = units[m]
                        pe.wait_ge(sem(f"prob_turned_moved{tag}"), m + 1)
                        if m >= 2:
                            pe.wait_ge(sem(f"attended{tag}"), m - 1)
                        for c in range(keys // P):
                            v0 = hd // 2 * P
                            last = nc.tensor.matmul(bank[m % 2][:, 0:P], values[:, c, v0:v0 + P],
                                                    probs_turned[:, m % 2, c * P:(c + 1) * P], start=c == 0,
                                                    stop=c == keys // P - 1)
                        last.then_inc(sem(f"attend_sum{tag}"), 1)
                pe.wait_ge(sem(f"attended{tag}"), len(units))
                pe.wait_ge(sem(f"conv_out{tag}"), 4)
                out_product(ITEMS[f"out{i}"], t0)

            def projections():
                await_normed("norm_a", 0)
                for kc in range(KC):
                    last = nc.tensor.matmul(bank[5][:, :], param("w_gate", kc * P, P), h[:, kc, :], start=kc == 0, stop=kc == KC - 1)
                last.then_inc(sem("gate_sum"), 1)
                for n, (name, c) in enumerate(UNITS_B):
                    item = ITEMS["in"] + n // 4
                    if c == 0:
                        await_item(item)
                    if n >= 4:
                        pe.wait_ge(sem("projected"), n - 3)
                    start = 0 if name in WIDE else CTX
                    for kc in range(KC):
                        if name.endswith("_v"):
                            last = nc.tensor.matmul(bank[n % 4][:, :], h[:, kc, c * P:(c + 1) * P], slots[item % RING][:, kc, :],
                                                    start=kc == 0, stop=kc == KC - 1)
                        else:
                            last = nc.tensor.matmul(bank[n % 4][:, 0:T - start], slots[item % RING][:, kc, c * P:(c + 1) * P],
                                                    h[:, kc, start:], start=kc == 0, stop=kc == KC - 1)
                        begins(last, c == kc == 0)
                    last.then_inc(sem("projection_sum"), 1)

            def hgrn():
                for n, stage in enumerate(HG_STAGES):
                    pe.wait_ge(sem("hg_scaled"), n + 1)
                    q, k = hg_factor[n % 2]
                    if stage in ("ctx0", "ctx1"):
                        if n == 0:
                            pe.wait_ge(sem("projected"), len(UNITS_B))
                        for hd in range(MH):
                            for c in range(2):
                                last = nc.tensor.matmul(bank[hd][:, c * LAT:(c + 1) * LAT], k[:, hd, c * P:(c + 1) * P], q[:, hd, :],
                                                        start=n == 0 and c == 0, stop=n == 1, skip_group_check=True)
                    else:
                        if n >= 4:
                            pe.wait_ge(sem("hg_placed"), n - 3)
                        for c in range(2):
                            t = 1 - c if stage == LEVELS else c
                            source = q_hg if stage == "diagonal" else q
                            for hd in range(MH):
                                last = nc.tensor.matmul(bank[4 + 2 * (n % 2) + c][:, hd * P:(hd + 1) * P], k[:, hd, c * P:(c + 1) * P],
                                                        source[:, hd, t * P:(t + 1) * P], start=True, stop=True)
                    last.then_inc(sem("hg_product"), 1)
                pe.wait_ge(sem("hg_placed"), len(HG_STAGES) - 2)
                for hd in range(MH):
                    pe.wait_ge(sem("hg_ctx_moved"), hd + 1)
                    for c in range(4):
                        w = hg_ctx_scores[:, hd % 2, c * LAT:(c + 1) * LAT] if c < 2 else hg_scores[:, hd, c - 2, :]
                        last = nc.tensor.matmul(bank[4 + hd][:, 0:LAT], v_hg[:, c, hd * P:(hd + 1) * P], w, start=c == 0, stop=c == 3)
                    last.then_inc(sem("hg_out_sum"), 1)

            def mlstm():
                pe.wait_ge(sem("gate_rows"), 1)
                pe.wait_ge(sem("hg_ctx_moved"), MH)
                for d in range(2):
                    for c in range(4):
                        at = MH * (4 * d + c)
                        last = nc.tensor.matmul(bank[2][:, at:at + MH], u_rows[d][:, c * P:(c + 1) * P], const("ident", 0, MH, rows=MH),
                                                start=True, stop=True)
                last.then_inc(sem("u_turned"), 1)
                pe.wait_ge(sem("u_cols"), 1)
                pe.wait_ge(sem("conv_silu"), 2)
                pe.wait_ge(sem("hg_out_moved"), MH)

                def maxima(n):
                    hd, d = n // 2, n % 2
                    if n >= 2:
                        pe.wait_ge(sem("ml_decayed"), n - 1)
                    nc.tensor.matmul(bank[2 + d][:, 0:LAT], const("row_of", hd * P, P, rows=MH), m_rows[d], start=True, stop=True)\
                        .then_inc(sem("ml_max"), 1)

                def scores(hd):
                    if hd:
                        pe.wait_ge(sem("ml_weighted"), 2 * hd)
                    for c in range(4):
                        last = nc.tensor.matmul(bank[c // 2][:, c % 2 * LAT:(c % 2 + 1) * LAT], k_ml[:, hd, c * P:(c + 1) * P],
                                                q_ml[:, hd, :], start=c % 2 == 0, stop=c % 2 == 1, skip_group_check=True)
                    last.then_inc(sem("ml_score"), 1)

                maxima(0)
                maxima(1)
                scores(0)
                for n in range(2 * MH):
                    hd, d = n // 2, n % 2
                    pe.wait_ge(sem("ml_weighted"), n + 1)
                    if n >= 2:
                        pe.wait_ge(sem("ml_num_moved"), n - 1)
                    for target in range(2):
                        for c in range(4):
                            a, b = (0, LAT) if c < 2 else lat_valid(d, c - 2)
                            w = ml_weight[d][:, c, a:b]
                            if target == 0:
                                last = nc.tensor.matmul(bank[4 + d][:, a:b], v_ml[:, c, hd * P:(hd + 1) * P], w,
                                                        start=c == 0, stop=c == 3, skip_group_check=True)
                            else:
                                last = nc.tensor.matmul(bank[6 + d][0:8, a:b], const("col_of", 8 * hd, 8), w,
                                                        start=c == hd == 0, stop=c == hd == 3, skip_group_check=True)
                    last.then_inc(sem("ml_num_sum"), 1)
                    if n + 2 < 2 * MH:
                        maxima(n + 2)
                    if d == 1 and hd + 1 < MH:
                        scores(hd + 1)
                pe.wait_ge(sem("ml_den_ready"), 1)
                for hd in range(MH):
                    nc.tensor.matmul(bank[hd][:, :], const("row_of", hd * P, P, rows=MH), ml_den, start=True, stop=True)\
                        .then_inc(sem("ml_den_spread"), 1)

            def head_norms():
                for j in range(8):
                    pe.wait_ge(sem("out_square"), j + 1)
                    last = nc.tensor.matmul(bank[4][0:8, 0:LAT], const("col_of", 8 * j, 8), out_squares[:, j, :],
                                            start=j == 0, stop=j == 7)
                last.then_inc(sem("out_norm_sum"), 1)
                pe.wait_ge(sem("out_rinv"), 1)
                for j in range(8):
                    nc.tensor.matmul(bank[j // 2][:, j % 2 * LAT:(j % 2 + 1) * LAT], const("row_of", j * P, P, rows=8), out_rinv,
                                     start=True, stop=True, skip_group_check=True)\
                        .then_inc(sem("out_rinv_spread"), 1)

            def conv_ffn():
                await_normed("norm_b", CTX)

                def pairs(slot, item_in_stage):
                    for sub in range(2):
                        pe.wait_ge(sem("up_moved"), item_in_stage * 2 + (sub + 1))
                        for gv in range(2):
                            for kc in range(KC):
                                at = gv * (ITEM // 2) + sub * P
                                last = begins(nc.tensor.matmul(bank[2 * sub + gv][:, 0:LAT], slots[slot][:, kc, at:at + P],
                                                               h[:, kc, CTX:], start=kc == 0, stop=kc == KC - 1),
                                              sub == gv == kc == 0)
                        last.then_inc(sem("up_sum"), 1)

                pe.sem_inc(sem("up_moved"), 2)
                up = ITEMS["up"]
                looped = FFN_IN // RING
                with pe.Fori(0, looped) as i:
                    for j in range(RING):
                        await_item(up + j, i)
                        pairs((up + j) % RING, i * RING + j)
                for j in range(looped * RING, FFN_IN):
                    await_item(up + j)
                    pairs((up + j) % RING, j)
                pe.wait_ge(sem("hidden_b"), UP_B + 1)
                down_product(ITEMS["down"], arena, CTX)

            pe.wait_ge(loaded, 48)
            pe.sem_inc(sem("hidden_ready"), 2)
            for i in range(DEPTH):
                conditioning(i, ITEMS[f"ada{i}"], N_MOD * D // ITEM)
                norm_sum(f"norm1{i}")
                swiglu(f"ffn1{i}", f"norm1{i}", ITEMS[f"up1{i}"], ITEMS[f"down1{i}"])
                norm_sum(f"norm2{i}")
                mla_and_conv(i)
                norm_sum(f"norm3{i}")
                swiglu(f"ffn2{i}", f"norm3{i}", ITEMS[f"up2{i}"], ITEMS[f"down2{i}"])
            norm_sum("final1")
            if until is None:
                conditioning("b", ITEMS["mod"], N_MOD_2 * D // ITEM)
                norm_sum("norm_a")
                projections()
                hgrn()
                mlstm()
                head_norms()
                pe.wait_ge(sem("mixed_b"), 8)
                out_product(ITEMS["out"], CTX)
                norm_sum("norm_b")
                conv_ffn()
                norm_sum("final2")

        @block.scalar
        def _(act):
            def conditioning(tag, name, n):
                act.sem_inc(sem(f"mod_row{tag}"), 3)
                act.wait_ge(sem(f"cond_zero"), 1)
                if tag != 0:
                    act.wait_ge(sem(f"mod_turned{PREVIOUS[tag][0]}"), PREVIOUS[tag][1] + 3)
                nc.scalar.activation(cond[:, :, 0:2], param(name).rearrange("p (k c) -> p k c", c=2), ACT.Silu)\
                    .then_inc(sem(f"cond_ready{tag}"), 1)
                with act.Fori(0, n // 3) as i:
                    for j in range(3):
                        act.wait_ge(sem(f"mod_sum{tag}"), i * 3 + (j + 1))
                        act.wait_ge(sem(f"mod_turned{tag}"), i * 3 + (j + 1))
                        nc.scalar.activation(mod_rows[:, j, :], bank[4 + j][:, :], ACT.Copy).then_inc(sem(f"mod_row{tag}"), 1)

            def norm(name):
                n, t0, u = NORM_AT[name], START[name], UPDATED[name]
                for kc in range(KC):
                    if KC * u + kc >= 0 and u > 0:
                        act.wait_ge(x_updated, KC * (u - 1) + kc + 1)
                    if KC * n + kc >= 4:
                        act.wait_ge(sem("square_used"), KC * n + kc - 3)
                    nc.scalar.activation(squares[:, kc % 4, t0:], x[:, kc, t0:], ACT.Square).then_inc(sem("square_ready"), 1)
                act.wait_ge(sem("square_used"), KC * (n + 1))
                nc.scalar.activation(rms[:, t0:], bank[4][:, 0:T - t0], ACT.Sqrt, bias=const("eps"), scale=1.0 / D)\
                    .then_inc(sem("rms_ready"), 1)
                if name.startswith("final") or t0:
                    return
                which = 1
                for kc in range(KC):
                    act.wait_ge(sem("h_scaled"), h_scaled_before(name) + kc + 1)
                    s, b = modulation(name, kc, which)
                    nc.scalar.activation(h[:, kc, 0:CTX], h[:, kc, 0:CTX], ACT.Identity, bias=b, scale=s)\
                        .then_inc(sem("h_ctx_ready"), 1)

            def swiglu(name, norm_name):
                f, t0 = SWIGLU.index(name), START[norm_name]

                def pairs(item_in_stage):
                    for sub in range(2):
                        act.wait_ge(sem("pair_ready"), item_in_stage * 2 + (2 * FFN_IN * f + sub + 1))
                        nc.scalar.activation(arena[:, item_in_stage * 2 + sub, t0:], bank[2 * sub][:, 0:T - t0], ACT.Silu)\
                            .then_inc(sem("silu_ready"), 1)

                looped = FFN_IN // RING
                with act.Fori(0, looped) as i:
                    for j in range(RING):
                        pairs(i * RING + j)
                for j in range(looped * RING, FFN_IN):
                    pairs(j)

            def mla_and_conv(i):
                tag, t0 = MIXERS[i], CTX if i == DEPTH - 1 else 0
                for c in range(3):
                    first = t0 if c < 2 else 0
                    act.wait_ge(sem(f"latent_moved{tag}"), c + 1)
                    nc.scalar.activation(squares[:, c, first:], latent[:, c, first:], ACT.Square)\
                        .then_inc(sem(f"latent_square{tag}"), 1)
                for n in range(8):
                    act.wait_ge(sem(f"conv_sum{tag}"), n + 1)
                    nc.scalar.activation(conv_in[:, n, t0:], bank[4 + n % 4][:, 0:T - t0], ACT.Copy)\
                        .then_inc(sem(f"conv_moved{tag}"), 1)
                    if n == 3:
                        for j, width in ((0, QR), (1, KVR)):
                            first = t0 if j == 0 else 0
                            act.wait_ge(sem(f"latent_norm_sum{tag}"), j + 1)
                            nc.scalar.activation(latent_rms[:, j, first:], bank[j][:, 0:T - first], ACT.Sqrt, bias=const("eps"),
                                                 scale=1.0 / width).then_inc(sem(f"latent_rms{tag}"), 1)
                for n in list(range(0, 16, 2)) + list(range(16, 20)):
                    act.wait_ge(sem(f"head_sum{tag}"), n + 1)
                    acc = bank[4 + n % 4]
                    if n < 16:
                        nc.scalar.activation(q_heads[0:QK, n // 2, t0:], acc[0:QK, 0:T - t0], ACT.Copy)\
                            .then_inc(sem(f"query_moved{tag}"), 1)
                    else:
                        nc.scalar.activation(values[:, n - 16, :], acc[:, :], ACT.Copy).then_inc(sem(f"query_moved{tag}"), 1)
                units = attention_units(t0)
                for n in range(len(units) + 2):
                    if n < len(units):
                        keys = units[n][2]
                        act.wait_ge(sem(f"negmax{tag}"), n + 1)
                        if n >= 3:
                            act.wait_ge(sem(f"prob_turned{tag}"), n - 2)
                        nc.scalar.activation(probs[:, n % 3, 0:keys], bank[SCORE_BANKS[n % 3]][:, 0:keys], ACT.Exp,
                                             bias=small[:, n % 4:n % 4 + 1], scale=SCALE,
                                             accum_out=small[:, 8 + n % 4:9 + n % 4]).then_inc(sem(f"exp{tag}"), 1)
                    m = n - 2
                    if m >= 0:
                        keys = units[m][2]
                        act.wait_ge(sem(f"prob_turned{tag}"), m + 1)
                        if m >= 2:
                            act.wait_ge(sem(f"attend_sum{tag}"), m - 1)
                        nc.scalar.activation(probs_turned[:, m % 2, 0:keys], bank[6 + m % 2][:, 0:keys], ACT.Copy)\
                            .then_inc(sem(f"prob_turned_moved{tag}"), 1)

            own = Chain(act, "scalar_own")

            def projections():
                act.wait_ge(sem("gate_abs"), 1)
                own.link(nc.scalar.activation(squares[:, 1, :], squares[:, 1, :], ACT.Exp, scale=-1.0))
                nc.scalar.activation(squares[:, 1, :], squares[:, 1, :], ACT.Ln, bias=const("ones", 0, 1)).then_inc(sem("gate_log"), 1)
                for k in range(2):
                    own.link(nc.scalar.activation(bounds[:, k, :, :], small[:, 56:64].rearrange("p (d c) -> p d c", d=2), ACT.Sigmoid,
                                                  scale=-1.0 if k else 1.0))
                own.link(nc.scalar.activation(small[:, 32:33], bounds[:, 0, 0, 0:1], ACT.Copy))
                nc.scalar.activation(small[:, 33:34], bounds[:, 0, 0, 0:1], ACT.Copy).then_inc(sem("bounds"), 1)
                for n, (name, c) in enumerate(UNITS_B):
                    act.wait_ge(sem("projection_sum"), n + 1)
                    acc = bank[n % 4]
                    if name == "ml_q":
                        last = nc.scalar.activation(q_raw[:, c, :], acc[:, 0:LAT], ACT.Copy)
                    elif name == "ml_k":
                        last = nc.scalar.activation(k_raw[:, c, :], acc[:, :], ACT.Copy)
                    elif name in ("hg_zf", "hg_zb"):
                        d = int(name == "hg_zb")
                        own.mark(nc.scalar.activation(decay[d][:, c, :], acc[:, :], ACT.Sigmoid))
                        last = nc.scalar.activation(k_hg[d][:, c, :], acc[:, :], ACT.Sigmoid, scale=-1.0)
                    elif name == "hg_q":
                        last = nc.scalar.activation(q_hg[:, c, :], acc[:, 0:LAT], ACT.Silu)
                    elif name == "ml_v":
                        last = nc.scalar.activation(v_ml[:, c, :], acc[:, :], ACT.Copy)
                    elif name == "hg_v":
                        last = nc.scalar.activation(v_hg[:, c, :], acc[:, :], ACT.Copy, scale=MSCALE)
                    elif name == "ml_o":
                        last = nc.scalar.activation(o_gate[:, c, :], acc[:, 0:LAT], ACT.Sigmoid)
                    else:
                        last = nc.scalar.activation(g_gate[:, c, :], acc[:, 0:LAT], ACT.Silu)
                    last.then_inc(sem("projected"), 1)
                    if (name, c) == ("hg_zb", 3):
                        own.wait(own.n)
                        for d in range(2):
                            for cc in range(4):
                                nc.scalar.activation(decay[d][:, cc, :], decay[d][:, cc, :], ACT.Ln, bias=bounds[:, 0, d, cc:cc + 1],
                                                     scale=bounds[:, 1, d, cc:cc + 1]).then_inc(sem("log_decay"), 1)
                for k, (what, count) in enumerate(((q_ml, 4), (k_ml, 8))):
                    act.wait_ge(sem("qk_conv"), count)
                    nc.scalar.activation(what, what, ACT.Silu).then_inc(sem("conv_silu"), 1)

            def hgrn():
                for n, stage in enumerate(HG_STAGES):
                    q, k = hg_factor[n % 2]
                    if stage in ("ctx0", "ctx1"):
                        d = n
                        act.wait_ge(sem("projected"), len(UNITS_B))
                        act.wait_ge(sem("decay_summed"), 16)
                        own.mark(nc.scalar.activation(q, decay[d][:, :, CTX:], ACT.Exp))
                        for hd in range(MH):
                            total = decay[d][:, hd, CTX - 1:CTX] if d == 0 else decay[d][:, hd, 0:1]
                            last = nc.scalar.activation(k[:, hd, :], decay[d][:, hd, 0:CTX], ACT.Exp, bias=total, scale=-1.0)
                            own.mark(last) if hd < MH - 1 else None
                        own.wait(own.n)
                        last.then_inc(sem("hg_exp"), 1)
                    elif stage != "diagonal":
                        act.wait_ge(sem("hg_differences"), n - 1)
                        nc.scalar.activation(hg_factors[n % 2], hg_factors[n % 2], ACT.Exp).then_inc(sem("hg_exp"), 1)
                for hd in range(MH):
                    act.wait_ge(sem("hg_product"), 2)
                    if hd >= 2:
                        act.wait_ge(sem("hg_out_sum"), hd - 1)
                    nc.scalar.activation(hg_ctx_scores[:, hd % 2, :], bank[hd][:, :], ACT.Copy).then_inc(sem("hg_ctx_moved"), 1)
                for hd in range(MH):
                    act.wait_ge(sem("hg_out_sum"), hd + 1)
                    nc.scalar.activation(hg_out[:, hd, :], bank[4 + hd][:, 0:LAT], ACT.Copy).then_inc(sem("hg_out_moved"), 1)

            def mlstm():
                for n in range(2 * MH):
                    hd, d = n // 2, n % 2
                    act.wait_ge(sem("ml_masked"), n + 1)
                    open_chunk = (2, P, LAT) if d == 0 else (3, 0, P)
                    for c, a, b in ((0, 0, LAT), (1, 0, LAT), open_chunk):
                        u = u_cols[:, MH * (4 * d + c) + hd:MH * (4 * d + c) + hd + 1]
                        nc.scalar.activation(ml_decay[d][:, c, a:b], bank[2 + d][:, a:b], ACT.Exp, bias=u, scale=-1.0)\
                            .then_inc(sem("ml_open"), 1)
                    for c in range(2):
                        block_ = ml_decay[d][:, 2 + c, c * P:(c + 1) * P]
                        last = nc.scalar.activation(block_, block_, ACT.Exp)
                        if c == 0:
                            own.mark(last)
                    own.wait(own.n)
                    last.then_inc(sem("ml_decayed"), 1)
                    if n >= 1:
                        num_out(n - 1)
                num_out(2 * MH - 1)
                for d in range(2):
                    nc.scalar.activation(ml_floor[:, d * LAT:(d + 1) * LAT], floor_rows[d], ACT.Exp).then_inc(sem("ml_floor"), 1)

            def num_out(n):
                act.wait_ge(sem("ml_num_sum"), n + 1)
                nc.scalar.activation(ml_num[:, n // 2, n % 2 * LAT:(n % 2 + 1) * LAT], bank[4 + n % 2][:, 0:LAT], ACT.Copy)\
                    .then_inc(sem("ml_num_moved"), 1)

            def head_norms():
                for j in range(8):
                    if j < MH:
                        act.wait_ge(sem("ml_out"), j + 1)
                    source = ml_out[:, j, :] if j < MH else hg_out[:, j - MH, :]
                    nc.scalar.activation(out_squares[:, j, :], source, ACT.Square).then_inc(sem("out_square"), 1)
                act.wait_ge(sem("out_norm_sum"), 1)
                nc.scalar.activation(out_rms, bank[4][0:8, 0:LAT], ACT.Sqrt, bias=const("eps", rows=8), scale=1.0 / P)\
                    .then_inc(sem("out_rms"), 1)

            def conv_ffn():
                def move(sub, p, first=False):
                    act.wait_ge(sem("up_sum"), p + 1)
                    if not first:
                        act.wait_ge(sem("hidden_b"), p)
                    for part in range(2):
                        own_sum = bank[2 * sub + part][:, 0:LAT]
                        nc.scalar.activation(raw_b[sub][part], own_sum, ACT.Copy).then_inc(sem("up_copied"), 1)
                        centre = params[:, bass.ds(p + (PARAMS["ffn_conv"][0] + 4 * 2 * FC + part * FC), 1)]
                        last = nc.scalar.activation(acc_b[sub][part], own_sum, ACT.Copy, scale=centre)
                        if part == 0:
                            last.then_inc(sem("up_copied"), 1)
                    last.then_inc(sem("up_moved"), 1)

                def gate(sub, p):
                    act.wait_ge(sem("tap"), p * N_TAPS + N_TAPS)
                    nc.scalar.activation(acc_b[sub][0], acc_b[sub][0], ACT.Silu).then_inc(sem("gate_b"), 1)

                move(0, 0, True)
                with act.Fori(0, (UP_B - 2) // 2) as i:
                    for sub in (1, 0):
                        p = i * 2 + (1 if sub else 2)
                        move(sub, p)
                        gate(1 - sub, i * 2 + (0 if sub else 1))
                move(1, UP_B - 1)
                gate(0, UP_B - 2)
                gate(1, UP_B - 1)

            act.wait_ge(loaded, 48)
            for i in range(DEPTH):
                conditioning(i, "c1", N_MOD * D // ITEM)
                norm(f"norm1{i}")
                swiglu(f"ffn1{i}", f"norm1{i}")
                norm(f"norm2{i}")
                mla_and_conv(i)
                norm(f"norm3{i}")
                swiglu(f"ffn2{i}", f"norm3{i}")
            norm("final1")
            if until is None:
                conditioning("b", "c2", N_MOD_2 * D // ITEM)
                act.wait_ge(sem("ctx2_loaded"), 16)
                norm("norm_a")
                projections()
                hgrn()
                mlstm()
                head_norms()
                norm("norm_b")
                conv_ffn()
                norm("final2")

        @block.vector
        def _(dve):
            own = Chain(dve, "vector_own")

            def conditioning(tag, n, bias, norms, halves):
                dve.wait_ge(sem(f"mod_turned{tag}"), n + 3)
                chunks = n * ITEM // P
                own.link(nc.vector.tensor_tensor(mod[:, 0:chunks, :], bank[7][:, 0:2 * chunks].rearrange("p (n c) -> p n c", c=2),
                                                 param(bias).unsqueeze(2).broadcast_to([P, chunks, 2]), ALU.add))
                for j, (name, first) in enumerate(norms):
                    last = nc.vector.scalar_tensor_tensor(scales[:, KC * j:KC * (j + 1), :], mod[:, first:first + KC, :], 1.0,
                                                          param(*name).unsqueeze(2).broadcast_to([P, KC, 2]), ALU.add, ALU.mult)
                    own.mark(last)
                for j, (first, factor) in enumerate(halves):
                    own.mark(nc.vector.tensor_scalar(gates[:, KC * j:KC * (j + 1), :], mod[:, first:first + KC, :], factor, None, ALU.mult))
                own.wait(own.n)
                nc.vector.memset(small[:, 63:64], 0.0).then_inc(sem("mod_ready"), 1)

            def norm(name):
                n, t0 = NORM_AT[name], START[name]
                dve.wait_ge(sem("rms_ready"), n + 1)
                own.link(nc.vector.reciprocal(rinv[:, t0:], rms[:, t0:]))
                if name.startswith("final"):
                    weight = "final1" if name == "final1" else "final2"
                    for kc in range(KC):
                        nc.vector.scalar_tensor_tensor(x[:, kc, t0:], x[:, kc, t0:], param(weight, kc, 1), rinv[:, t0:],
                                                       ALU.mult, ALU.mult).then_inc(x_updated, 1)
                    return
                for kc in range(KC + 1):
                    if kc < KC:
                        nc.vector.tensor_tensor(h[:, kc, t0:], x[:, kc, t0:], rinv[:, t0:], ALU.mult).then_inc(sem("h_scaled"), 1)
                    if kc > 0:
                        dve.wait_ge(sem("h_scaled"), h_scaled_before(name) + kc)
                        s, b = modulation(name, kc - 1, 0)
                        nc.vector.tensor_scalar(h[:, kc - 1, CTX:], h[:, kc - 1, CTX:], s, b, ALU.mult, ALU.add)\
                            .then_inc(sem("h_lat_ready"), 1)

            def swiglu(name, norm_name):
                f, t0 = SWIGLU.index(name), START[norm_name]

                def pairs(item_in_stage):
                    for sub in range(2):
                        dve.wait_ge(sem("silu_ready"), item_in_stage * 2 + (2 * FFN_IN * f + sub + 1))
                        hidden = arena[:, item_in_stage * 2 + sub, t0:]
                        nc.vector.tensor_tensor(hidden, hidden, bank[2 * sub + 1][:, 0:T - t0], ALU.mult)\
                            .then_inc(sem("hidden_ready"), 1)

                looped = FFN_IN // RING
                with dve.Fori(0, looped) as i:
                    for j in range(RING):
                        pairs(i * RING + j)
                for j in range(looped * RING, FFN_IN):
                    pairs(j)

            def update(name, t0, gate):
                before = KC * BANKED.index(name)
                for kc in range(KC):
                    dve.wait_ge(sem("acc_ready"), before + kc + 1)
                    acc = bank[kc - 4 if kc >= 4 else 4 + kc]
                    for start, which in ((0, 1), (CTX, 0)):
                        if start >= t0:
                            last = nc.vector.scalar_tensor_tensor(x[:, kc, start:start + CTX], acc[:, start - t0:start - t0 + CTX],
                                                                  gate(kc)[:, which:which + 1], x[:, kc, start:start + CTX],
                                                                  ALU.mult, ALU.add)
                    last.then_inc(x_updated, 1)

            def mla_and_conv(i):
                tag, t0 = MIXERS[i], CTX if i == DEPTH - 1 else 0
                for c in range(4):
                    first = t0 if c < 2 else 0
                    dve.wait_ge(sem(f"latent_sum{tag}"), c + 1)
                    target = latent[:, c, first:] if c < 3 else q_heads[:, HEADS, :]
                    nc.vector.tensor_copy(target, bank[c][:, 0:T - first]).then_inc(sem(f"latent_moved{tag}"), 1)
                for j in range(2):
                    first = t0 if j == 0 else 0
                    dve.wait_ge(sem(f"latent_rms{tag}"), j + 1)
                    own.link(nc.vector.reciprocal(latent_rinv[:, j, first:], latent_rms[:, j, first:]))
                    for c, w in ((0, param(f"q_norm{i}", 0, 1)), (1, param(f"q_norm{i}", 1, 1))) if j == 0 else \
                            ((2, param(f"kv_norm{i}")),):
                        nc.vector.scalar_tensor_tensor(latent[:, c, first:], latent[:, c, first:], w, latent_rinv[:, j, first:],
                                                       ALU.mult, ALU.mult).then_inc(sem(f"latent_ready{tag}"), 1)
                for c in range(4):
                    dve.wait_ge(sem(f"conv_sum{tag}"), 9 + c)
                    dve.wait_ge(sem(f"conv_moved{tag}"), 5 + c)
                    nc.vector.tensor_tensor(conv_in[:, 4 + c, t0:], conv_in[:, 4 + c, t0:], bank[4 + c][:, 0:T - t0], ALU.mult)\
                        .then_inc(sem(f"conv_u{tag}"), 1)

                def conv(c):
                    segments = (T - t0) // CTX
                    u = conv_in[:, 4 + c, t0:].rearrange("p (s t) -> p s t", s=segments)
                    gb = conv_in[:, c, t0:].rearrange("p (s t) -> p s t", s=segments)
                    y = h[:, 4 + c, t0:].rearrange("p (s t) -> p s t", s=segments)
                    w = lambda tap: param(f"conv{i}", 4 * tap + c, 1)
                    dve.wait_ge(sem(f"conv_u{tag}"), 4)
                    own.link(nc.vector.tensor_scalar(y, u, w(1), None, ALU.mult))
                    own.link(nc.vector.scalar_tensor_tensor(y[:, :, 1:], u[:, :, :-1], w(0), y[:, :, 1:], ALU.mult, ALU.add))
                    own.link(nc.vector.scalar_tensor_tensor(y[:, :, :-1], u[:, :, 1:], w(2), y[:, :, :-1], ALU.mult, ALU.add))
                    nc.vector.tensor_tensor(y, y, gb, ALU.mult).then_inc(sem(f"conv_out{tag}"), 1)

                for hd in range(HEADS):
                    dve.wait_ge(sem(f"head_sum{tag}"), 2 * hd + 2)
                    nc.vector.tensor_copy(k_heads[0:NOPE, hd, :], bank[4 + (2 * hd + 1) % 4][0:NOPE, :])\
                        .then_inc(sem(f"key_moved{tag}"), 1)
                    if hd % 2:
                        conv(hd // 2)
                R = slice(NOPE, QK)
                for r in range(5):
                    dve.wait_ge(sem(f"exchanged{tag}"), r + 1)
                    n = 1 if r == 0 else 2
                    f = q_heads[R, HEADS:HEADS + 1, CTX:] if r == 0 else q_heads[R, 2 * r - 2:2 * r, CTX:]
                    cos = const("cos")[R].unsqueeze(1).broadcast_to([ROPE, n, LAT])
                    sin = const("sin")[R].unsqueeze(1).broadcast_to([ROPE, n, LAT])
                    turned = rope_tmp[R, 0:n * LAT].rearrange("p (n t) -> p n t", n=n)
                    own.mark(nc.vector.tensor_tensor(turned, bank[r % 4][R, 0:n * LAT].rearrange("p (n t) -> p n t", n=n), sin, ALU.mult))
                    own.link(nc.vector.tensor_tensor(f, f, cos, ALU.mult))
                    nc.vector.tensor_tensor(f, f, turned, ALU.add).then_inc(sem(f"roped{tag}"), 1)
                    dve.wait_ge(sem(f"roped{tag}"), r + 1)
                units = attention_units(t0)
                for n in range(len(units) + 3):
                    if n < len(units):
                        keys = units[n][2]
                        dve.wait_ge(sem(f"score{tag}"), n + 1)
                        own.link(nc.vector.tensor_reduce(small[:, 24 + n % 4:25 + n % 4], bank[SCORE_BANKS[n % 3]][:, 0:keys],
                                                         axis=AX_X, op=ALU.max))
                        nc.vector.tensor_scalar(small[:, n % 4:n % 4 + 1], small[:, 24 + n % 4:25 + n % 4], -SCALE, None, ALU.mult)\
                            .then_inc(sem(f"negmax{tag}"), 1)
                    m = n - 1
                    if 0 <= m < len(units):
                        keys = units[m][2]
                        dve.wait_ge(sem(f"exp{tag}"), m + 1)
                        own.link(nc.vector.reciprocal(small[:, 16 + m % 4:17 + m % 4], small[:, 8 + m % 4:9 + m % 4]))
                        nc.vector.tensor_scalar(probs[:, m % 3, 0:keys], probs[:, m % 3, 0:keys], small[:, 16 + m % 4:17 + m % 4],
                                                None, ALU.mult).then_inc(sem(f"prob{tag}"), 1)
                    m = n - 3
                    if 0 <= m < len(units):
                        hd, tc, _ = units[m]
                        half = slice(VD * (hd % 2), VD * (hd % 2) + VD)
                        dve.wait_ge(sem(f"attend_sum{tag}"), m + 1)
                        nc.vector.tensor_copy(h[half, hd // 2, tc * P:(tc + 1) * P], bank[m % 2][half, 0:P])\
                            .then_inc(sem(f"attended{tag}"), 1)

            def gate_rows():
                dve.wait_ge(loaded, 48)
                logits = param("lb").rearrange("p (d l c) -> p d l c", d=2, l=2)
                own.mark(nc.vector.tensor_tensor(small[:, 56:64].rearrange("p (d c) -> p d c", d=2), logits[:, :, 0, :], logits[:, :, 1, :],
                                                 ALU.subtract))
                dve.wait_ge(sem("gate_sum"), 1)
                g = squares[:, 0, :]
                own.link(nc.vector.tensor_scalar(g, bank[5][:, :], param("gate_b"), None, ALU.add))
                nc.vector.scalar_tensor_tensor(squares[:, 1, :], g, -1.0, g, ALU.mult, ALU.max).then_inc(sem("gate_abs"), 1)
                dve.wait_ge(sem("gate_log"), 1)
                log_f = squares[:, 1, :]
                own.link(nc.vector.scalar_tensor_tensor(log_f, g, 0.0, log_f, ALU.min, ALU.subtract))

                def segments(a, backwards):
                    v = a.rearrange("p (s t) -> p s t", s=2)
                    return v[:, :, ::-1] if backwards else v

                sums = [squares[0:MH, 2, :], squares[0:MH, 3, :]]
                u_back = arena[0:MH, 43, :]
                own.mark(nc.vector.tensor_copy(sums[0], squares[32:32 + MH, 1, :]))
                own.mark(nc.vector.tensor_copy(segments(sums[1], False), segments(squares[96:96 + MH, 1, :], True)))
                own.link(nc.vector.tensor_copy(segments(u_back, False), segments(squares[64:64 + MH, 0, :], True)))
                for d in range(2):
                    own.link(nc.vector.tensor_tensor_scan(sums[d], sums[d], sums[d], 0.0, ALU.add, ALU.bypass))
                own.mark(nc.vector.tensor_tensor(u_rows[0], squares[0:MH, 0, :], sums[0], ALU.subtract))
                own.link(nc.vector.tensor_tensor(u_back, u_back, sums[1], ALU.subtract))
                maxima = [rms[0:MH, :], rinv[0:MH, :]]
                for d, u in enumerate((u_rows[0], u_back)):
                    own.link(nc.vector.tensor_tensor_scan(maxima[d], u, u, 0.0, ALU.max, ALU.bypass))
                for d in range(2):
                    own.link(nc.vector.scalar_tensor_tensor(sums[d][:, CTX:], maxima[d][:, CTX:], -1.0, sums[d][:, CTX:],
                                                            ALU.mult, ALU.subtract))
                own.mark(nc.vector.tensor_copy(segments(u_rows[1], False), segments(u_back, True)))
                own.mark(nc.vector.tensor_copy(m_rows[1], maxima[1][:, CTX:][:, ::-1]))
                own.mark(nc.vector.tensor_copy(floor_rows[1], sums[1][:, CTX:][:, ::-1]))
                own.wait(own.n)
                nc.vector.memset(small[:, 39:40], 0.0).then_inc(sem("gate_rows"), 1)

            def qk_conv():
                for group in range(2):
                    done = {}

                    def weight(tap, c):
                        return param("qk_conv", KC * tap + 4 * group + c, 1)

                    windows = [("lat", ROWS, GRID)] + ([("ctx", 1, CTX)] if group else [])
                    for which, rows, cols in windows:
                        dve.wait_ge(sem("projected"), 4 * (group + 1))
                        raws = [(q_raw[:, c, :] if group == 0 else k_raw[:, c, CTX:]) if which == "lat" else k_raw[:, c, 0:CTX] for c in range(4)]
                        outs = [(q_ml[:, c, :] if group == 0 else k_ml[:, c, CTX:]) if which == "lat" else k_ml[:, c, 0:CTX] for c in range(4)]
                        raws = [r.rearrange("p (r c) -> p r c", c=cols) for r in raws]
                        outs = [r.rearrange("p (r c) -> p r c", c=cols) for r in outs]
                        for c in range(4):
                            done[c] = own.mark(nc.vector.tensor_scalar(outs[c], raws[c], weight(4, c), None, ALU.mult))
                        for tap, (ro, co), (ri, ci) in taps(rows, cols):
                            for c in range(4):
                                own.wait(done[c])
                                to = outs[c][:, ro, co]
                                done[c] = own.mark(nc.vector.scalar_tensor_tensor(to, raws[c][:, ri, ci], weight(tap, c), to, ALU.mult, ALU.add))
                    own.wait(own.n)
                    dve.sem_inc(sem("qk_conv"), 4)

            def hgrn():
                dve.wait_ge(sem("bounds"), 1)
                dve.wait_ge(sem("projected"), 16)
                for d in range(2):
                    for c in range(4):
                        own.mark(nc.vector.tensor_scalar(k_hg[d][:, c, :], k_hg[d][:, c, :], bounds[:, 1, d, c:c + 1], None, ALU.mult))
                for d in range(2):
                    for c in range(4):
                        dve.wait_ge(sem("log_decay"), 4 * d + c + 1)
                        for s in range(2):
                            part = decay[d][:, c, s * CTX:(s + 1) * CTX]
                            part = part[:, ::-1] if d else part
                            nc.vector.tensor_tensor_scan(part, part, part, 0.0, ALU.add, ALU.bypass).then_inc(sem("decay_summed"), 1)
                dve.wait_ge(sem("decay_summed"), 16)
                dve.wait_ge(sem("qk_conv"), 8)
                own.wait(own.n)

                def blocks(a, size):
                    return a.rearrange("p h (n two b) -> p h n two b", two=2, b=size)

                def differences(n):
                    stage = HG_STAGES[n]
                    dve.wait_ge(sem("hg_product"), n - 1)
                    if stage == "diagonal":
                        return
                    size = 1 << stage
                    q, k = (blocks(f, size) for f in hg_factor[n % 2])
                    f, b = (blocks(decay[d][:, :, CTX:], size) for d in range(2))
                    shape = [P, MH, LAT // (2 * size), size]
                    last_left = f[:, :, :, 0, size - 1:size].broadcast_to(shape)
                    first_right = b[:, :, :, 1, 0:1].broadcast_to(shape)
                    last = None
                    for out_, a, c in ((q[:, :, :, 1, :], f[:, :, :, 1, :], last_left), (k[:, :, :, 0, :], last_left, f[:, :, :, 0, :]),
                                       (q[:, :, :, 0, :], b[:, :, :, 0, :], first_right), (k[:, :, :, 1, :], first_right, b[:, :, :, 1, :])):
                        if last is not None:
                            own.mark(last)
                        last = nc.vector.tensor_tensor(out_, a, c, ALU.subtract)
                    last.then_inc(sem("hg_differences"), 1)

                def scale(n):
                    stage = HG_STAGES[n]
                    q, k = hg_factor[n % 2]
                    if stage == "diagonal":
                        nc.vector.tensor_tensor(k, k_hg[0][:, :, CTX:], k_hg[1][:, :, CTX:], ALU.add).then_inc(sem("hg_scaled"), 1)
                        return
                    dve.wait_ge(sem("hg_exp"), n + 1)
                    own.mark(nc.vector.tensor_tensor(q, q, q_hg, ALU.mult))
                    if stage in ("ctx0", "ctx1"):
                        last = nc.vector.tensor_tensor(k, k, k_hg[n][:, :, 0:CTX], ALU.mult)
                    else:
                        kb = blocks(k, 1 << stage)
                        for d in range(2):
                            source = blocks(k_hg[d][:, :, CTX:], 1 << stage)
                            last = nc.vector.tensor_tensor(kb[:, :, :, d, :], kb[:, :, :, d, :], source[:, :, :, d, :], ALU.mult)
                            if d == 0:
                                own.mark(last)
                    own.wait(own.n)
                    last.then_inc(sem("hg_scaled"), 1)

                def place(n):
                    stage = HG_STAGES[n]
                    dve.wait_ge(sem("hg_product"), n + 1)
                    for c in range(2):
                        scores = bank[4 + 2 * (n % 2) + c][:, :].rearrange("p (h t) -> p h t", h=MH)
                        if stage == LEVELS:
                            last = nc.vector.tensor_copy(hg_scores[:, :, c, (1 - c) * P:(2 - c) * P], scores)
                        else:
                            level = LEVELS if stage == "diagonal" else stage
                            mask = const("level", level * P, P).bitcast(U32).unsqueeze(1).broadcast_to([P, MH, P])
                            last = nc.vector.copy_predicated(hg_scores[:, :, c, c * P:(c + 1) * P], mask, scores)
                        if c == 0:
                            own.mark(last)
                    own.wait(own.n)
                    last.then_inc(sem("hg_placed"), 1)

                own.link(nc.vector.memset(hg_scores, 0.0))
                scale(0)
                differences(2)
                scale(1)
                for n in range(3, len(HG_STAGES)):
                    differences(n)
                    scale(n - 1)
                    if n >= 4:
                        place(n - 2)
                place(len(HG_STAGES) - 2)
                scale(len(HG_STAGES) - 1)
                place(len(HG_STAGES) - 1)

            def mlstm():
                dve.wait_ge(sem("u_turned"), 1)
                nc.vector.tensor_copy(u_cols, bank[2][:, 0:2 * 4 * MH]).then_inc(sem("u_cols"), 1)
                dve.wait_ge(sem("u_cols"), 1)

                def mask(n):
                    hd, d = n // 2, n % 2
                    dve.wait_ge(sem("ml_max"), n + 1)
                    for c in range(2):
                        u = u_cols[:, MH * (4 * d + 2 + c) + hd:MH * (4 * d + 2 + c) + hd + 1]
                        last = nc.vector.scalar_tensor_tensor(ml_decay[d][:, 2 + c, c * P:(c + 1) * P], const("causal", d * P, P), u,
                                                              bank[2 + d][:, c * P:(c + 1) * P], ALU.add, ALU.subtract)
                        if c == 0:
                            own.mark(last)
                    own.wait(own.n)
                    last.then_inc(sem("ml_masked"), 1)

                def weigh(n):
                    hd, d = n // 2, n % 2
                    dve.wait_ge(sem("ml_score"), hd + 1)
                    dve.wait_ge(sem("ml_decayed"), n + 1)
                    if n >= 2:
                        dve.wait_ge(sem("ml_num_sum"), n - 1)
                    own.mark(nc.vector.scalar_tensor_tensor(ml_weight[d][:, 0:2, :], bank[0][:, :].rearrange("p (c t) -> p c t", c=2), MSCALE,
                                                            ml_decay[d][:, 0:2, :], ALU.mult, ALU.mult))
                    for c in range(2):
                        a, b = lat_valid(d, c)
                        last = nc.vector.scalar_tensor_tensor(ml_weight[d][:, 2 + c, a:b], bank[1][:, c * LAT + a:c * LAT + b], MSCALE,
                                                              ml_decay[d][:, 2 + c, a:b], ALU.mult, ALU.mult)
                        if c == 0:
                            own.mark(last)
                    own.wait(own.n)
                    last.then_inc(sem("ml_weighted"), 1)

                mask(0)
                for n in range(2 * MH):
                    if n + 1 < 2 * MH:
                        mask(n + 1)
                    weigh(n)
                dve.wait_ge(sem("ml_num_sum"), 2 * MH)
                for d in range(2):
                    own.mark(nc.vector.tensor_copy(ml_den[:, d * LAT:(d + 1) * LAT], bank[6 + d][0:MH, 0:LAT]))
                own.wait(own.n)
                own.link(nc.vector.scalar_tensor_tensor(ml_den, ml_den, -1.0, ml_den, ALU.mult, ALU.max))
                dve.wait_ge(sem("ml_floor"), 2)
                own.link(nc.vector.tensor_tensor(ml_den, ml_den, ml_floor, ALU.max))
                nc.vector.reciprocal(ml_den, ml_den).then_inc(sem("ml_den_ready"), 1)
                dve.wait_ge(sem("ml_num_moved"), 2 * MH)
                for hd in range(MH):
                    dve.wait_ge(sem("ml_den_spread"), hd + 1)
                    own.link(nc.vector.tensor_tensor(ml_num[:, hd, :], ml_num[:, hd, :], bank[hd][:, :], ALU.mult))
                    nc.vector.tensor_tensor(ml_out[:, hd, :], ml_num[:, hd, 0:LAT], ml_num[:, hd, LAT:], ALU.add).then_inc(sem("ml_out"), 1)

            def head_norms():
                dve.wait_ge(sem("out_rms"), 1)
                nc.vector.reciprocal(out_rinv, out_rms).then_inc(sem("out_rinv"), 1)
                for j in range(8):
                    source = ml_out[:, j, :] if j < MH else hg_out[:, j - MH, :]
                    gate = o_gate[:, j, :] if j < MH else g_gate[:, j - MH, :]
                    weight = param("ml_norm", j, 1) if j < MH else param("hg_norm", j - MH, 1)
                    dve.wait_ge(sem("out_rinv_spread"), 8 if j % 2 == 0 else j + 1)
                    own.link(nc.vector.scalar_tensor_tensor(h[:, j, CTX:], source, weight, bank[j // 2][:, j % 2 * LAT:(j % 2 + 1) * LAT],
                                                            ALU.mult, ALU.mult))
                    nc.vector.tensor_tensor(h[:, j, CTX:], h[:, j, CTX:], gate, ALU.mult).then_inc(sem("mixed_b"), 1)

            def conv_ffn():
                def convolve(sub, p):
                    k = 0
                    dve.wait_ge(sem("up_moved"), p + 3)
                    for tap, (ro, co), (ri, ci) in taps(ROWS, GRID):
                        for part in range(2):
                            raw = raw_b[sub][part].rearrange("p (r c) -> p r c", c=GRID)
                            acc = acc_b[sub][part].rearrange("p (r c) -> p r c", c=GRID)
                            w = params[:, bass.ds(p + (PARAMS["ffn_conv"][0] + tap * 2 * FC + part * FC), 1)]
                            if k >= 2:
                                dve.wait_ge(sem("tap"), p * N_TAPS + (k - 1))
                            last = nc.vector.scalar_tensor_tensor(acc[:, ro, co], raw[:, ri, ci], w, acc[:, ro, co], ALU.mult, ALU.add)
                            last.then_inc(sem("tap"), 1)
                            k += 1

                def finish(sub, p):
                    dve.wait_ge(sem("gate_b"), p + 1)
                    nc.vector.tensor_tensor(arena[:, p, CTX:], acc_b[sub][0], acc_b[sub][1], ALU.mult).then_inc(sem("hidden_b"), 1)

                dve.sem_inc(sem("hidden_b"), 1)
                convolve(0, 0)
                with dve.Fori(0, (UP_B - 2) // 2) as i:
                    for sub in (1, 0):
                        convolve(sub, i * 2 + (1 if sub else 2))
                        finish(1 - sub, i * 2 + (0 if sub else 1))
                convolve(1, UP_B - 1)
                finish(0, UP_B - 2)
                finish(1, UP_B - 1)

            dve.wait_ge(loaded, 48)
            nc.vector.memset(cond[:, :, :], 0.0).then_inc(sem("cond_zero"), 1)
            for i in range(DEPTH):
                t0 = CTX if i == DEPTH - 1 else 0
                conditioning(i, N_MOD * D // ITEM, f"b_ada{i}",
                             [((f"norm{i}", KC * j, KC), KC * (3 * j + 1)) for j in range(3)],
                             [(KC * (3 * j + 2), 1.0 if j == 1 else 0.5) for j in range(3)])
                gate = lambda j: (lambda kc: gates[:, KC * j + kc, :])
                norm(f"norm1{i}")
                swiglu(f"ffn1{i}", f"norm1{i}")
                update(f"ffn1{i}", 0, gate(0))
                norm(f"norm2{i}")
                mla_and_conv(i)
                update(f"mix{i}", t0, gate(1))
                norm(f"norm3{i}")
                swiglu(f"ffn2{i}", f"norm3{i}")
                update(f"ffn2{i}", t0, gate(2))
            norm("final1")
            if until is None:
                conditioning("b", N_MOD_2 * D // ITEM, "b_mod", [(("norm_a",), KC), (("norm_b",), 4 * KC)],
                             [(2 * KC, 1.0), (5 * KC, 1.0)])
                dve.wait_ge(sem("ctx2_loaded"), 16)
                norm("norm_a")
                gate_rows()
                qk_conv()
                hgrn()
                mlstm()
                head_norms()
                update("mix_b", CTX, gate(0))
                norm("norm_b")
                conv_ffn()
                update("ffn_b", CTX, gate(1))
                norm("final2")

        @block.gpsimd
        def _(pool):
            for i in range(DEPTH):
                tag = MIXERS[i]
                pool.wait_ge(sem(f"roped{tag}"), 1)
                nc.gpsimd.tensor_copy(k_heads[NOPE:QK, :, :], q_heads[NOPE:QK, HEADS, :].unsqueeze(1).broadcast_to([ROPE, HEADS, T]))\
                    .then_inc(sem(f"key_rope{tag}"), 1)
            if until is None:
                pool.wait_ge(x_updated, KC * UPDATED["norm_a"])
                pool.dma_start(x[:, :, 0:CTX], ctx2_in).then_inc(sem("ctx2_loaded"), 16)
                pool.wait_ge(sem("ctx2_loaded"), 16)




def columns(v):
    v = np.asarray(v)
    return v.reshape(-1, P).T


def lay_params(a):
    out = np.zeros((P, N_PARAMS), np.float32)

    def put(name, value, rows=P):
        first, width = PARAMS[name]
        out[0:rows, first:first + value.shape[1]] = value

    for i in range(DEPTH):
        put(f"norm{i}", columns(a["norm_w"][i].reshape(-1)))
        put(f"b_ada{i}", columns(a["b_ada"][i]))
        put(f"q_norm{i}", columns(a["q_norm_w"][i]))
        put(f"kv_norm{i}", columns(a["kv_norm_w"][i]))
        put(f"conv{i}", columns(a["conv_w"][i].reshape(-1)))
    put("final1", columns(a["final_norm_w"]))
    put("c1", np.stack([columns(a["c"][0]), columns(a["c_ctx"])], 2).reshape(P, -1))
    put("c2", np.stack([columns(a["c_2"][0]), columns(a["c_ctx_2"])], 2).reshape(P, -1))
    put("b_mod", columns(a["b_mod_2"][0]))
    put("norm_a", columns(a["norm1_w_2"][0]))
    put("norm_b", columns(a["norm2_w_2"][0]))
    gate_b = np.zeros((P, 1), np.float32)
    w_gate = np.zeros((KC, P, P), np.float32)
    g0 = 4 * MH * P
    for j in range(4):
        gate_b[32 * j:32 * j + MH, 0] = a["mlstm_gate_b_2"][0, MH * j:MH * (j + 1)]
        w_gate[:, :, 32 * j:32 * j + MH] = a["w_in_2"][0][:, g0 + MH * j:g0 + MH * (j + 1)].reshape(KC, P, MH)
    put("gate_b", gate_b)
    put("w_gate", w_gate.transpose(1, 0, 2).reshape(P, -1))
    put("qk_conv", columns(a["mlstm_conv_w_2"][0].reshape(-1)))
    put("ml_norm", columns(a["mlstm_norm_w_2"][0]))
    put("lb", columns(a["hgrn_lb_logits_2"].reshape(-1)))
    put("hg_norm", columns(a["hgrn_norm_w_2"][0]))
    put("ffn_conv", columns(a["ffn_conv_w_2"][0].reshape(-1)))
    put("final2", columns(a["final_norm_w_2"]))
    return out


def lay_consts():
    out = np.zeros((P, N_CONSTS), np.float32)

    def put(name, value, first_row=0):
        first, _ = CONSTS[name]
        out[first_row:first_row + value.shape[0], first:first + value.shape[1]] = value

    put("ident", np.eye(P, dtype=np.float32))
    put("ones", np.ones((P, P), np.float32))
    put("sum_rows", (np.arange(P)[:, None] % 32 == np.arange(2)[None, :]).astype(np.float32))
    put("eps", np.full((P, 1), EPS, np.float32))
    axis, half = ROPE // 2, ROPE // 4
    inv = np.float32(10000.0) ** (-np.arange(0, axis, 2, dtype=np.float32) / np.float32(axis))
    t = np.arange(LAT)
    angle = np.concatenate([np.outer(inv, (t // GRID).astype(np.float32))] * 2
                           + [np.outer(inv, (t % GRID).astype(np.float32))] * 2)
    put("cos", np.cos(angle), NOPE)
    put("sin", np.sin(angle), NOPE)
    perm = np.zeros((P, P), np.float32)
    for d in range(ROPE):
        low = d % axis < half
        perm[NOPE + (d + half if low else d - half), NOPE + d] = -1.0 if low else 1.0
    put("perm", perm)
    s, t = np.arange(P)[:, None], np.arange(P)[None, :]
    for j in range(LEVELS):
        put_at = (s >> (j + 1) == t >> (j + 1)) & (s >> j != t >> j)
        out[:, CONSTS["level"][0] + j * P:CONSTS["level"][0] + (j + 1) * P] = put_at
    out[:, CONSTS["level"][0] + LEVELS * P:CONSTS["level"][0] + (LEVELS + 1) * P] = s == t
    put("causal", np.concatenate([np.where(s <= t, 0.0, NEG), np.where(s >= t, 0.0, NEG)], 1).astype(np.float32))
    for j in range(8):
        out[j, CONSTS["row_of"][0] + j * P:CONSTS["row_of"][0] + (j + 1) * P] = 1.0
        out[:, CONSTS["col_of"][0] + 8 * j + j] = 1.0
    return out


def lay_stream(a):
    out = np.zeros((N_ITEMS, P, KC, ITEM), np.float32)

    def rows(w):
        return w.reshape(-1, P, w.shape[1]).transpose(1, 0, 2)

    def by_columns(first, w):
        for j in range(-(-w.shape[1] // ITEM)):
            part = rows(w[:, j * ITEM:(j + 1) * ITEM])
            out[first + j, :, 0:part.shape[1], 0:part.shape[2]] = part

    def gate_and_value(first, w):
        for j in range(FFN_IN):
            out[first + j, :, :, 0:ITEM // 2] = rows(w[:, j * ITEM // 2:(j + 1) * ITEM // 2])
            out[first + j, :, :, ITEM // 2:] = rows(w[:, FF + j * ITEM // 2:FF + (j + 1) * ITEM // 2])

    def down(first, w):
        for half in range(2):
            for g in range(3):
                part = rows(w[g * KC * P:(g + 1) * KC * P, half * ITEM:(half + 1) * ITEM])
                out[first + 3 * half + g, :, 0:part.shape[1], :] = part

    for i in range(DEPTH):
        by_columns(ITEMS[f"ada{i}"], a["w_ada"][i])
        gate_and_value(ITEMS[f"up1{i}"], a["w_ffn1_in"][i])
        down(ITEMS[f"down1{i}"], a["w_ffn1_out"][i])
        w = a["w_in"][i]
        latents = np.zeros((D, ITEM), np.float32)
        latents[:, 0:QR + KVR] = w[:, 0:QR + KVR]
        latents[:, QR + KVR + NOPE:QR + KVR + QK] = w[:, QR + KVR:QR + KVR + ROPE]
        by_columns(ITEMS[f"in{i}"], latents)
        by_columns(ITEMS[f"in{i}"] + 1, w[:, QR + KVR + ROPE:])
        flat = out[ITEMS[f"uqkv{i}"]].reshape(P, KC * ITEM)
        flat[:, 0:2 * HEADS * QK] = rows(a["w_uq"][i]).reshape(P, -1)
        flat[:, 2 * HEADS * QK:2 * HEADS * QK + HEADS * (NOPE + VD)] = a["w_ukv"][i]
        by_columns(ITEMS[f"out{i}"], a["w_out"][i])
        gate_and_value(ITEMS[f"up2{i}"], a["w_ffn2_in"][i])
        down(ITEMS[f"down2{i}"], a["w_ffn2_out"][i])
    by_columns(ITEMS["mod"], a["w_mod_2"][0])
    w, width = a["w_in_2"][0], MH * P
    hg = 4 * width + 4 * MH
    for j, first in enumerate(PROJECTIONS.values()):
        by_columns(ITEMS["in"] + j, w[:, first(width, hg):first(width, hg) + width])
    by_columns(ITEMS["out"], a["w_out_2"][0])
    gate_and_value(ITEMS["up"], a["w_up_2"][0])
    down(ITEMS["down"], a["w_down_2"][0])
    return out


def feature_major(a):
    return np.ascontiguousarray(a.T.reshape(KC, P, -1).transpose(1, 0, 2))


def lay_out(a):
    return {
        "stream": lay_stream(a),
        "x_in": feature_major(np.concatenate([a["ctx"][0], a["x"][0]], 0)),
        "ctx2_in": feature_major(a["ctx_2"][0]),
        "params_in": lay_params(a),
        "consts_in": lay_consts(),
    }


def kernel(**inputs):
    import concourse.bacc as bacc
    from concourse.bass_utils import run_bass_kernel_spmd

    nc = bacc.Bacc("TRN2", target_bir_lowering=False, num_devices=1)
    arrays = lay_out({k: np.asarray(v) for k, v in inputs.items()})
    args = [nc.dram_tensor(n, v.shape, F32, kind="ExternalInput").ap() for n, v in arrays.items()]
    out = nc.dram_tensor("out", (P, KC, LAT), F32, kind="ExternalOutput").ap()
    build_program(nc, *args, out)
    result = run_bass_kernel_spmd(nc, [arrays], core_ids=[0])
    out = result.results[0]["out"]
    return np.ascontiguousarray(out.transpose(1, 0, 2).reshape(D, LAT).T)[None]
```

```python
from contextlib import ExitStack

import numpy as np

import concourse.bass as bass
from concourse import mybir

F32 = mybir.dt.float32
F32R = mybir.dt.float32r
U32 = mybir.dt.uint32
ACT = mybir.ActivationFunctionType
ALU = mybir.AluOpType
AX_X = mybir.AxisListType.X

P = 128
D = 1024
KC = D // P
CTX, LAT = 256, 256
T = CTX + LAT
FF = 2816
FC = FF // P
DEPTH = 2
N_MOD, N_MOD_2 = 9, 6
HEADS, NOPE, ROPE, VD = 8, 64, 32, 64
QK = NOPE + ROPE
QR, KVR = 256, 128
CONV = 512
GRID = 64
ROWS = LAT // GRID
EPS = 1e-6
SCALE = QK ** -0.5
UNIT = 2 * P
RING = 3
MH = 4
MSCALE = P ** -0.5
NEG = -1.0e30



def _columns(parts):
    at, where = 0, {}
    for name, n in parts:
        where[name] = (at, n)
        at += n
    return where, at


PARAMS, N_PARAMS = _columns(
    [(f"norm{i}", 3 * KC) for i in range(DEPTH)] + [(f"b_ada{i}", N_MOD * KC) for i in range(DEPTH)]
    + [(f"q_norm{i}", QR // P) for i in range(DEPTH)] + [(f"kv_norm{i}", 1) for i in range(DEPTH)]
    + [(f"conv{i}", 3 * (CONV // P)) for i in range(DEPTH)]
    + [("final1", KC), ("c1", 2 * KC), ("c2", 2 * KC), ("b_mod", N_MOD_2 * KC), ("norm_a", KC), ("norm_b", KC),
       ("gate_b", 1), ("qk_conv", 9 * KC), ("ml_norm", MH), ("lb", 2 * 2 * MH), ("hg_norm", MH),
       ("ffn_conv", 9 * 2 * FC), ("final2", KC)])
LEVELS = 7
CONSTS, N_CONSTS = _columns(
    [("ident", P), ("ones", P), ("sum_rows", 2), ("perm", P), ("cos", LAT), ("sin", LAT), ("eps", 1),
     ("level", (LEVELS + 1) * P), ("causal", 2 * P), ("col_of", 8 * 8)])

UP = FC
GROUPS = (KC, KC, FC - 2 * KC)
SIDES = {"ada0": N_MOD * D // UNIT, "ada1": N_MOD * D // UNIT, "mod": N_MOD_2 * D // UNIT}
SIDE_UNITS = [(name, j) for name, n in SIDES.items() for j in range(n)]
FIRST_SIDES = 2 * D // UNIT
SWIGLU = {"10": (UP - 1, 10), "20": (UP - 1, 12), "11": (UP - 1, 3), "21": (0, 0)}


def _order():
    order, sides = [], iter(SIDE_UNITS)
    order += [next(sides) for _ in range(FIRST_SIDES)]
    for i in range(DEPTH):
        for n in (1, 2):
            name = f"{n}{i}"
            with_up, with_down = SWIGLU[name]
            for p in range(UP):
                order += [next(sides)] if with_up and p else []
                order.append((f"up{name}", p))
            for j in range(4 * len(GROUPS)):
                order += [next(sides)] if j < with_down else []
                order.append((f"down{name}", j))
            if n == 1:
                order += [(f"in{i}", j) for j in range(8)] + [(f"uq{i}", 0), (f"ukv{i}", 0)] + [(f"out{i}", j) for j in range(4)]
    order += [("gate", 0)] + [("in", j) for j in range(18)] + [("out", j) for j in range(4)]
    order += [("up", j) for j in range(UP)] + [("down", j) for j in range(4 * len(GROUPS))]
    assert next(sides, None) is None
    return order


ORDER = _order()
AT = {unit: at for at, unit in enumerate(ORDER)}
N_UNITS = -(-len(ORDER) // RING) * RING

PROJECTIONS = {
    "ml_q": lambda w, hg: 0, "ml_k": lambda w, hg: w, "hg_zf": lambda w, hg: hg + w, "hg_zb": lambda w, hg: hg + 2 * w,
    "hg_q": lambda w, hg: hg, "ml_v": lambda w, hg: 2 * w, "hg_v": lambda w, hg: hg + 3 * w,
    "ml_o": lambda w, hg: 3 * w, "hg_g": lambda w, hg: hg + 4 * w}



def build_program(nc, stream, x_in, ctx2_in, params_in, consts_in, out, until=None):
    with ExitStack() as stack:
        def sb(name, shape):
            return stack.enter_context(nc.sbuf_tensor(name, shape, F32))

        raw = [sb(f"raw{s}", [P, KC, UNIT]) for s in range(RING)]
        x = sb("x", [P, KC, T])
        squares = sb("squares", [P, 4, T])
        rms = sb("rms", [P, T])
        rinv = sb("rinv", [P, T])
        params = sb("params", [P, N_PARAMS])
        consts = sb("consts", [P, N_CONSTS])
        cond = sb("cond", [P, 2, KC, 32])
        mods = [sb(f"mod_{name}", [P, n * UNIT // P, 2]) for name, n in SIDES.items()]
        scales = sb("scales", [P, KC, 2])
        gates = sb("gates", [P, KC, 2])
        side_row = sb("side_row", [P, UNIT])
        small = sb("small", [P, 64])
        w_hi = stack.enter_context(nc.sbuf_tensor("w_hi", [P, 2, KC, P], F32R))
        w_lo = stack.enter_context(nc.sbuf_tensor("w_lo", [P, 2, KC, P], F32R))
        with ExitStack() as shared:
            h_hi = shared.enter_context(nc.sbuf_tensor("h_hi", [P, KC, T], F32R))
            h_lo = shared.enter_context(nc.sbuf_tensor("h_lo", [P, KC, T], F32R))
            hidden_hi = shared.enter_context(nc.sbuf_tensor("hidden_hi", [P, FC, T], F32R))
            hidden_lo = shared.enter_context(nc.sbuf_tensor("hidden_lo", [P, FC, T], F32R))
        h = sb("h", [P, 2 * KC, T])
        arena = sb("arena", [P, 2 * FC, T])
        bank = [stack.enter_context(nc.psum_tensor(f"bank{b}", [P, 512], F32)) for b in range(8)]
        sems = {}

        def sem(name):
            if name not in sems:
                sems[name] = stack.enter_context(nc.semaphore(name))
            return sems[name]

        def param(name, a=0, n=None):
            first, width = PARAMS[name]
            return params[:, first + a:first + a + (width - a if n is None else n)]

        def const(name, a=0, n=None, rows=P):
            first, width = CONSTS[name]
            return consts[0:rows, first + a:first + a + (width - a if n is None else n)]

        ident, ones = const("ident"), const("ones")

        unit_full = [sem(f"unit_full{s}") for s in range(RING)]
        unit_begun = sem("unit_begun")
        half_begun = sem("half_begun")
        half_high = sem("half_high")
        half_ready = sem("half_ready")
        loaded = sem("inputs_loaded")
        x_updated = sem("x_updated")

        UPDATES = [f"{s}{i}" for i in range(DEPTH) for s in ("ffn1", "mix", "ffn2")]
        BANKED = UPDATES + ["mix_b", "ffn_b"]
        NORMS = [(f"norm{n + 1}{i}", 3 * i + n, CTX if i == DEPTH - 1 and n == 2 else 0)
                 for i in range(DEPTH) for n in range(3)]
        NORMS += [("final1", 3 * DEPTH, CTX), ("norm_a", 3 * DEPTH + 1, 0), ("norm_b", 3 * DEPTH + 2, CTX),
                  ("final2", 3 * DEPTH + 3, CTX)]
        NORM_AT = {name: n for n, (name, _, _) in enumerate(NORMS)}
        UPDATED = {name: updates for name, updates, _ in NORMS}
        START = {name: t0 for name, _, t0 in NORMS}
        OUT_BANK = (2, 3, 6, 7, 0, 1, 2, 3)
        PAIR_BANKS = ((0, 1), (2, 3), (6, 7))
        ROW_BANK, TURN_BANK, NORM_BANK = 4, 5, 4

        def earlier(name, counts):
            return sum(1 for n, (other, _, t0) in enumerate(NORMS) if n < NORM_AT[name] and counts(other, t0))

        def modulated(name, t0):
            return not name.startswith("final")

        def h_before(name):
            return KC * earlier(name, modulated)

        def wide(name, t0):
            return modulated(name, t0) and t0 == 0

        def before_updates(update):
            return KC * (UPDATES.index(update) if update in UPDATES else 3 * DEPTH + 1 + BANKED.index(update) - 3 * DEPTH)

        IN_BANK = (0, 1, 2, 3) + (6, 7, 2, 3) * 3
        ROPE_BANK = (0, 1, 4, 5, 0)

        def full_wait(engine, at, rounds=0):
            engine.wait_ge(unit_full[at % RING], rounds * 16 + 16 * (at // RING + 1))

        FFNS = list(SWIGLU)

        class Chain:

            def __init__(self, engine, name):
                self.engine, self.sem, self.n = engine, sem(name), 0

            def mark(self, instruction):
                self.n += 1
                instruction.then_inc(self.sem, 1)
                return self.n

            def wait(self, n):
                self.engine.wait_ge(self.sem, n)

            def link(self, instruction):
                self.wait(self.mark(instruction))

        latent = arena[:, 0:4, :]
        conv_in = arena[:, 4:12, :]
        q_heads, k_heads = arena[:, 12:21, :], arena[:, 21:29, :]
        values = arena[:, 29:33, :]
        probs, probs_turned = arena[:, 33:36, :], arena[:, 36:38, :]
        latent_rms, latent_rinv = arena[:, 38:40, :], arena[:, 40:42, :]
        rope_tmp = arena[:, 42, :]
        SCORE_BANKS = (2, 4, 5)

        q_raw = arena[:, 0:2, :].rearrange("p a (b t) -> p (a b) t", b=2)
        k_raw = arena[:, 2:6, :]
        q_ml = arena[:, 6:8, :].rearrange("p a (b t) -> p (a b) t", b=2)
        k_ml, v_ml, v_hg = arena[:, 8:12, :], arena[:, 12:16, :], arena[:, 16:20, :]
        o_gate = arena[:, 20:22, :].rearrange("p a (b t) -> p (a b) t", b=2)
        g_gate = arena[:, 22:24, :].rearrange("p a (b t) -> p (a b) t", b=2)
        q_hg = arena[:, 24:26, :].rearrange("p a (b t) -> p (a b) t", b=2)
        k_hg = [arena[:, 26:30, :], arena[:, 30:34, :]]
        decay = [arena[:, 34:38, :], arena[:, 38:42, :]]
        hg_scores = arena[:, 0:4, :].rearrange("p h (c t) -> p h c t", c=2)
        hg_ctx_scores = arena[:, 4:6, :]
        hg_out = q_hg
        hg_factor = [[h[:, 4 * e + 2 * part:4 * e + 2 * part + 2, :].rearrange("p a (b t) -> p (a b) t", b=2)
                      for part in range(2)] for e in range(2)]
        hg_factors = [h[:, 4 * e:4 * e + 4, :] for e in range(2)]
        ml_decay = [arena[:, 26 + 2 * e:28 + 2 * e, :].rearrange("p a (b t) -> p (a b) t", b=2) for e in range(2)]
        ml_weight = [arena[:, 30 + 2 * e:32 + 2 * e, :].rearrange("p a (b t) -> p (a b) t", b=2) for e in range(2)]
        ml_num = arena[:, 34:38, :]
        ml_out = arena[:, 38:40, :].rearrange("p a (b t) -> p (a b) t", b=2)
        ml_floor, ml_den = arena[0:MH, 40, :], arena[0:MH, 41, :]
        out_squares = arena[:, 26:30, :].rearrange("p a (b t) -> p (a b) t", b=2)
        out_rms, out_rinv = arena[0:2 * MH, 30, 0:LAT], arena[0:2 * MH, 31, 0:LAT]
        u_rows = [arena[0:MH, 42, :], squares[0:MH, 3, :]]
        m_rows = [rms[0:MH, CTX:], squares[0:MH, 1, 0:LAT]]
        floor_rows = [squares[0:MH, 2, CTX:], squares[0:MH, 1, LAT:]]
        u_cols = small[:, 0:2 * 4 * MH]
        bounds = small[:, 40:56].rearrange("p (k d c) -> p k d c", k=2, d=2)
        HALVES_B = [(name, c) for name in PROJECTIONS for c in range(4)]
        LOG_STEPS = (16, 17, 18, 19)
        V_HALVES = [n for n, (name, _) in enumerate(HALVES_B) if name.endswith("_v")]
        WIDE = ("ml_k", "hg_zf", "hg_zb", "ml_v", "hg_v")
        HG_STAGES = ["ctx0", "ctx1"] + list(range(LEVELS + 1)) + ["diagonal"]
        N_TAPS = 2 * 8
        raw_b = [[arena[:, 2 * e + part, 0:LAT] for part in range(2)] for e in range(3)]
        acc_b = [[arena[:, 6 + 2 * e + part, 0:LAT] for part in range(2)] for e in range(3)]
        product_b = [arena[:, 12 + e, 0:LAT] for e in range(3)]

        def later(n):
            return not (isinstance(n, int) and n == 0)

        def spread(j, rows):
            return const("ident", j, 1, rows=rows).broadcast_to([rows, P])

        def lat_valid(direction, c):
            if direction == 0:
                return c * P, LAT
            return 0, (c + 1) * P

        def taps(rows, cols):
            for dy in (-1, 0, 1):
                for dx in (-1, 0, 1):
                    if (dy or dx) and abs(dy) < rows:
                        r = slice(max(0, -dy), rows - max(0, dy)), slice(max(0, dy), rows - max(0, -dy))
                        c = slice(max(0, -dx), cols - max(0, dx)), slice(max(0, dx), cols - max(0, -dx))
                        yield 3 * (dy + 1) + dx + 1, (r[0], c[0]), (r[1], c[1])

        def attention_units(t0):
            return [(hd, tc, CTX if tc * P < CTX else T) for hd in range(HEADS) for tc in range(t0 // P, T // P)]

        def modulation(name, kc, which):
            if name in ("norm_a", "norm_b"):
                mod, j = mods[2], ("norm_a", "norm_b").index(name)
            else:
                mod, j = mods[int(name[5])], int(name[4]) - 1
            shift = KC * 3 * j + kc
            return scales[:, kc, which:which + 1], mod[:, shift, which:which + 1]

        n_rounds = N_UNITS // RING if until is None else -(-AT["gate", 0] // RING)
        block = stack.enter_context(nc.Block())

        @block.sync
        def _(sp):
            sp.dma_start(params[:, :], params_in).then_inc(loaded, 16)
            sp.dma_start(consts[:, :], consts_in).then_inc(loaded, 16)
            sp.dma_start(x[:, :, :], x_in).then_inc(loaded, 16)
            for s in range(RING):
                sp.dma_start(raw[s][:, :, :], stream[s]).then_inc(unit_full[s], 16)
            with sp.Fori(1, n_rounds) as i:
                for s in range(RING):
                    sp.wait_ge(unit_begun, i * RING + (s + 2 - RING))
                    sp.dma_start(raw[s][:, :, :], stream[i * RING + s]).then_inc(unit_full[s], 16)
            for s in range(RING):
                sp.wait_ge(unit_full[s], 16 * n_rounds)
            if until is None:
                for part in range(2):
                    sp.wait_ge(x_updated, KC * (UPDATED["final2"]) + 4 * (part + 1))
                    sp.dma_start(out[:, 4 * part:4 * part + 4, :], x[:, 4 * part:4 * part + 4, CTX:])\
                        .then_inc(sem("stored"), 16)
                sp.wait_ge(sem("stored"), 32)
            else:
                sp.wait_ge(x_updated, KC * (3 * DEPTH + 1))
                sp.dma_start(out, x[:, :, CTX:]).then_inc(sem("stored"), 16)
                sp.wait_ge(sem("stored"), 16)

        @block.tensor
        def _(pe):
            class At:
                half, side = 0, 0

            def side_sum(at, rounds=0):
                full_wait(pe, at, rounds)
                which = 0 if ORDER[at][0] != "mod" else 1
                for kc in range(KC):
                    g = 32 * (kc % 4)
                    last = nc.tensor.matmul(bank[ROW_BANK][g:g + 32, 0:UNIT], cond[:, which, kc, :], raw[at % RING][:, kc, :],
                                            start=kc < 4, stop=kc >= 4)
                    if kc == 0:
                        last.then_inc(unit_begun, 1)
                last.then_inc(sem("side_sum"), 1)

            def side_turn(side):
                pe.wait_ge(sem("side_row"), side + 1)
                if later(side):
                    pe.wait_ge(sem("side_done"), side)
                for q in range(2):
                    last = nc.tensor.matmul(bank[TURN_BANK][:, 2 * q:2 * q + 2], side_row[:, q * P:(q + 1) * P],
                                            const("sum_rows"), start=True, stop=True)
                last.then_inc(sem("side_turned"), 1)

            def split_product(acc, half, operand, chunks, first_chunk=0, begins_unit=False, start=True, stop=True, await_chunk=None):
                pe.wait_ge(half_ready, half + 1)
                buffer = At.half % 2
                hi, lo = operand
                for kc in range(chunks):
                    if await_chunk:
                        await_chunk(kc)
                    for n, (w, v) in enumerate(((w_hi, hi), (w_hi, lo), (w_lo, hi))):
                        last = nc.tensor.matmul(acc, w[:, buffer, kc, :], v(first_chunk + kc), start=start and kc == n == 0,
                                                stop=stop and kc == chunks - 1 and n == 2)
                        if kc == 0 and n == 0:
                            last.then_inc(half_begun, 1)
                        if kc == 0 and n == 1 and begins_unit:
                            last.then_inc(unit_begun, 1)
                At.half += 1
                return last

            def normed(t0):
                return (lambda kc: h_hi[:, kc, t0:]), (lambda kc: h_lo[:, kc, t0:])

            def norm_sum(name):
                n, t0 = NORM_AT[name], START[name]
                for kc in range(KC):
                    pe.wait_ge(sem("square_ready"), KC * n + kc + 1)
                    nc.tensor.matmul(bank[NORM_BANK][:, 0:T - t0], ones, squares[:, kc % 4, t0:], start=kc == 0,
                                     stop=kc == KC - 1).then_inc(sem("square_used"), 1)

            def swiglu(name, norm):
                f, t0 = FFNS.index(name), START[norm]
                with_up, with_down = SWIGLU[name]

                def pair(p, j, at, half, side=None, rounds=0, await_chunk=None):
                    pe.wait_ge(sem("pair_moved"), p + (UP * f + 1))
                    full_wait(pe, at, rounds)
                    for gv in range(2):
                        last = split_product(bank[PAIR_BANKS[j][gv]][:, 0:T - t0], half + gv, normed(t0), KC,
                                             begins_unit=gv == 0, await_chunk=await_chunk if gv == 0 else None)
                        if gv == 0 and side is not None:
                            side_turn(side)
                    last.then_inc(sem("pair_ready"), 1)

                def await_chunk(kc):
                    pe.wait_ge(sem("h_ready"), h_before(norm) + kc + 1)

                pair(0, 0, AT[f"up{name}", 0], At.half, await_chunk=await_chunk)
                half, side = At.half, At.side
                per_round = 2 if with_up else 1
                with pe.Fori(0, (UP - 1) // RING) as i:
                    for j in range(RING):
                        at = AT[f"up{name}", 1 + j]
                        if with_up:
                            side_sum(at - 1, i * per_round)
                        pair(i * RING + (1 + j), (1 + j) % RING, at, i * 2 * RING + (half + 2 * j),
                             i * RING + (side + j) if with_up else None, i * per_round)
                At.half = half + 2 * (UP - 1)
                At.side = side + with_up
                pe.wait_ge(sem("pair_moved"), UP * f + UP + 1)
                down(name, f"ffn{name}", UP * f, with_down, t0)

            def down(name, update, hidden_before, sides, t0):
                before = KC * BANKED.index(update)
                operand = (lambda kc: hidden_hi[:, kc, t0:]), (lambda kc: hidden_lo[:, kc, t0:])
                for j in range(4 * len(GROUPS)):
                    at = AT[f"down{name}", j]
                    g, pair_of_chunks = j % len(GROUPS), j // len(GROUPS)
                    if j < sides:
                        side_sum(at - 1)
                    full_wait(pe, at)
                    pe.wait_ge(sem("hidden_ready"), hidden_before + min(KC * (g + 1), FC) if j < len(GROUPS) else hidden_before + FC)
                    if j == 3 * len(GROUPS):
                        pe.wait_ge(x_updated, before_updates(update) + 2)
                    for sub in range(2):
                        c = 2 * pair_of_chunks + sub
                        last = split_product(bank[OUT_BANK[c]][:, 0:T - t0], At.half, operand, GROUPS[g], KC * g, sub == 0,
                                             g == 0, g == len(GROUPS) - 1)
                        if g == len(GROUPS) - 1:
                            last.then_inc(sem("acc_ready"), 1)
                        if sub == 0 and j < sides:
                            side_turn(At.side)
                            At.side += 1

            def out_product(name, update, t0):
                for j in range(4):
                    full_wait(pe, AT[name, j])
                    if j == 3:
                        pe.wait_ge(x_updated, before_updates(update) + 2)
                    for sub in range(2):
                        split_product(bank[OUT_BANK[2 * j + sub]][:, 0:T - t0], At.half, normed(t0), KC, 0, sub == 0)\
                            .then_inc(sem("acc_ready"), 1)

            def mla_and_conv(i):
                tag, t0 = f"mix{i}", CTX if i == DEPTH - 1 else 0

                def await_chunk(kc):
                    pe.wait_ge(sem("h_ready"), h_before(f"norm2{i}") + kc + 1)

                for n in range(16):
                    if n % 2 == 0:
                        full_wait(pe, AT[f"in{i}", n // 2])
                    if n == 6:
                        pe.wait_ge(sem(f"latent_moved{tag}"), 4)
                    if n >= 8:
                        pe.wait_ge(sem(f"conv_moved{tag}"), n - 7)
                    start = 0 if n in (2, 3) else t0
                    split_product(bank[IN_BANK[n]][:, 0:T - start], At.half, normed(start), KC, 0, n % 2 == 0,
                                  await_chunk=await_chunk if n == 0 else None)\
                        .then_inc(sem(f"latent_sum{tag}" if n < 4 else f"conv_sum{tag}"), 1)
                    if n == 7:
                        pe.wait_ge(sem(f"latent_square{tag}"), 3)
                        for c in range(2):
                            last = nc.tensor.matmul(bank[0][:, 0:T - t0], ones, squares[:, c, t0:], start=c == 0, stop=c == 1)
                        last.then_inc(sem(f"latent_norm_sum{tag}"), 1)
                        nc.tensor.matmul(bank[1][:, :], ones, squares[:, 2, :], start=True, stop=True)\
                            .then_inc(sem(f"latent_norm_sum{tag}"), 1)
                at_q, at_kv = AT[f"uq{i}", 0], AT[f"ukv{i}", 0]
                full_wait(pe, at_q)
                full_wait(pe, at_kv)
                flat = [raw[at % RING][:, :, :].rearrange("p a b -> p (a b)") for at in (at_q, at_kv)]
                w_q = flat[0][:, 0:2 * HEADS * QK].rearrange("p (k n) -> p k n", k=2)
                w_kv = flat[1][:, 0:HEADS * (NOPE + VD)].rearrange("p (h n) -> p h n", h=HEADS)
                pe.wait_ge(sem(f"latent_ready{tag}"), 3)
                for n in range(20):
                    acc = bank[IN_BANK[8 + n % 4]]
                    if n < 4:
                        pe.wait_ge(sem(f"conv_u{tag}"), n + 1)
                    elif n % 2 and n < 20:
                        pe.wait_ge(sem(f"key_moved{tag}"), (n - 4) // 2 + 1)
                    else:
                        pe.wait_ge(sem(f"query_moved{tag}"), (n - 4) // 2 + 1)
                    hd = n // 2
                    if n >= 16:
                        c = n - 16
                        for q in range(2):
                            last = nc.tensor.matmul(acc[:, q * LAT:(q + 1) * LAT], latent[:, 2, c * P:(c + 1) * P],
                                                    w_kv[:, 4 * q:4 * q + 4, NOPE:], start=True, stop=True, skip_group_check=True)
                            if c == q == 0:
                                last.then_inc(unit_begun, 1)
                    elif n % 2:
                        last = nc.tensor.matmul(acc[0:NOPE, :], w_kv[:, hd, 0:NOPE], latent[:, 2, :], start=True, stop=True)
                    else:
                        for c in range(2):
                            last = nc.tensor.matmul(acc[0:QK, 0:T - t0], w_q[:, c, hd * QK:(hd + 1) * QK],
                                                    latent[:, c, t0:], start=c == 0, stop=c == 1)
                            if n == c == 0:
                                last.then_inc(unit_begun, 1)
                    last.then_inc(sem(f"head_sum{tag}"), 1)
                for r in range(5):
                    if r == 4:
                        pe.wait_ge(sem(f"roped{tag}"), 1)
                    if r:
                        pe.wait_ge(sem(f"query_moved{tag}"), 2 * r)
                    src = q_heads[0:QK, 8:9, CTX:] if r == 0 else q_heads[0:QK, 2 * r - 2:2 * r, CTX:]
                    width = LAT if r == 0 else 2 * LAT
                    nc.tensor.matmul(bank[ROPE_BANK[r]][0:QK, 0:width], const("perm", 0, QK, rows=QK), src, start=True, stop=True)\
                        .then_inc(sem(f"exchanged{tag}"), 1)
                pe.wait_ge(sem(f"roped{tag}"), 5)
                pe.wait_ge(sem(f"key_rope{tag}"), 1)
                pe.wait_ge(sem(f"key_moved{tag}"), HEADS)
                pe.wait_ge(sem(f"query_moved{tag}"), HEADS + 4)
                units = attention_units(t0)
                for n in range(len(units) + 3):
                    if n < len(units):
                        hd, tc, keys = units[n]
                        if n >= 3:
                            pe.wait_ge(sem(f"exp{tag}"), n - 2)
                        nc.tensor.matmul(bank[SCORE_BANKS[n % 3]][:, 0:keys], q_heads[0:QK, hd, tc * P:(tc + 1) * P],
                                         k_heads[0:QK, hd, 0:keys], start=True, stop=True).then_inc(sem(f"score{tag}"), 1)
                    m = n - 2
                    if 0 <= m < len(units):
                        keys = units[m][2]
                        pe.wait_ge(sem(f"prob{tag}"), m + 1)
                        if m >= 2:
                            pe.wait_ge(sem(f"prob_turned_moved{tag}"), m - 1)
                        for c in range(keys // P):
                            last = nc.tensor.transpose(bank[6 + m % 2][:, c * P:(c + 1) * P],
                                                       probs[:, m % 3, c * P:(c + 1) * P], ident)
                        last.then_inc(sem(f"prob_turned{tag}"), 1)
                    m = n - 3
                    if 0 <= m < len(units):
                        hd, tc, keys = units[m]
                        pe.wait_ge(sem(f"prob_turned_moved{tag}"), m + 1)
                        if m >= 2:
                            pe.wait_ge(sem(f"attended{tag}"), m - 1)
                        for c in range(keys // P):
                            v0 = hd // 2 * P
                            last = nc.tensor.matmul(bank[m % 2][:, 0:P], values[:, c, v0:v0 + P],
                                                    probs_turned[:, m % 2, c * P:(c + 1) * P], start=c == 0,
                                                    stop=c == keys // P - 1)
                        last.then_inc(sem(f"attend_sum{tag}"), 1)
                pe.wait_ge(sem(f"attended{tag}"), len(units))
                pe.wait_ge(sem(f"conv_out{tag}"), 4)
                out_product(f"out{i}", tag, t0)

            def projections():
                def await_chunk(kc):
                    pe.wait_ge(sem("h_ready"), h_before("norm_a") + kc + 1)

                full_wait(pe, AT["gate", 0])
                split_product(bank[5][:, :], At.half, normed(0), KC, 0, True, await_chunk=await_chunk).then_inc(sem("gate_sum"), 1)

                def turn(n):
                    m = V_HALVES.index(n)
                    pe.wait_ge(sem("projected"), n + 1)
                    if m >= 1:
                        pe.wait_ge(sem("value_moved"), m)
                    for c in range(4):
                        last = nc.tensor.transpose(bank[4][:, c * P:(c + 1) * P], squares[:, m % 2, c * P:(c + 1) * P], ident)
                    last.then_inc(sem("value_turned"), 1)

                for n, (name, c) in enumerate(HALVES_B):
                    if n % 2 == 0:
                        full_wait(pe, AT["in", n // 2])
                    if n >= 4:
                        pe.wait_ge(sem("projected"), n - 3)
                    start = 0 if name in WIDE else CTX
                    split_product(bank[n % 4][:, 0:T - start], At.half, normed(start), KC, 0, n % 2 == 0)\
                        .then_inc(sem("projection_sum"), 1)
                    if n - 1 in V_HALVES:
                        turn(n - 1)

            def hgrn():
                for n, stage in enumerate(HG_STAGES):
                    pe.wait_ge(sem("hg_scaled"), n + 1)
                    q, k = hg_factor[n % 2]
                    if stage in ("ctx0", "ctx1"):
                        if n == 0:
                            pe.wait_ge(sem("projected"), len(HALVES_B))
                        for hd in range(MH):
                            for c in range(2):
                                last = nc.tensor.matmul(bank[hd][:, c * LAT:(c + 1) * LAT], k[:, hd, c * P:(c + 1) * P], q[:, hd, :],
                                                        start=n == 0 and c == 0, stop=n == 1, skip_group_check=True)
                    else:
                        if n >= 4:
                            pe.wait_ge(sem("hg_placed"), n - 3)
                        for c in range(2):
                            t = 1 - c if stage == LEVELS else c
                            source = q_hg if stage == "diagonal" else q
                            for hd in range(MH):
                                last = nc.tensor.matmul(bank[4 + 2 * (n % 2) + c][:, hd * P:(hd + 1) * P], k[:, hd, c * P:(c + 1) * P],
                                                        source[:, hd, t * P:(t + 1) * P], start=True, stop=True)
                    last.then_inc(sem("hg_product"), 1)
                pe.wait_ge(sem("hg_placed"), len(HG_STAGES) - 2)
                pe.wait_ge(sem("value_moved"), len(V_HALVES))
                for hd in range(MH):
                    pe.wait_ge(sem("hg_ctx_moved"), hd + 1)
                    for c in range(4):
                        w = hg_ctx_scores[:, hd % 2, c * LAT:(c + 1) * LAT] if c < 2 else hg_scores[:, hd, c - 2, :]
                        last = nc.tensor.matmul(bank[4 + hd][:, 0:LAT], v_hg[:, c, hd * P:(hd + 1) * P], w, start=c == 0, stop=c == 3)
                    last.then_inc(sem("hg_out_sum"), 1)

            def mlstm():
                pe.wait_ge(sem("gate_rows"), 1)
                pe.wait_ge(sem("hg_ctx_moved"), MH)
                for d in range(2):
                    for c in range(4):
                        at = MH * (4 * d + c)
                        last = nc.tensor.matmul(bank[2][:, at:at + MH], u_rows[d][:, c * P:(c + 1) * P], const("ident", 0, MH, rows=MH),
                                                start=True, stop=True)
                last.then_inc(sem("u_turned"), 1)
                pe.wait_ge(sem("u_cols"), 1)
                pe.wait_ge(sem("conv_silu"), 2)
                pe.wait_ge(sem("hg_out_moved"), MH)

                def maxima(n):
                    hd, d = n // 2, n % 2
                    if n >= 2:
                        pe.wait_ge(sem("ml_decayed"), n - 1)
                    nc.tensor.matmul(bank[2 + d][:, 0:LAT], spread(hd, MH), m_rows[d], start=True, stop=True)\
                        .then_inc(sem("ml_max"), 1)

                def scores(hd):
                    if hd:
                        pe.wait_ge(sem("ml_weighted"), 2 * hd)
                    for c in range(4):
                        last = nc.tensor.matmul(bank[c // 2][:, c % 2 * LAT:(c % 2 + 1) * LAT], k_ml[:, hd, c * P:(c + 1) * P],
                                                q_ml[:, hd, :], start=c % 2 == 0, stop=c % 2 == 1, skip_group_check=True)
                    last.then_inc(sem("ml_score"), 1)

                maxima(0)
                maxima(1)
                scores(0)
                for n in range(2 * MH):
                    hd, d = n // 2, n % 2
                    pe.wait_ge(sem("ml_weighted"), n + 1)
                    if n >= 2:
                        pe.wait_ge(sem("ml_num_moved"), n - 1)
                    for target in range(2):
                        for c in range(4):
                            a, b = (0, LAT) if c < 2 else lat_valid(d, c - 2)
                            w = ml_weight[d][:, c, a:b]
                            if target == 0:
                                last = nc.tensor.matmul(bank[4 + d][:, a:b], v_ml[:, c, hd * P:(hd + 1) * P], w,
                                                        start=c == 0, stop=c == 3, skip_group_check=True)
                            else:
                                last = nc.tensor.matmul(bank[6 + d][0:8, a:b], const("col_of", 8 * hd, 8), w,
                                                        start=c == hd == 0, stop=c == hd == 3, skip_group_check=True)
                    last.then_inc(sem("ml_num_sum"), 1)
                    if n + 2 < 2 * MH:
                        maxima(n + 2)
                    if d == 1 and hd + 1 < MH:
                        scores(hd + 1)
                pe.wait_ge(sem("ml_den_ready"), 1)
                for hd in range(MH):
                    nc.tensor.matmul(bank[hd][:, :], spread(hd, MH), ml_den, start=True, stop=True)\
                        .then_inc(sem("ml_den_spread"), 1)

            def head_norms():
                for j in range(8):
                    pe.wait_ge(sem("out_square"), j + 1)
                    last = nc.tensor.matmul(bank[4][0:8, 0:LAT], const("col_of", 8 * j, 8), out_squares[:, j, :],
                                            start=j == 0, stop=j == 7)
                last.then_inc(sem("out_norm_sum"), 1)
                pe.wait_ge(sem("out_rinv"), 1)
                for j in range(8):
                    nc.tensor.matmul(bank[j // 2][:, j % 2 * LAT:(j % 2 + 1) * LAT], spread(j, 8), out_rinv,
                                     start=True, stop=True, skip_group_check=True)\
                        .then_inc(sem("out_rinv_spread"), 1)

            def conv_ffn():
                pe.wait_ge(sem("h_ready"), h_before("norm_b") + KC)

                def pair(p, j, at, rounds=0):
                    pe.wait_ge(sem("up_moved"), p + 1)
                    full_wait(pe, at, rounds)
                    for gv in range(2):
                        for kc in range(KC):
                            last = nc.tensor.matmul(bank[PAIR_BANKS[j][gv]][:, 0:LAT], raw[at % RING][:, kc, gv * P:(gv + 1) * P],
                                                    h[:, kc, CTX:], start=kc == 0, stop=kc == KC - 1)
                            if gv == kc == 0:
                                last.then_inc(unit_begun, 1)
                    last.then_inc(sem("up_sum"), 1)

                pe.sem_inc(sem("up_moved"), 3)
                pair(0, 0, AT["up", 0])
                with pe.Fori(0, (UP - 1) // RING) as i:
                    for j in range(RING):
                        pair(i * RING + (1 + j), (1 + j) % RING, AT["up", 1 + j], i)
                pe.wait_ge(sem("up_moved"), UP + 3)
                down("", "ffn_b", UP * len(FFNS), 0, CTX)

            pe.wait_ge(loaded, 48)
            pe.sem_inc(sem("pair_moved"), 3)
            pe.wait_ge(sem("cond_ready"), 1)
            for j in range(FIRST_SIDES):
                side_sum(j)
                side_turn(j)
            At.side = FIRST_SIDES
            for i in range(DEPTH):
                norm_sum(f"norm1{i}")
                swiglu(f"1{i}", f"norm1{i}")
                norm_sum(f"norm2{i}")
                mla_and_conv(i)
                norm_sum(f"norm3{i}")
                swiglu(f"2{i}", f"norm3{i}")
            norm_sum("final1")
            if until is None:
                norm_sum("norm_a")
                projections()
                hgrn()
                mlstm()
                head_norms()
                pe.wait_ge(sem("mixed_b"), 8)
                out_product("out", "mix_b", CTX)
                norm_sum("norm_b")
                conv_ffn()
                norm_sum("final2")

        @block.scalar
        def _(act):
            own = Chain(act, "scalar_own")

            class At:
                half, side = 0, 0

            def convert(at, sub, half=None, rounds=0, chunks=KC):
                half = At.half if half is None else half
                buffer = At.half % 2
                full_wait(act, at, rounds)
                if later(half):
                    act.wait_ge(half_begun, half)
                nc.scalar.activation(w_hi[:, buffer, 0:chunks, :], raw[at % RING][:, 0:chunks, sub * P:(sub + 1) * P], ACT.Copy)\
                    .then_inc(half_high, 1)
                At.half += 1

            def side(number):
                act.wait_ge(sem("side_sum"), number + 1)
                if later(number):
                    act.wait_ge(sem("side_turned"), number)
                nc.scalar.activation(side_row[:, :], bank[ROW_BANK][:, 0:UNIT], ACT.Copy).then_inc(sem("side_row"), 1)

            def norm(name):
                n, t0, u = NORM_AT[name], START[name], UPDATED[name]
                for kc in range(KC):
                    if u > 0:
                        act.wait_ge(x_updated, KC * (u - 1) + kc + 1)
                    if KC * n + kc >= 4:
                        act.wait_ge(sem("square_used"), KC * n + kc - 3)
                    nc.scalar.activation(squares[:, kc % 4, t0:], x[:, kc, t0:], ACT.Square).then_inc(sem("square_ready"), 1)
                act.wait_ge(sem("square_used"), KC * (n + 1))
                nc.scalar.activation(rms[:, t0:], bank[NORM_BANK][:, 0:T - t0], ACT.Sqrt, bias=const("eps"), scale=1.0 / D)\
                    .then_inc(sem("rms_ready"), 1)
                if not modulated(name, t0) or name == "norm_b":
                    return
                for kc in range(KC + 1):
                    if t0 == 0 and kc < KC:
                        act.wait_ge(sem("h_scaled"), h_before(name) + kc + 1)
                        s, b = modulation(name, kc, 1)
                        own.mark(nc.scalar.activation(squares[:, kc % 4, 0:CTX], squares[:, kc % 4, 0:CTX], ACT.Identity, bias=b, scale=s))
                    if kc > 0:
                        act.wait_ge(sem("h_lat_ready"), h_before(name) + kc)
                        own.wait(own.n - (1 if kc < KC and t0 == 0 else 0))
                        nc.scalar.activation(h_hi[:, kc - 1, t0:], squares[:, (kc - 1) % 4, t0:], ACT.Copy).then_inc(sem("h_high"), 1)

            def swiglu(name, norm_name):
                f, t0 = FFNS.index(name), START[norm_name]
                with_up, with_down = SWIGLU[name]

                def silu(p, j):
                    act.wait_ge(sem("pair_ready"), p + (UP * f + 1))
                    nc.scalar.activation(squares[:, j, t0:], bank[PAIR_BANKS[j][0]][:, 0:T - t0], ACT.Silu).then_inc(sem("silu_ready"), 1)

                def high(p, j):
                    act.wait_ge(sem("pair_moved"), p + (UP * f + 4))
                    nc.scalar.activation(hidden_hi[:, p, t0:], squares[:, j, t0:], ACT.Copy).then_inc(sem("hidden_high"), 1)

                first = AT[f"up{name}", 0]
                per_unit = 2 if with_up else 1
                convert(first, 1)
                convert(first + per_unit, 0)
                half = At.half
                with act.Fori(0, (UP - 1) // RING) as i:
                    for j in range(RING):
                        at = first + per_unit * (1 + j)
                        if with_up:
                            side(i * RING + (At.side + j))
                        convert(at, 1, i * 2 * RING + (half + 2 * j), i * per_unit)
                        silu(i * RING + j, j)
                        convert(at + per_unit, 0, i * 2 * RING + (half + 2 * j + 1), i * per_unit)
                        high(i * RING + j, j)
                At.half = half + 2 * (UP - 1)
                At.side += with_up
                last = (UP - 1, (UP - 1) % RING)
                down(name, with_down, lambda: silu(*last), lambda: high(*last))

            def down(name, sides, *ahead, then=None):
                for n in range(2 * 4 * len(GROUPS)):
                    j, sub = n // 2, n % 2
                    if sub == 0 and j < sides:
                        side(At.side)
                        At.side += 1
                    if n + 1 < 2 * 4 * len(GROUPS):
                        at = AT[f"down{name}", (n + 1) // 2]
                        convert(at, (n + 1) % 2, chunks=GROUPS[(n + 1) // 2 % len(GROUPS)])
                    elif then is not None:
                        convert(then, 0)
                    if n < len(ahead):
                        ahead[n]()

            def out_product(name, then=None):
                for n in range(7):
                    convert(AT[name, (n + 1) // 2], (n + 1) % 2)
                if then is not None:
                    convert(then, 0)

            def mla_and_conv(i):
                tag, t0 = f"mix{i}", CTX if i == DEPTH - 1 else 0
                for n in range(16):
                    if n < 15:
                        convert(AT[f"in{i}", (n + 1) // 2], (n + 1) % 2)
                    c = n - 1
                    if 0 <= c < 3:
                        first = t0 if c < 2 else 0
                        act.wait_ge(sem(f"latent_moved{tag}"), c + 1)
                        nc.scalar.activation(squares[:, c, first:], latent[:, c, first:], ACT.Square)\
                            .then_inc(sem(f"latent_square{tag}"), 1)
                    if 4 <= c < 12:
                        act.wait_ge(sem(f"conv_sum{tag}"), c - 3)
                        nc.scalar.activation(conv_in[:, c - 4, t0:], bank[IN_BANK[c]][:, 0:T - t0], ACT.Copy)\
                            .then_inc(sem(f"conv_moved{tag}"), 1)
                    if n == 9:
                        for j, width in ((0, QR), (1, KVR)):
                            first = t0 if j == 0 else 0
                            act.wait_ge(sem(f"latent_norm_sum{tag}"), j + 1)
                            nc.scalar.activation(latent_rms[:, j, first:], bank[j][:, 0:T - first], ACT.Sqrt, bias=const("eps"),
                                                 scale=1.0 / width).then_inc(sem(f"latent_rms{tag}"), 1)
                for n in list(range(0, 16, 2)) + list(range(16, 20)):
                    act.wait_ge(sem(f"head_sum{tag}"), n + 1)
                    acc = bank[IN_BANK[8 + n % 4]]
                    if n < 16:
                        nc.scalar.activation(q_heads[0:QK, n // 2, t0:], acc[0:QK, 0:T - t0], ACT.Copy)\
                            .then_inc(sem(f"query_moved{tag}"), 1)
                    else:
                        nc.scalar.activation(values[:, n - 16, :], acc[:, :], ACT.Copy).then_inc(sem(f"query_moved{tag}"), 1)
                convert(AT[f"out{i}", 0], 0)
                for c in range(4):
                    act.wait_ge(sem(f"conv_gated{tag}"), c + 1)
                    nc.scalar.activation(h_hi[:, 4 + c, t0:], squares[:, c, t0:], ACT.Copy).then_inc(sem(f"conv_high{tag}"), 1)
                units = attention_units(t0)
                for n in range(len(units) + 2):
                    if n < len(units):
                        keys = units[n][2]
                        act.wait_ge(sem(f"negmax{tag}"), n + 1)
                        if n >= 3:
                            act.wait_ge(sem(f"prob_turned{tag}"), n - 2)
                        nc.scalar.activation(probs[:, n % 3, 0:keys], bank[SCORE_BANKS[n % 3]][:, 0:keys], ACT.Exp,
                                             bias=small[:, n % 4:n % 4 + 1], scale=SCALE,
                                             accum_out=small[:, 8 + n % 4:9 + n % 4]).then_inc(sem(f"exp{tag}"), 1)
                    m = n - 2
                    if m >= 0:
                        keys = units[m][2]
                        act.wait_ge(sem(f"prob_turned{tag}"), m + 1)
                        if m >= 2:
                            act.wait_ge(sem(f"attend_sum{tag}"), m - 1)
                        nc.scalar.activation(probs_turned[:, m % 2, 0:keys], bank[6 + m % 2][:, 0:keys], ACT.Copy)\
                            .then_inc(sem(f"prob_turned_moved{tag}"), 1)
                out_product(f"out{i}", AT[f"up2{i}", 0])

            def gate_rows():
                act.wait_ge(sem("gate_abs"), 1)
                own.link(nc.scalar.activation(squares[:, 1, :], squares[:, 1, :], ACT.Exp, scale=-1.0))
                nc.scalar.activation(squares[:, 1, :], squares[:, 1, :], ACT.Ln, bias=const("ones", 0, 1)).then_inc(sem("gate_log"), 1)

            def move(n):
                name, c = HALVES_B[n]
                act.wait_ge(sem("projection_sum"), n + 1)
                acc = bank[n % 4]
                if name == "ml_q":
                    last = nc.scalar.activation(q_raw[:, c, :], acc[:, 0:LAT], ACT.Copy)
                elif name == "ml_k":
                    last = nc.scalar.activation(k_raw[:, c, :], acc[:, :], ACT.Copy)
                elif name in ("hg_zf", "hg_zb"):
                    d = int(name == "hg_zb")
                    own.mark(nc.scalar.activation(decay[d][:, c, :], acc[:, :], ACT.Sigmoid))
                    last = nc.scalar.activation(k_hg[d][:, c, :], acc[:, :], ACT.Sigmoid, scale=-1.0)
                elif name == "hg_q":
                    last = nc.scalar.activation(q_hg[:, c, :], acc[:, 0:LAT], ACT.Silu)
                elif name.endswith("_v"):
                    m = V_HALVES.index(n)
                    if m >= 2:
                        act.wait_ge(sem("value_turned"), m - 1)
                    last = nc.scalar.activation(squares[:, m % 2, :], acc[:, :], ACT.Copy)
                elif name == "ml_o":
                    last = nc.scalar.activation(o_gate[:, c, :], acc[:, 0:LAT], ACT.Sigmoid)
                else:
                    last = nc.scalar.activation(g_gate[:, c, :], acc[:, 0:LAT], ACT.Silu)
                last.then_inc(sem("projected"), 1)

            def projections():
                act.wait_ge(sem("bound_logits"), 1)
                for k in range(2):
                    own.link(nc.scalar.activation(bounds[:, k, :, :], small[:, 56:64].rearrange("p (d c) -> p d c", d=2), ACT.Sigmoid,
                                                  scale=-1.0 if k else 1.0))
                nc.scalar.activation(small[:, 33:34], bounds[:, 0, 0, 0:1], ACT.Copy).then_inc(sem("bounds"), 1)
                convert(AT["in", 0], 0)
                for n in range(len(HALVES_B) + 2):
                    if n + 1 < len(HALVES_B):
                        convert(AT["in", (n + 1) // 2], (n + 1) % 2)
                    if 1 <= n <= len(HALVES_B):
                        move(n - 1)
                    if n - 2 in V_HALVES:
                        m = V_HALVES.index(n - 2)
                        act.wait_ge(sem("value_turned"), m + 1)
                        target, scale = (v_ml, 1.0) if m < 4 else (v_hg, MSCALE)
                        nc.scalar.activation(target[:, :, m % 4 * P:(m % 4 + 1) * P], bank[4][:, :].rearrange("p (c f) -> p c f", c=4),
                                             ACT.Copy, scale=scale).then_inc(sem("value_moved"), 1)
                    if n in LOG_STEPS:
                        own.wait(own.n)
                        d, pair = divmod(LOG_STEPS.index(n), 2)
                        for cc in (2 * pair, 2 * pair + 1):
                            nc.scalar.activation(decay[d][:, cc, :], decay[d][:, cc, :], ACT.Ln, bias=bounds[:, 0, d, cc:cc + 1],
                                                 scale=bounds[:, 1, d, cc:cc + 1]).then_inc(sem("log_decay"), 1)
                for k, (what, count) in enumerate(((q_ml, 4), (k_ml, 8))):
                    act.wait_ge(sem("qk_conv"), count)
                    nc.scalar.activation(what, what, ACT.Silu).then_inc(sem("conv_silu"), 1)

            def hgrn():
                for n, stage in enumerate(HG_STAGES):
                    q, k = hg_factor[n % 2]
                    if stage in ("ctx0", "ctx1"):
                        d = n
                        act.wait_ge(sem("projected"), len(HALVES_B))
                        act.wait_ge(sem("decay_summed"), 16)
                        own.mark(nc.scalar.activation(q, decay[d][:, :, CTX:], ACT.Exp))
                        for hd in range(MH):
                            total = decay[d][:, hd, CTX - 1:CTX] if d == 0 else decay[d][:, hd, 0:1]
                            last = nc.scalar.activation(k[:, hd, :], decay[d][:, hd, 0:CTX], ACT.Exp, bias=total, scale=-1.0)
                            own.mark(last) if hd < MH - 1 else None
                        own.wait(own.n)
                        last.then_inc(sem("hg_exp"), 1)
                    elif stage != "diagonal":
                        act.wait_ge(sem("hg_differences"), n - 1)
                        nc.scalar.activation(hg_factors[n % 2], hg_factors[n % 2], ACT.Exp).then_inc(sem("hg_exp"), 1)
                for hd in range(MH):
                    act.wait_ge(sem("hg_product"), 2)
                    if hd >= 2:
                        act.wait_ge(sem("hg_out_sum"), hd - 1)
                    nc.scalar.activation(hg_ctx_scores[:, hd % 2, :], bank[hd][:, :], ACT.Copy).then_inc(sem("hg_ctx_moved"), 1)
                for hd in range(MH):
                    act.wait_ge(sem("hg_out_sum"), hd + 1)
                    nc.scalar.activation(hg_out[:, hd, :], bank[4 + hd][:, 0:LAT], ACT.Copy).then_inc(sem("hg_out_moved"), 1)

            def mlstm():
                for n in range(2 * MH):
                    hd, d = n // 2, n % 2
                    act.wait_ge(sem("ml_masked"), n + 1)
                    open_chunk = (2, P, LAT) if d == 0 else (3, 0, P)
                    for c, a, b in ((0, 0, LAT), (1, 0, LAT), open_chunk):
                        u = u_cols[:, MH * (4 * d + c) + hd:MH * (4 * d + c) + hd + 1]
                        nc.scalar.activation(ml_decay[d][:, c, a:b], bank[2 + d][:, a:b], ACT.Exp, bias=u, scale=-1.0)\
                            .then_inc(sem("ml_open"), 1)
                    for c in range(2):
                        block_ = ml_decay[d][:, 2 + c, c * P:(c + 1) * P]
                        last = nc.scalar.activation(block_, block_, ACT.Exp)
                        if c == 0:
                            own.mark(last)
                    own.wait(own.n)
                    last.then_inc(sem("ml_decayed"), 1)
                    if n >= 1:
                        num_out(n - 1)
                num_out(2 * MH - 1)
                for d in range(2):
                    nc.scalar.activation(ml_floor[:, d * LAT:(d + 1) * LAT], floor_rows[d], ACT.Exp).then_inc(sem("ml_floor"), 1)

            def num_out(n):
                act.wait_ge(sem("ml_num_sum"), n + 1)
                nc.scalar.activation(ml_num[:, n // 2, n % 2 * LAT:(n % 2 + 1) * LAT], bank[4 + n % 2][:, 0:LAT], ACT.Copy)\
                    .then_inc(sem("ml_num_moved"), 1)

            def head_norms():
                convert(AT["out", 0], 0)
                for j in range(8):
                    if j < MH:
                        act.wait_ge(sem("ml_out"), j + 1)
                    source = ml_out[:, j, :] if j < MH else hg_out[:, j - MH, :]
                    nc.scalar.activation(out_squares[:, j, :], source, ACT.Square).then_inc(sem("out_square"), 1)
                act.wait_ge(sem("out_norm_sum"), 1)
                nc.scalar.activation(out_rms, bank[4][0:8, 0:LAT], ACT.Sqrt, bias=const("eps", rows=8), scale=1.0 / P)\
                    .then_inc(sem("out_rms"), 1)
                for j in range(8):
                    source = ml_out[:, j, :] if j < MH else hg_out[:, j - MH, :]
                    act.wait_ge(sem("out_gated"), j + 1)
                    nc.scalar.activation(h_hi[:, j, CTX:], source, ACT.Copy).then_inc(sem("out_high"), 1)
                out_product("out")

            def conv_ffn():
                def move(p, j, first=False):
                    act.wait_ge(sem("up_sum"), p + 1)
                    if not first:
                        act.wait_ge(sem("product_b"), p + 1)
                    for part in range(2):
                        source = bank[PAIR_BANKS[j][part]][:, 0:LAT]
                        own_copy = nc.scalar.activation(raw_b[j][part], source, ACT.Copy)
                        own_copy.then_inc(sem("up_copied"), 1)
                        centre = params[:, bass.ds(p + (PARAMS["ffn_conv"][0] + 4 * 2 * FC + part * FC), 1)]
                        last = nc.scalar.activation(acc_b[j][part], source, ACT.Copy, scale=centre)
                        if part == 0:
                            last.then_inc(sem("up_copied"), 1)
                    last.then_inc(sem("up_moved"), 1)

                def gate(p, j):
                    act.wait_ge(sem("tap"), p * N_TAPS + N_TAPS)
                    nc.scalar.activation(acc_b[j][0], acc_b[j][0], ACT.Silu).then_inc(sem("gate_b"), 1)

                def high(p, j):
                    act.wait_ge(sem("product_b"), p + 4)
                    nc.scalar.activation(hidden_hi[:, p, CTX:], product_b[j], ACT.Copy).then_inc(sem("hidden_high"), 1)

                move(0, 0, True)
                move(1, 1, True)
                gate(0, 0)
                move(2, 2, True)
                gate(1, 1)
                with act.Fori(0, (UP - 4) // RING) as i:
                    for j in range(RING):
                        high(i * RING + j, j)
                        move(i * RING + (3 + j), j)
                        gate(i * RING + (2 + j), (2 + j) % RING)
                high(UP - 4, 0)
                move(UP - 1, 0)
                gate(UP - 2, 2)
                high(UP - 3, 1)
                gate(UP - 1, 0)
                high(UP - 2, 2)
                high(UP - 1, 0)
                convert(AT["down", 0], 0)
                down("", 0)

            act.wait_ge(loaded, 48)
            act.wait_ge(sem("cond_zero"), 1)
            own.mark(nc.scalar.activation(cond[:, 0, :, 0:2], param("c1").rearrange("p (k c) -> p k c", c=2), ACT.Silu))
            last = nc.scalar.activation(cond[:, 1, :, 0:2], param("c2").rearrange("p (k c) -> p k c", c=2), ACT.Silu)
            own.wait(own.n)
            last.then_inc(sem("cond_ready"), 1)
            for j in range(FIRST_SIDES):
                side(j)
            At.side = FIRST_SIDES
            for i in range(DEPTH):
                if i == 0:
                    convert(AT["up10", 0], 0)
                norm(f"norm1{i}")
                swiglu(f"1{i}", f"norm1{i}")
                convert(AT[f"in{i}", 0], 0)
                norm(f"norm2{i}")
                mla_and_conv(i)
                norm(f"norm3{i}")
                swiglu(f"2{i}", f"norm3{i}")
                if i + 1 < DEPTH:
                    convert(AT[f"up1{i + 1}", 0], 0)
            norm("final1")
            if until is None:
                convert(AT["gate", 0], 0)
                act.wait_ge(sem("ctx2_loaded"), 16)
                norm("norm_a")
                projections()
                gate_rows()
                hgrn()
                mlstm()
                head_norms()
                norm("norm_b")
                conv_ffn()
                norm("final2")

        @block.vector
        def _(dve):
            own = Chain(dve, "vector_own")

            class At:
                half, side = 0, 0

            def convert(at, sub, half=None, chunks=KC):
                half = At.half if half is None else half
                buffer = At.half % 2
                dve.wait_ge(half_high, half + 1)
                nc.vector.tensor_tensor(w_lo[:, buffer, 0:chunks, :], raw[at % RING][:, 0:chunks, sub * P:(sub + 1) * P],
                                        w_hi[:, buffer, 0:chunks, :].bitcast(F32), ALU.subtract).then_inc(half_ready, 1)
                At.half += 1

            def side(number, which, unit):
                dve.wait_ge(sem("side_turned"), number + 1)
                first = PARAMS[("b_ada0", "b_ada1", "b_mod")[which]][0]
                nc.vector.tensor_tensor(mods[which][:, bass.ds(unit * 2, 2), :], bank[TURN_BANK][:, 0:4].rearrange("p (n c) -> p n c", c=2),
                                        params[:, bass.ds(unit * 2 + first, 2)].unsqueeze(2).broadcast_to([P, 2, 2]), ALU.add)\
                    .then_inc(sem("side_done"), 1)

            def side_static(number):
                name, unit = SIDE_UNITS[number]
                side(number, list(SIDES).index(name), unit)

            def factors(which, j, weight):
                dve.wait_ge(sem("side_done"), At.side)
                shift = KC * 3 * j
                own.link(nc.vector.scalar_tensor_tensor(scales[:, :, :], mods[which][:, shift + KC:shift + 2 * KC, :], 1.0,
                                                        param(*weight).unsqueeze(2).broadcast_to([P, KC, 2]), ALU.add, ALU.mult))

            def gate_factors(which, j, factor):
                dve.wait_ge(sem("side_done"), At.side)
                first = KC * (3 * j + 2)
                own.link(nc.vector.tensor_scalar(gates[:, :, :], mods[which][:, first:first + KC, :], factor, None, ALU.mult))

            def norm(name):
                n, t0 = NORM_AT[name], START[name]
                dve.wait_ge(sem("rms_ready"), n + 1)
                own.link(nc.vector.reciprocal(rinv[:, t0:], rms[:, t0:]))
                if name.startswith("final"):
                    for kc in range(KC):
                        nc.vector.scalar_tensor_tensor(x[:, kc, t0:], x[:, kc, t0:], param(name, kc, 1), rinv[:, t0:],
                                                       ALU.mult, ALU.mult).then_inc(x_updated, 1)
                    return
                split = name != "norm_b"
                before = h_before(name)
                marks = []
                for kc in range(KC + 2):
                    if kc < KC:
                        if split and kc >= 4:
                            dve.wait_ge(sem("h_ready"), before + kc - 3)
                        target = squares[:, kc % 4, t0:] if split else h[:, kc, t0:]
                        nc.vector.tensor_tensor(target, x[:, kc, t0:], rinv[:, t0:], ALU.mult).then_inc(sem("h_scaled"), 1)
                    if 1 <= kc <= KC:
                        dve.wait_ge(sem("h_scaled"), before + kc)
                        s, b = modulation(name, kc - 1, 0)
                        target = squares[:, (kc - 1) % 4, CTX:] if split else h[:, kc - 1, CTX:]
                        nc.vector.tensor_scalar(target, target, s, b, ALU.mult, ALU.add)\
                            .then_inc(sem("h_lat_ready" if split else "h_ready"), 1)
                    if split and kc >= 2:
                        c = kc - 2
                        dve.wait_ge(sem("h_high"), before + c + 1)
                        dve.wait_ge(sem("h_lat_ready"), before + c + 1)
                        nc.vector.tensor_tensor(h_lo[:, c, t0:], squares[:, c % 4, t0:], h_hi[:, c, t0:].bitcast(F32), ALU.subtract)\
                            .then_inc(sem("h_ready"), 1)

            def swiglu(name, norm_name):
                f, t0 = FFNS.index(name), START[norm_name]
                with_up, with_down = SWIGLU[name]

                def product(p, j):
                    dve.wait_ge(sem("silu_ready"), p + (UP * f + 1))
                    nc.vector.tensor_tensor(squares[:, j, t0:], squares[:, j, t0:], bank[PAIR_BANKS[j][1]][:, 0:T - t0], ALU.mult)\
                        .then_inc(sem("pair_moved"), 1)

                def rest(p, j):
                    dve.wait_ge(sem("hidden_high"), p + (UP * f + 1))
                    nc.vector.tensor_tensor(hidden_lo[:, p, t0:], squares[:, j, t0:], hidden_hi[:, p, t0:].bitcast(F32), ALU.subtract)\
                        .then_inc(sem("hidden_ready"), 1)

                first = AT[f"up{name}", 0]
                per_unit = 2 if with_up else 1
                convert(first, 1)
                convert(first + per_unit, 0)
                half = At.half
                with dve.Fori(0, (UP - 1) // RING) as i:
                    for j in range(RING):
                        at = first + per_unit * (1 + j)
                        convert(at, 1, i * 2 * RING + (half + 2 * j))
                        product(i * RING + j, j)
                        if with_up:
                            tag, unit = SIDE_UNITS[At.side + j]
                            side(i * RING + (At.side + j), list(SIDES).index(tag), i * RING + (unit))
                        convert(at + per_unit, 0, i * 2 * RING + (half + 2 * j + 1))
                        rest(i * RING + j, j)
                At.half = half + 2 * (UP - 1)
                At.side += with_up
                last = (UP - 1, (UP - 1) % RING)
                return (lambda: product(*last)), (lambda: rest(*last))

            def update_chunk(name, kc, t0):
                dve.wait_ge(sem("acc_ready"), KC * BANKED.index(name) + kc + 1)
                acc = bank[OUT_BANK[kc]]
                for start, which in ((0, 1), (CTX, 0)):
                    if start >= t0:
                        last = nc.vector.scalar_tensor_tensor(x[:, kc, start:start + CTX], acc[:, start - t0:start - t0 + CTX],
                                                              gates[:, kc, which:which + 1], x[:, kc, start:start + CTX],
                                                              ALU.mult, ALU.add)
                last.then_inc(x_updated, 1)

            def down(name, update, sides, t0, which, j_gate, factor, ahead=()):
                for n in range(2 * 4 * len(GROUPS)):
                    j, sub = n // 2, n % 2
                    if n + 1 < 2 * 4 * len(GROUPS):
                        convert(AT[f"down{name}", (n + 1) // 2], (n + 1) % 2, chunks=GROUPS[(n + 1) // 2 % len(GROUPS)])
                    if n < len(ahead):
                        ahead[n]()
                    if sub == 0 and j < sides:
                        side_static(At.side)
                        At.side += 1
                    if n == 3:
                        gate_factors(which, j_gate, factor)
                    done = n - 1
                    if done >= 0 and done // 2 % len(GROUPS) == len(GROUPS) - 1:
                        update_chunk(update, 2 * (done // 2 // len(GROUPS)) + done % 2, t0)
                update_chunk(update, KC - 1, t0)

            def out_product(name, update, t0, then=None):
                for n in range(8):
                    if n < 7:
                        convert(AT[name, (n + 1) // 2], (n + 1) % 2)
                    if n:
                        update_chunk(update, n - 1, t0)
                update_chunk(update, 7, t0)
                if then is not None:
                    convert(then, 0)

            def mla_and_conv(i):
                tag, t0 = f"mix{i}", CTX if i == DEPTH - 1 else 0

                def latent_out(c):
                    first = t0 if c < 2 else 0
                    dve.wait_ge(sem(f"latent_sum{tag}"), c + 1)
                    target = latent[:, c, first:] if c < 3 else q_heads[:, HEADS, :]
                    nc.vector.tensor_copy(target, bank[c][:, 0:T - first]).then_inc(sem(f"latent_moved{tag}"), 1)

                def latent_norm(j):
                    first = t0 if j == 0 else 0
                    dve.wait_ge(sem(f"latent_rms{tag}"), j + 1)
                    own.link(nc.vector.reciprocal(latent_rinv[:, j, first:], latent_rms[:, j, first:]))
                    for c, w in ((0, param(f"q_norm{i}", 0, 1)), (1, param(f"q_norm{i}", 1, 1))) if j == 0 else \
                            ((2, param(f"kv_norm{i}")),):
                        nc.vector.scalar_tensor_tensor(latent[:, c, first:], latent[:, c, first:], w, latent_rinv[:, j, first:],
                                                       ALU.mult, ALU.mult).then_inc(sem(f"latent_ready{tag}"), 1)

                def conv_product(c):
                    dve.wait_ge(sem(f"conv_sum{tag}"), 9 + c)
                    dve.wait_ge(sem(f"conv_moved{tag}"), 5 + c)
                    nc.vector.tensor_tensor(conv_in[:, 4 + c, t0:], conv_in[:, 4 + c, t0:], bank[IN_BANK[12 + c]][:, 0:T - t0], ALU.mult)\
                        .then_inc(sem(f"conv_u{tag}"), 1)

                for n in range(17):
                    if n < 15:
                        convert(AT[f"in{i}", (n + 1) // 2], (n + 1) % 2)
                    if 1 <= n <= 4:
                        latent_out(n - 1)
                    if n in (10, 12):
                        latent_norm((n - 10) // 2)
                    if n >= 13:
                        conv_product(n - 13)

                def conv(c):
                    segments = (T - t0) // CTX
                    u = conv_in[:, 4 + c, t0:].rearrange("p (s t) -> p s t", s=segments)
                    gb = conv_in[:, c, t0:].rearrange("p (s t) -> p s t", s=segments)
                    y = squares[:, c, t0:].rearrange("p (s t) -> p s t", s=segments)
                    w = lambda tap: param(f"conv{i}", 4 * tap + c, 1)
                    dve.wait_ge(sem(f"conv_u{tag}"), 4)
                    own.link(nc.vector.tensor_scalar(y, u, w(1), None, ALU.mult))
                    own.link(nc.vector.scalar_tensor_tensor(y[:, :, 1:], u[:, :, :-1], w(0), y[:, :, 1:], ALU.mult, ALU.add))
                    own.link(nc.vector.scalar_tensor_tensor(y[:, :, :-1], u[:, :, 1:], w(2), y[:, :, :-1], ALU.mult, ALU.add))
                    nc.vector.tensor_tensor(y, y, gb, ALU.mult).then_inc(sem(f"conv_gated{tag}"), 1)

                for hd in range(HEADS):
                    dve.wait_ge(sem(f"head_sum{tag}"), 2 * hd + 2)
                    nc.vector.tensor_copy(k_heads[0:NOPE, hd, :], bank[IN_BANK[8 + (2 * hd + 1) % 4]][0:NOPE, :])\
                        .then_inc(sem(f"key_moved{tag}"), 1)
                    if hd % 2:
                        conv(hd // 2)
                R = slice(NOPE, QK)
                for r in range(5):
                    dve.wait_ge(sem(f"exchanged{tag}"), r + 1)
                    n = 1 if r == 0 else 2
                    f = q_heads[R, HEADS:HEADS + 1, CTX:] if r == 0 else q_heads[R, 2 * r - 2:2 * r, CTX:]
                    cos = const("cos")[R].unsqueeze(1).broadcast_to([ROPE, n, LAT])
                    sin = const("sin")[R].unsqueeze(1).broadcast_to([ROPE, n, LAT])
                    turned = rope_tmp[R, 0:n * LAT].rearrange("p (n t) -> p n t", n=n)
                    own.mark(nc.vector.tensor_tensor(turned, bank[ROPE_BANK[r]][R, 0:n * LAT].rearrange("p (n t) -> p n t", n=n), sin, ALU.mult))
                    own.link(nc.vector.tensor_tensor(f, f, cos, ALU.mult))
                    nc.vector.tensor_tensor(f, f, turned, ALU.add).then_inc(sem(f"roped{tag}"), 1)
                    dve.wait_ge(sem(f"roped{tag}"), r + 1)
                convert(AT[f"out{i}", 0], 0)
                for c in range(4):
                    dve.wait_ge(sem(f"conv_high{tag}"), c + 1)
                    nc.vector.tensor_tensor(h_lo[:, 4 + c, t0:], squares[:, c, t0:], h_hi[:, 4 + c, t0:].bitcast(F32), ALU.subtract)\
                        .then_inc(sem(f"conv_out{tag}"), 1)
                units = attention_units(t0)
                for n in range(len(units) + 3):
                    if n < len(units):
                        keys = units[n][2]
                        dve.wait_ge(sem(f"score{tag}"), n + 1)
                        own.link(nc.vector.tensor_reduce(small[:, 24 + n % 4:25 + n % 4], bank[SCORE_BANKS[n % 3]][:, 0:keys],
                                                         axis=AX_X, op=ALU.max))
                        nc.vector.tensor_scalar(small[:, n % 4:n % 4 + 1], small[:, 24 + n % 4:25 + n % 4], -SCALE, None, ALU.mult)\
                            .then_inc(sem(f"negmax{tag}"), 1)
                    m = n - 1
                    if 0 <= m < len(units):
                        keys = units[m][2]
                        dve.wait_ge(sem(f"exp{tag}"), m + 1)
                        own.link(nc.vector.reciprocal(small[:, 16 + m % 4:17 + m % 4], small[:, 8 + m % 4:9 + m % 4]))
                        nc.vector.tensor_scalar(probs[:, m % 3, 0:keys], probs[:, m % 3, 0:keys], small[:, 16 + m % 4:17 + m % 4],
                                                None, ALU.mult).then_inc(sem(f"prob{tag}"), 1)
                    m = n - 3
                    if 0 <= m < len(units):
                        hd, tc, _ = units[m]
                        half = slice(VD * (hd % 2), VD * (hd % 2) + VD)
                        dve.wait_ge(sem(f"attend_sum{tag}"), m + 1)
                        high = h_hi[half, hd // 2, tc * P:(tc + 1) * P]
                        own.link(nc.vector.tensor_copy(high, bank[m % 2][half, 0:P]))
                        nc.vector.tensor_tensor(h_lo[half, hd // 2, tc * P:(tc + 1) * P], bank[m % 2][half, 0:P], high.bitcast(F32),
                                                ALU.subtract).then_inc(sem(f"attended{tag}"), 1)

            def bounds_of_decay():
                logits = param("lb").rearrange("p (d l c) -> p d l c", d=2, l=2)
                nc.vector.tensor_tensor(small[:, 56:64].rearrange("p (d c) -> p d c", d=2), logits[:, :, 0, :], logits[:, :, 1, :],
                                        ALU.subtract).then_inc(sem("bound_logits"), 1)

            def gate_rows():
                g = squares[:, 3, :]
                dve.wait_ge(sem("value_turned"), len(V_HALVES))
                nc.vector.scalar_tensor_tensor(squares[:, 1, :], g, -1.0, g, ALU.mult, ALU.max).then_inc(sem("gate_abs"), 1)
                dve.wait_ge(sem("gate_log"), 1)
                log_f = squares[:, 1, :]
                own.link(nc.vector.scalar_tensor_tensor(log_f, g, 0.0, log_f, ALU.min, ALU.subtract))

                def segments(a, backwards):
                    v = a.rearrange("p (s t) -> p s t", s=2)
                    return v[:, :, ::-1] if backwards else v

                sums = [squares[0:MH, 2, :], squares[0:MH, 0, :]]
                u_back = arena[0:MH, 43, :]
                own.mark(nc.vector.tensor_copy(sums[0], squares[32:32 + MH, 1, :]))
                own.mark(nc.vector.tensor_copy(segments(sums[1], False), segments(squares[96:96 + MH, 1, :], True)))
                own.link(nc.vector.tensor_copy(segments(u_back, False), segments(squares[64:64 + MH, 3, :], True)))
                for d in range(2):
                    own.link(nc.vector.tensor_tensor_scan(sums[d], sums[d], sums[d], 0.0, ALU.add, ALU.bypass))
                own.mark(nc.vector.tensor_tensor(u_rows[0], squares[0:MH, 3, :], sums[0], ALU.subtract))
                own.link(nc.vector.tensor_tensor(u_back, u_back, sums[1], ALU.subtract))
                maxima = [rms[0:MH, :], rinv[0:MH, :]]
                for d, u in enumerate((u_rows[0], u_back)):
                    own.link(nc.vector.tensor_tensor_scan(maxima[d], u, u, 0.0, ALU.max, ALU.bypass))
                for d in range(2):
                    own.link(nc.vector.scalar_tensor_tensor(sums[d][:, CTX:], maxima[d][:, CTX:], -1.0, sums[d][:, CTX:],
                                                            ALU.mult, ALU.subtract))
                own.mark(nc.vector.tensor_copy(segments(u_rows[1], False), segments(u_back, True)))
                own.mark(nc.vector.tensor_copy(m_rows[1], maxima[1][:, CTX:][:, ::-1]))
                own.mark(nc.vector.tensor_copy(floor_rows[1], sums[1][:, CTX:][:, ::-1]))
                own.wait(own.n)
                nc.vector.memset(small[:, 39:40], 0.0).then_inc(sem("gate_rows"), 1)

            def qk_conv(group, c):
                dve.wait_ge(sem("projected"), 4 * group + c + 1)
                windows = [(q_raw[:, c, :], q_ml[:, c, :], ROWS, GRID)] if group == 0 else \
                    [(k_raw[:, c, CTX:], k_ml[:, c, CTX:], ROWS, GRID), (k_raw[:, c, 0:CTX], k_ml[:, c, 0:CTX], 1, CTX)]
                for source, target, rows, cols in windows:
                    source, target = (a.rearrange("p (r c) -> p r c", c=cols) for a in (source, target))
                    own.link(nc.vector.tensor_scalar(target, source, param("qk_conv", KC * 4 + 4 * group + c, 1), None, ALU.mult))
                    for tap, (ro, co), (ri, ci) in taps(rows, cols):
                        to = target[:, ro, co]
                        own.link(nc.vector.scalar_tensor_tensor(to, source[:, ri, ci], param("qk_conv", KC * tap + 4 * group + c, 1), to,
                                                                ALU.mult, ALU.add))
                dve.sem_inc(sem("qk_conv"), 1)

            def decay_sums(d, c):
                dve.wait_ge(sem("bounds"), 1)
                dve.wait_ge(sem("projected"), 16)
                own.mark(nc.vector.tensor_scalar(k_hg[d][:, c, :], k_hg[d][:, c, :], bounds[:, 1, d, c:c + 1], None, ALU.mult))
                dve.wait_ge(sem("log_decay"), 4 * d + c + 1)
                for s in range(2):
                    part = decay[d][:, c, s * CTX:(s + 1) * CTX]
                    part = part[:, ::-1] if d else part
                    nc.vector.tensor_tensor_scan(part, part, part, 0.0, ALU.add, ALU.bypass).then_inc(sem("decay_summed"), 1)

            def projections():
                convert(AT["in", 0], 0)
                dve.wait_ge(sem("gate_sum"), 1)
                own.link(nc.vector.tensor_scalar(squares[:, 3, :], bank[5][:, :], param("gate_b"), None, ALU.add))
                for n in range(len(HALVES_B) - 1):
                    convert(AT["in", (n + 1) // 2], (n + 1) % 2)
                    if 8 <= n < 16:
                        qk_conv((n - 8) // 4, n % 4)
                    if 20 <= n < 28:
                        decay_sums((n - 20) // 4, n % 4)

            def hgrn():
                dve.wait_ge(sem("decay_summed"), 16)
                dve.wait_ge(sem("qk_conv"), 8)
                own.wait(own.n)

                def blocks(a, size):
                    return a.rearrange("p h (n two b) -> p h n two b", two=2, b=size)

                def differences(n):
                    stage = HG_STAGES[n]
                    dve.wait_ge(sem("hg_product"), n - 1)
                    if stage == "diagonal":
                        return
                    size = 1 << stage
                    q, k = (blocks(f, size) for f in hg_factor[n % 2])
                    f, b = (blocks(decay[d][:, :, CTX:], size) for d in range(2))
                    shape = [P, MH, LAT // (2 * size), size]
                    last_left = f[:, :, :, 0, size - 1:size].broadcast_to(shape)
                    first_right = b[:, :, :, 1, 0:1].broadcast_to(shape)
                    last = None
                    for out_, a, c in ((q[:, :, :, 1, :], f[:, :, :, 1, :], last_left), (k[:, :, :, 0, :], last_left, f[:, :, :, 0, :]),
                                       (q[:, :, :, 0, :], b[:, :, :, 0, :], first_right), (k[:, :, :, 1, :], first_right, b[:, :, :, 1, :])):
                        if last is not None:
                            own.mark(last)
                        last = nc.vector.tensor_tensor(out_, a, c, ALU.subtract)
                    last.then_inc(sem("hg_differences"), 1)

                def scale(n):
                    stage = HG_STAGES[n]
                    q, k = hg_factor[n % 2]
                    if stage == "diagonal":
                        nc.vector.tensor_tensor(k, k_hg[0][:, :, CTX:], k_hg[1][:, :, CTX:], ALU.add).then_inc(sem("hg_scaled"), 1)
                        return
                    dve.wait_ge(sem("hg_exp"), n + 1)
                    own.mark(nc.vector.tensor_tensor(q, q, q_hg, ALU.mult))
                    if stage in ("ctx0", "ctx1"):
                        last = nc.vector.tensor_tensor(k, k, k_hg[n][:, :, 0:CTX], ALU.mult)
                    else:
                        kb = blocks(k, 1 << stage)
                        for d in range(2):
                            source = blocks(k_hg[d][:, :, CTX:], 1 << stage)
                            last = nc.vector.tensor_tensor(kb[:, :, :, d, :], kb[:, :, :, d, :], source[:, :, :, d, :], ALU.mult)
                            if d == 0:
                                own.mark(last)
                    own.wait(own.n)
                    last.then_inc(sem("hg_scaled"), 1)

                def place(n):
                    stage = HG_STAGES[n]
                    dve.wait_ge(sem("hg_product"), n + 1)
                    for c in range(2):
                        scores = bank[4 + 2 * (n % 2) + c][:, :].rearrange("p (h t) -> p h t", h=MH)
                        if stage == LEVELS:
                            last = nc.vector.tensor_copy(hg_scores[:, :, c, (1 - c) * P:(2 - c) * P], scores)
                        else:
                            level = LEVELS if stage == "diagonal" else stage
                            mask = const("level", level * P, P).bitcast(U32).unsqueeze(1).broadcast_to([P, MH, P])
                            last = nc.vector.copy_predicated(hg_scores[:, :, c, c * P:(c + 1) * P], mask, scores)
                        if c == 0:
                            own.mark(last)
                    own.wait(own.n)
                    last.then_inc(sem("hg_placed"), 1)

                dve.wait_ge(sem("projected"), len(HALVES_B))
                own.link(nc.vector.memset(hg_scores, 0.0))
                scale(0)
                differences(2)
                scale(1)
                for n in range(3, len(HG_STAGES)):
                    differences(n)
                    scale(n - 1)
                    if n >= 4:
                        place(n - 2)
                place(len(HG_STAGES) - 2)
                scale(len(HG_STAGES) - 1)
                place(len(HG_STAGES) - 1)

            def mlstm():
                dve.wait_ge(sem("u_turned"), 1)
                nc.vector.tensor_copy(u_cols, bank[2][:, 0:2 * 4 * MH]).then_inc(sem("u_cols"), 1)
                dve.wait_ge(sem("u_cols"), 1)

                def mask(n):
                    hd, d = n // 2, n % 2
                    dve.wait_ge(sem("ml_max"), n + 1)
                    for c in range(2):
                        u = u_cols[:, MH * (4 * d + 2 + c) + hd:MH * (4 * d + 2 + c) + hd + 1]
                        last = nc.vector.scalar_tensor_tensor(ml_decay[d][:, 2 + c, c * P:(c + 1) * P], const("causal", d * P, P), u,
                                                              bank[2 + d][:, c * P:(c + 1) * P], ALU.add, ALU.subtract)
                        if c == 0:
                            own.mark(last)
                    own.wait(own.n)
                    last.then_inc(sem("ml_masked"), 1)

                def weigh(n):
                    hd, d = n // 2, n % 2
                    dve.wait_ge(sem("ml_score"), hd + 1)
                    dve.wait_ge(sem("ml_decayed"), n + 1)
                    if n >= 2:
                        dve.wait_ge(sem("ml_num_sum"), n - 1)
                    own.mark(nc.vector.scalar_tensor_tensor(ml_weight[d][:, 0:2, :], bank[0][:, :].rearrange("p (c t) -> p c t", c=2), MSCALE,
                                                            ml_decay[d][:, 0:2, :], ALU.mult, ALU.mult))
                    for c in range(2):
                        a, b = lat_valid(d, c)
                        last = nc.vector.scalar_tensor_tensor(ml_weight[d][:, 2 + c, a:b], bank[1][:, c * LAT + a:c * LAT + b], MSCALE,
                                                              ml_decay[d][:, 2 + c, a:b], ALU.mult, ALU.mult)
                        if c == 0:
                            own.mark(last)
                    own.wait(own.n)
                    last.then_inc(sem("ml_weighted"), 1)

                mask(0)
                for n in range(2 * MH):
                    if n + 1 < 2 * MH:
                        mask(n + 1)
                    weigh(n)
                dve.wait_ge(sem("ml_num_sum"), 2 * MH)
                for d in range(2):
                    own.mark(nc.vector.tensor_copy(ml_den[:, d * LAT:(d + 1) * LAT], bank[6 + d][0:MH, 0:LAT]))
                own.wait(own.n)
                own.link(nc.vector.scalar_tensor_tensor(ml_den, ml_den, -1.0, ml_den, ALU.mult, ALU.max))
                dve.wait_ge(sem("ml_floor"), 2)
                own.link(nc.vector.tensor_tensor(ml_den, ml_den, ml_floor, ALU.max))
                nc.vector.reciprocal(ml_den, ml_den).then_inc(sem("ml_den_ready"), 1)
                dve.wait_ge(sem("ml_num_moved"), 2 * MH)
                for hd in range(MH):
                    dve.wait_ge(sem("ml_den_spread"), hd + 1)
                    own.link(nc.vector.tensor_tensor(ml_num[:, hd, :], ml_num[:, hd, :], bank[hd][:, :], ALU.mult))
                    nc.vector.tensor_tensor(ml_out[:, hd, :], ml_num[:, hd, 0:LAT], ml_num[:, hd, LAT:], ALU.add).then_inc(sem("ml_out"), 1)

            def head_norms():
                convert(AT["out", 0], 0)
                dve.wait_ge(sem("out_rms"), 1)
                nc.vector.reciprocal(out_rinv, out_rms).then_inc(sem("out_rinv"), 1)
                for j in range(8):
                    source = ml_out[:, j, :] if j < MH else hg_out[:, j - MH, :]
                    gate = o_gate[:, j, :] if j < MH else g_gate[:, j - MH, :]
                    weight = param("ml_norm", j, 1) if j < MH else param("hg_norm", j - MH, 1)
                    dve.wait_ge(sem("out_rinv_spread"), 8 if j % 2 == 0 else j + 1)
                    own.link(nc.vector.scalar_tensor_tensor(source, source, weight, bank[j // 2][:, j % 2 * LAT:(j % 2 + 1) * LAT],
                                                            ALU.mult, ALU.mult))
                    nc.vector.tensor_tensor(source, source, gate, ALU.mult).then_inc(sem("out_gated"), 1)
                    if j:
                        out_rest(j - 1)
                out_rest(7)

            def out_rest(j):
                source = ml_out[:, j, :] if j < MH else hg_out[:, j - MH, :]
                dve.wait_ge(sem("out_high"), j + 1)
                nc.vector.tensor_tensor(h_lo[:, j, CTX:], source, h_hi[:, j, CTX:].bitcast(F32), ALU.subtract).then_inc(sem("mixed_b"), 1)

            def conv_ffn():
                def convolve(p, j):
                    k = 0
                    dve.wait_ge(sem("up_moved"), p + 4)
                    for tap, (ro, co), (ri, ci) in taps(ROWS, GRID):
                        for part in range(2):
                            source = raw_b[j][part].rearrange("p (r c) -> p r c", c=GRID)
                            acc = acc_b[j][part].rearrange("p (r c) -> p r c", c=GRID)
                            w = params[:, bass.ds(p + (PARAMS["ffn_conv"][0] + tap * 2 * FC + part * FC), 1)]
                            if k >= 2:
                                dve.wait_ge(sem("tap"), p * N_TAPS + (k - 1))
                            nc.vector.scalar_tensor_tensor(acc[:, ro, co], source[:, ri, ci], w, acc[:, ro, co], ALU.mult, ALU.add)\
                                .then_inc(sem("tap"), 1)
                            k += 1

                def product(p, j):
                    dve.wait_ge(sem("tap"), p * N_TAPS + N_TAPS)
                    dve.wait_ge(sem("gate_b"), p + 1)
                    dve.wait_ge(sem("hidden_ready"), p + (UP * len(FFNS) - 2))
                    nc.vector.tensor_tensor(product_b[j], acc_b[j][0], acc_b[j][1], ALU.mult).then_inc(sem("product_b"), 1)

                def rest(p, j):
                    dve.wait_ge(sem("product_b"), p + 4)
                    dve.wait_ge(sem("hidden_high"), p + (UP * len(FFNS) + 1))
                    nc.vector.tensor_tensor(hidden_lo[:, p, CTX:], product_b[j], hidden_hi[:, p, CTX:].bitcast(F32), ALU.subtract)\
                        .then_inc(sem("hidden_ready"), 1)

                dve.sem_inc(sem("product_b"), 3)
                convolve(0, 0)
                convolve(1, 1)
                product(0, 0)
                with dve.Fori(0, (UP - 4) // RING) as i:
                    for j in range(RING):
                        convolve(i * RING + (2 + j), (2 + j) % RING)
                        product(i * RING + (1 + j), (1 + j) % RING)
                        rest(i * RING + j, j)
                for p in range(UP - 4, UP):
                    if p + 2 < UP:
                        convolve(p + 2, (p + 2) % RING)
                    if p + 1 < UP:
                        product(p + 1, (p + 1) % RING)
                    rest(p, p % RING)
                convert(AT["down", 0], 0)

            dve.wait_ge(loaded, 48)
            nc.vector.memset(cond[:, :, :, :], 0.0).then_inc(sem("cond_zero"), 1)
            for j in range(FIRST_SIDES):
                side_static(j)
            At.side = FIRST_SIDES
            for i in range(DEPTH):
                t0 = CTX if i == DEPTH - 1 else 0
                if i == 0:
                    convert(AT["up10", 0], 0)
                factors(i, 0, (f"norm{i}", 0, KC))
                norm(f"norm1{i}")
                down(f"1{i}", f"ffn1{i}", SWIGLU[f"1{i}"][1], 0, i, 0, 0.5, swiglu(f"1{i}", f"norm1{i}"))
                convert(AT[f"in{i}", 0], 0)
                factors(i, 1, (f"norm{i}", KC, KC))
                norm(f"norm2{i}")
                mla_and_conv(i)
                gate_factors(i, 1, 1.0)
                out_product(f"out{i}", f"mix{i}", t0, AT[f"up2{i}", 0])
                factors(i, 2, (f"norm{i}", 2 * KC, KC))
                norm(f"norm3{i}")
                down(f"2{i}", f"ffn2{i}", SWIGLU[f"2{i}"][1], t0, i, 2, 0.5, swiglu(f"2{i}", f"norm3{i}"))
                if i + 1 < DEPTH:
                    convert(AT[f"up1{i + 1}", 0], 0)
            norm("final1")
            if until is None:
                convert(AT["gate", 0], 0)
                factors(2, 0, ("norm_a",))
                dve.wait_ge(sem("ctx2_loaded"), 16)
                norm("norm_a")
                bounds_of_decay()
                projections()
                gate_rows()
                hgrn()
                mlstm()
                head_norms()
                gate_factors(2, 0, 1.0)
                out_product("out", "mix_b", CTX)
                factors(2, 1, ("norm_b",))
                norm("norm_b")
                conv_ffn()
                down("", "ffn_b", 0, CTX, 2, 1, 1.0)
                norm("final2")

        @block.gpsimd
        def _(pool):
            for i in range(DEPTH):
                tag = f"mix{i}"
                pool.wait_ge(sem(f"roped{tag}"), 1)
                nc.gpsimd.tensor_copy(k_heads[NOPE:QK, :, :], q_heads[NOPE:QK, HEADS, :].unsqueeze(1).broadcast_to([ROPE, HEADS, T]))\
                    .then_inc(sem(f"key_rope{tag}"), 1)
            if until is None:
                pool.wait_ge(x_updated, KC * UPDATED["norm_a"])
                pool.dma_start(x[:, :, 0:CTX], ctx2_in).then_inc(sem("ctx2_loaded"), 16)
                pool.wait_ge(sem("ctx2_loaded"), 16)




def columns(v):
    v = np.asarray(v)
    return v.reshape(-1, P).T


def lay_params(a):
    out = np.zeros((P, N_PARAMS), np.float32)

    def put(name, value, rows=P):
        first, width = PARAMS[name]
        out[0:rows, first:first + value.shape[1]] = value

    for i in range(DEPTH):
        put(f"norm{i}", columns(a["norm_w"][i].reshape(-1)))
        put(f"b_ada{i}", columns(a["b_ada"][i]))
        put(f"q_norm{i}", columns(a["q_norm_w"][i]))
        put(f"kv_norm{i}", columns(a["kv_norm_w"][i]))
        put(f"conv{i}", columns(a["conv_w"][i].reshape(-1)))
    put("final1", columns(a["final_norm_w"]))
    put("c1", np.stack([columns(a["c"][0]), columns(a["c_ctx"])], 2).reshape(P, -1))
    put("c2", np.stack([columns(a["c_2"][0]), columns(a["c_ctx_2"])], 2).reshape(P, -1))
    put("b_mod", columns(a["b_mod_2"][0]))
    put("norm_a", columns(a["norm1_w_2"][0]))
    put("norm_b", columns(a["norm2_w_2"][0]))
    gate_b = np.zeros((P, 1), np.float32)
    for j in range(4):
        gate_b[32 * j:32 * j + MH, 0] = a["mlstm_gate_b_2"][0, MH * j:MH * (j + 1)]
    put("gate_b", gate_b)
    put("qk_conv", columns(a["mlstm_conv_w_2"][0].reshape(-1)))
    put("ml_norm", columns(a["mlstm_norm_w_2"][0]))
    put("lb", columns(a["hgrn_lb_logits_2"].reshape(-1)))
    put("hg_norm", columns(a["hgrn_norm_w_2"][0]))
    put("ffn_conv", columns(a["ffn_conv_w_2"][0].reshape(-1)))
    put("final2", columns(a["final_norm_w_2"]))
    return out


def lay_consts():
    out = np.zeros((P, N_CONSTS), np.float32)

    def put(name, value, first_row=0):
        first, _ = CONSTS[name]
        out[first_row:first_row + value.shape[0], first:first + value.shape[1]] = value

    put("ident", np.eye(P, dtype=np.float32))
    put("ones", np.ones((P, P), np.float32))
    put("sum_rows", (np.arange(P)[:, None] % 32 == np.arange(2)[None, :]).astype(np.float32))
    put("eps", np.full((P, 1), EPS, np.float32))
    axis, half = ROPE // 2, ROPE // 4
    inv = np.float32(10000.0) ** (-np.arange(0, axis, 2, dtype=np.float32) / np.float32(axis))
    t = np.arange(LAT)
    angle = np.concatenate([np.outer(inv, (t // GRID).astype(np.float32))] * 2
                           + [np.outer(inv, (t % GRID).astype(np.float32))] * 2)
    put("cos", np.cos(angle), NOPE)
    put("sin", np.sin(angle), NOPE)
    perm = np.zeros((P, P), np.float32)
    for d in range(ROPE):
        low = d % axis < half
        perm[NOPE + (d + half if low else d - half), NOPE + d] = -1.0 if low else 1.0
    put("perm", perm)
    s, t = np.arange(P)[:, None], np.arange(P)[None, :]
    for j in range(LEVELS):
        put_at = (s >> (j + 1) == t >> (j + 1)) & (s >> j != t >> j)
        out[:, CONSTS["level"][0] + j * P:CONSTS["level"][0] + (j + 1) * P] = put_at
    out[:, CONSTS["level"][0] + LEVELS * P:CONSTS["level"][0] + (LEVELS + 1) * P] = s == t
    put("causal", np.concatenate([np.where(s <= t, 0.0, NEG), np.where(s >= t, 0.0, NEG)], 1).astype(np.float32))
    for j in range(8):
        out[:, CONSTS["col_of"][0] + 8 * j + j] = 1.0
    return out


def lay_stream(a):
    out = np.zeros((N_UNITS, P, KC, UNIT), np.float32)

    def rows(w):
        return w.reshape(-1, P, w.shape[1]).transpose(1, 0, 2)

    def by_columns(name, w):
        for j in range(w.shape[1] // UNIT):
            out[AT[name, j]] = rows(w[:, j * UNIT:(j + 1) * UNIT])

    def up(name, w):
        for j in range(UP):
            out[AT[name, j], :, :, 0:P] = rows(w[:, j * P:(j + 1) * P])
            out[AT[name, j], :, :, P:] = rows(w[:, FF + j * P:FF + (j + 1) * P])

    def down(name, w):
        for j in range(4 * len(GROUPS)):
            g, pair = j % len(GROUPS), j // len(GROUPS)
            out[AT[name, j], :, 0:GROUPS[g], :] = rows(w[g * KC * P:(g + 1) * KC * P, pair * UNIT:(pair + 1) * UNIT])

    for i in range(DEPTH):
        by_columns(f"ada{i}", a["w_ada"][i])
        for n in (1, 2):
            up(f"up{n}{i}", a[f"w_ffn{n}_in"][i])
            down(f"down{n}{i}", a[f"w_ffn{n}_out"][i])
        w = a["w_in"][i]
        w_in = np.zeros((D, 4 * P + 3 * CONV), np.float32)
        w_in[:, 0:QR + KVR] = w[:, 0:QR + KVR]
        w_in[:, QR + KVR + NOPE:QR + KVR + QK] = w[:, QR + KVR:QR + KVR + ROPE]
        w_in[:, 4 * P:] = w[:, QR + KVR + ROPE:]
        by_columns(f"in{i}", w_in)
        out[AT[f"uq{i}", 0]].reshape(P, -1)[:, 0:2 * HEADS * QK] = rows(a["w_uq"][i]).reshape(P, -1)
        out[AT[f"ukv{i}", 0]].reshape(P, -1)[:, 0:HEADS * (NOPE + VD)] = a["w_ukv"][i]
        by_columns(f"out{i}", a["w_out"][i])
    by_columns("mod", a["w_mod_2"][0])
    w, width = a["w_in_2"][0], MH * P
    hg = 4 * width + 4 * MH
    for j in range(4):
        out[AT["gate", 0], :, :, 32 * j:32 * j + MH] = rows(w[:, 4 * width + MH * j:4 * width + MH * (j + 1)])
    by_columns("in", np.concatenate([w[:, first(width, hg):first(width, hg) + width] for first in PROJECTIONS.values()], 1))
    by_columns("out", a["w_out_2"][0])
    up("up", a["w_up_2"][0])
    down("down", a["w_down_2"][0])
    return out


def feature_major(a):
    return np.ascontiguousarray(a.T.reshape(KC, P, -1).transpose(1, 0, 2))


def lay_out(a):
    return {
        "stream": lay_stream(a),
        "x_in": feature_major(np.concatenate([a["ctx"][0], a["x"][0]], 0)),
        "ctx2_in": feature_major(a["ctx_2"][0]),
        "params_in": lay_params(a),
        "consts_in": lay_consts(),
    }


def kernel(**inputs):
    import concourse.bacc as bacc
    from concourse.bass_utils import run_bass_kernel_spmd

    nc = bacc.Bacc("TRN2", target_bir_lowering=False, num_devices=1)
    arrays = lay_out({k: np.asarray(v) for k, v in inputs.items()})
    args = [nc.dram_tensor(n, v.shape, F32, kind="ExternalInput").ap() for n, v in arrays.items()]
    out = nc.dram_tensor("out", (P, KC, LAT), F32, kind="ExternalOutput").ap()
    build_program(nc, *args, out)
    result = run_bass_kernel_spmd(nc, [arrays], core_ids=[0])
    out = result.results[0]["out"]
    return np.ascontiguousarray(out.transpose(1, 0, 2).reshape(D, LAT).T)[None]
```

```python
from contextlib import ExitStack

import numpy as np

import concourse.bass as bass
from concourse import mybir

F32 = mybir.dt.float32
F32R = mybir.dt.float32r
U32 = mybir.dt.uint32
ACT = mybir.ActivationFunctionType
ALU = mybir.AluOpType
AX_X = mybir.AxisListType.X

P = 128
D = 1024
KC = D // P
CTX, LAT = 256, 256
T = CTX + LAT
FF = 2816
FC = FF // P
DEPTH = 2
N_MOD, N_MOD_2 = 9, 6
HEADS, NOPE, ROPE, VD = 8, 64, 32, 64
QK = NOPE + ROPE
QR, KVR = 256, 128
CONV = 512
GRID = 64
ROWS = LAT // GRID
EPS = 1e-6
SCALE = QK ** -0.5
UNIT = 2 * P
RING = 3
MH = 4
MSCALE = P ** -0.5
NEG = -1.0e30



def _columns(parts):
    at, where = 0, {}
    for name, n in parts:
        where[name] = (at, n)
        at += n
    return where, at


PARAMS, N_PARAMS = _columns(
    [(f"norm{i}", 3 * KC) for i in range(DEPTH)] + [(f"b_ada{i}", N_MOD * KC) for i in range(DEPTH)]
    + [(f"q_norm{i}", QR // P) for i in range(DEPTH)] + [(f"kv_norm{i}", 1) for i in range(DEPTH)]
    + [(f"conv{i}", 3 * (CONV // P)) for i in range(DEPTH)]
    + [("final1", KC), ("c1", 2 * KC), ("c2", 2 * KC), ("b_mod", N_MOD_2 * KC), ("norm_a", KC), ("norm_b", KC),
       ("gate_b", 1), ("qk_conv", 9 * KC), ("ml_norm", MH), ("lb", 2 * 2 * MH), ("hg_norm", MH),
       ("ffn_conv", 9 * 2 * FC), ("final2", KC)])
LEVELS = 7
CONSTS, N_CONSTS = _columns(
    [("ident", P), ("ones", P), ("sum_rows", 2), ("perm", P), ("cos", LAT), ("sin", LAT), ("eps", 1),
     ("level", (LEVELS + 1) * P), ("causal", 2 * P), ("col_of", 8 * 8)])

UP = FC
GROUPS = (KC, KC, FC - 2 * KC)
SIDES = {"ada0": N_MOD * D // UNIT, "ada1": N_MOD * D // UNIT, "mod": N_MOD_2 * D // UNIT}
SIDE_UNITS = [(name, j) for name, n in SIDES.items() for j in range(n)]
FIRST_SIDES = 2 * D // UNIT
SWIGLU = {"10": (UP - 1, 10), "20": (UP - 1, 12), "11": (UP - 1, 3), "21": (0, 0)}


def _order():
    order, sides = [], iter(SIDE_UNITS)
    order += [next(sides) for _ in range(FIRST_SIDES)]
    for i in range(DEPTH):
        for n in (1, 2):
            name = f"{n}{i}"
            with_up, with_down = SWIGLU[name]
            for p in range(UP):
                order += [next(sides)] if with_up and p else []
                order.append((f"up{name}", p))
            for j in range(4 * len(GROUPS)):
                order += [next(sides)] if j < with_down else []
                order.append((f"down{name}", j))
            if n == 1:
                order += [(f"in{i}", j) for j in range(8)] + [(f"uq{i}", 0), (f"ukv{i}", 0)] + [(f"out{i}", j) for j in range(4)]
    order += [("gate", 0)] + [("in", j) for j in range(18)] + [("out", j) for j in range(4)]
    order += [("up", j) for j in range(UP)] + [("down", j) for j in range(4 * len(GROUPS))]
    assert next(sides, None) is None
    return order


ORDER = _order()
AT = {unit: at for at, unit in enumerate(ORDER)}
N_UNITS = -(-len(ORDER) // RING) * RING

PROJECTIONS = {
    "ml_q": lambda w, hg: 0, "ml_k": lambda w, hg: w, "hg_zf": lambda w, hg: hg + w, "hg_zb": lambda w, hg: hg + 2 * w,
    "hg_q": lambda w, hg: hg, "ml_v": lambda w, hg: 2 * w, "hg_v": lambda w, hg: hg + 3 * w,
    "ml_o": lambda w, hg: 3 * w, "hg_g": lambda w, hg: hg + 4 * w}



def build_program(nc, stream, x_in, ctx2_in, params_in, consts_in, out, until=None):
    with ExitStack() as stack:
        def sb(name, shape):
            return stack.enter_context(nc.sbuf_tensor(name, shape, F32))

        raw = [sb(f"raw{s}", [P, KC, UNIT]) for s in range(RING)]
        x = sb("x", [P, KC, T])
        squares = sb("squares", [P, 4, T])
        rms = sb("rms", [P, T])
        rinv = sb("rinv", [P, T])
        params = sb("params", [P, N_PARAMS])
        consts = sb("consts", [P, N_CONSTS])
        cond = sb("cond", [P, 2, KC, 32])
        mods = [sb(f"mod_{name}", [P, n * UNIT // P, 2]) for name, n in SIDES.items()]
        scales = sb("scales", [P, KC, 2])
        gates = sb("gates", [P, KC, 2])
        side_row = sb("side_row", [P, UNIT])
        small = sb("small", [P, 80])
        w_hi = stack.enter_context(nc.sbuf_tensor("w_hi", [P, 2, KC, P], F32R))
        w_lo = stack.enter_context(nc.sbuf_tensor("w_lo", [P, 2, KC, P], F32R))
        with ExitStack() as shared:
            h_hi = shared.enter_context(nc.sbuf_tensor("h_hi", [P, KC, T], F32R))
            h_lo = shared.enter_context(nc.sbuf_tensor("h_lo", [P, KC, T], F32R))
            hidden_hi = shared.enter_context(nc.sbuf_tensor("hidden_hi", [P, FC, T], F32R))
            hidden_lo = shared.enter_context(nc.sbuf_tensor("hidden_lo", [P, FC, T], F32R))
        h = sb("h", [P, 2 * KC, T])
        arena = sb("arena", [P, 2 * FC, T])
        bank = [stack.enter_context(nc.psum_tensor(f"bank{b}", [P, 512], F32)) for b in range(8)]
        sems = {}

        def sem(name):
            if name not in sems:
                sems[name] = stack.enter_context(nc.semaphore(name))
            return sems[name]

        def param(name, a=0, n=None):
            first, width = PARAMS[name]
            return params[:, first + a:first + a + (width - a if n is None else n)]

        def const(name, a=0, n=None, rows=P):
            first, width = CONSTS[name]
            return consts[0:rows, first + a:first + a + (width - a if n is None else n)]

        ident, ones = const("ident"), const("ones")

        unit_full = [sem(f"unit_full{s}") for s in range(RING)]
        unit_begun = sem("unit_begun")
        half_begun = sem("half_begun")
        half_high = sem("half_high")
        half_ready = sem("half_ready")
        loaded = sem("inputs_loaded")
        x_updated = sem("x_updated")

        UPDATES = [f"{s}{i}" for i in range(DEPTH) for s in ("ffn1", "mix", "ffn2")]
        BANKED = UPDATES + ["mix_b", "ffn_b"]
        NORMS = [(f"norm{n + 1}{i}", 3 * i + n, CTX if i == DEPTH - 1 and n == 2 else 0)
                 for i in range(DEPTH) for n in range(3)]
        NORMS += [("final1", 3 * DEPTH, CTX), ("norm_a", 3 * DEPTH + 1, 0), ("norm_b", 3 * DEPTH + 2, CTX),
                  ("final2", 3 * DEPTH + 3, CTX)]
        NORM_AT = {name: n for n, (name, _, _) in enumerate(NORMS)}
        UPDATED = {name: updates for name, updates, _ in NORMS}
        START = {name: t0 for name, _, t0 in NORMS}
        OUT_BANK = (2, 3, 6, 7, 0, 1, 2, 3)
        PAIR_BANKS = ((0, 1), (2, 3), (6, 7))
        ROW_BANK, TURN_BANK = 4, 5
        HEAD_NORM_BANK = (0, 1, 4, 5)
        SUM_BANK, SPREAD_BANK = 4, 5
        norm_rms, norm_rinv = small[:, 64:68], small[:, 68:72]
        ADDED = KC - 2
        square_sum = rinv
        norm_diag = rms

        def earlier(name, counts):
            return sum(1 for n, (other, _, t0) in enumerate(NORMS) if n < NORM_AT[name] and counts(other, t0))

        def modulated(name, t0):
            return not name.startswith("final")

        def h_before(name):
            return KC * earlier(name, modulated)

        def joint(name):
            return name[:5] in ("norm1", "norm2", "norm3") or name == "norm_a"

        def diags_before(name):
            return sum((T - t0) // P for _, _, t0 in NORMS[:NORM_AT[name]])

        def before_updates(update):
            return KC * (UPDATES.index(update) if update in UPDATES else 3 * DEPTH + 1 + BANKED.index(update) - 3 * DEPTH)

        IN_BANK = (0, 1, 2, 3) + (6, 7, 2, 3) * 3
        ROPE_BANK = (4, 0, 4, 5, 0)

        def full_wait(engine, at, rounds=0):
            engine.wait_ge(unit_full[at % RING], rounds * 16 + 16 * (at // RING + 1))

        FFNS = list(SWIGLU)

        class Chain:

            def __init__(self, engine, name):
                self.engine, self.sem, self.n = engine, sem(name), 0

            def mark(self, instruction):
                self.n += 1
                instruction.then_inc(self.sem, 1)
                return self.n

            def wait(self, n):
                self.engine.wait_ge(self.sem, n)

            def link(self, instruction):
                self.wait(self.mark(instruction))

        def attention_units(t0):
            return [(hd, tc, CTX if tc * P < CTX else T) for hd in range(HEADS) for tc in range(t0 // P, T // P)]

        latent = arena[:, 0:4, :]
        conv_in = arena[:, 4:12, :]
        q_heads, k_heads = arena[:, 12:21, :], arena[:, 21:29, :]
        values = arena[:, 29:33, :]
        probs, probs_turned = arena[:, 33:36, :], arena[:, 36:38, :]
        latent_rms, latent_rinv = arena[:, 38:40, :], arena[:, 40:42, :]
        rope_tmp = arena[:, 42, :]
        SCORE_BANKS = (2, 4, 5)
        CONV_STEPS = [[len(attention_units(t)) * (c + 1) // 4 - 1 for c in range(4)] for t in (0, CTX)]

        q_raw = arena[:, 0:2, :].rearrange("p a (b t) -> p (a b) t", b=2)
        k_raw = arena[:, 2:6, :]
        q_ml = arena[:, 6:8, :].rearrange("p a (b t) -> p (a b) t", b=2)
        k_ml, v_ml, v_hg = arena[:, 8:12, :], arena[:, 12:16, :], arena[:, 16:20, :]
        o_gate = arena[:, 20:22, :].rearrange("p a (b t) -> p (a b) t", b=2)
        g_gate = arena[:, 22:24, :].rearrange("p a (b t) -> p (a b) t", b=2)
        q_hg = arena[:, 24:26, :].rearrange("p a (b t) -> p (a b) t", b=2)
        k_hg = [arena[:, 26:30, :], arena[:, 30:34, :]]
        decay = [arena[:, 34:38, :], arena[:, 38:42, :]]
        hg_scores = arena[:, 0:4, :].rearrange("p h (c t) -> p h c t", c=2)
        hg_ctx_scores = arena[:, 4:6, :]
        hg_out = q_hg
        N_FACTORS = 4
        hg_factor = [[h[:, 4 * e + 2 * part:4 * e + 2 * part + 2, :].rearrange("p a (b t) -> p (a b) t", b=2)
                      for part in range(2)] for e in range(N_FACTORS)]
        hg_factors = [h[:, 4 * e:4 * e + 4, :] for e in range(N_FACTORS)]
        ml_decay = [arena[:, 26 + 2 * e:28 + 2 * e, :].rearrange("p a (b t) -> p (a b) t", b=2) for e in range(2)]
        ml_weight = [arena[:, 30 + 2 * e:32 + 2 * e, :].rearrange("p a (b t) -> p (a b) t", b=2) for e in range(2)]
        ml_num = arena[:, 34:38, :]
        ml_out = arena[:, 38:40, :].rearrange("p a (b t) -> p (a b) t", b=2)
        ml_floor, ml_den = arena[0:MH, 40, :], arena[0:MH, 41, :]
        out_squares = arena[:, 26:30, :].rearrange("p a (b t) -> p (a b) t", b=2)
        out_rms, out_rinv = arena[0:2 * MH, 30, 0:LAT], arena[0:2 * MH, 31, 0:LAT]
        gate_tmp = [arena[:, 2 + j, :] for j in range(3)]
        u_rows = [arena[0:MH, 42, :], squares[0:MH, 2, :]]
        m_rows = [x[0:MH, 0, 0:CTX], x[0:MH, 1, 0:CTX]]
        floor_rows = [x[0:MH, 2, 0:CTX], x[0:MH, 3, 0:CTX]]
        u_cols = small[:, 0:2 * 4 * MH]
        bounds = small[:, 40:56].rearrange("p (k d c) -> p k d c", k=2, d=2)
        HALVES_B = [(name, c) for name in PROJECTIONS for c in range(4)]
        LOG_STEPS = (16, 17, 18, 19)
        V_HALVES = [n for n, (name, _) in enumerate(HALVES_B) if name.endswith("_v")]
        WIDE = ("ml_k", "hg_zf", "hg_zb", "ml_v", "hg_v")
        HG_STAGES = ["ctx0", "ctx1"] + list(range(LEVELS + 1)) + ["diagonal"]
        N_TAPS = 2 * 8
        raw_b = [[arena[:, 2 * e + part, 0:LAT] for part in range(2)] for e in range(3)]
        acc_b = [[arena[:, 6 + 2 * e + part, 0:LAT] for part in range(2)] for e in range(3)]
        product_b = [arena[:, 12 + e, 0:LAT] for e in range(3)]

        def later(n):
            return not (isinstance(n, int) and n == 0)

        def spread(j, rows):
            return const("ident", j, 1, rows=rows).broadcast_to([rows, P])

        def lat_valid(direction, c):
            if direction == 0:
                return c * P, LAT
            return 0, (c + 1) * P

        def taps(rows, cols):
            for dy in (-1, 0, 1):
                for dx in (-1, 0, 1):
                    if (dy or dx) and abs(dy) < rows:
                        r = slice(max(0, -dy), rows - max(0, dy)), slice(max(0, dy), rows - max(0, -dy))
                        c = slice(max(0, -dx), cols - max(0, dx)), slice(max(0, dx), cols - max(0, -dx))
                        yield 3 * (dy + 1) + dx + 1, (r[0], c[0]), (r[1], c[1])

        def modulation(name, kc, which):
            if name in ("norm_a", "norm_b"):
                mod, j = mods[2], ("norm_a", "norm_b").index(name)
            else:
                mod, j = mods[int(name[5])], int(name[4]) - 1
            shift = KC * 3 * j + kc
            return scales[:, kc, which:which + 1], mod[:, shift, which:which + 1]

        n_rounds = N_UNITS // RING if until is None else -(-AT["gate", 0] // RING)
        block = stack.enter_context(nc.Block())

        @block.sync
        def _(sp):
            sp.dma_start(params[:, :], params_in).then_inc(loaded, 16)
            sp.dma_start(consts[:, :], consts_in).then_inc(loaded, 16)
            sp.dma_start(x[:, :, :], x_in).then_inc(loaded, 16)
            for s in range(RING):
                sp.dma_start(raw[s][:, :, :], stream[s]).then_inc(unit_full[s], 16)
            with sp.Fori(1, n_rounds) as i:
                for s in range(RING):
                    sp.wait_ge(unit_begun, i * RING + (s + 2 - RING))
                    sp.dma_start(raw[s][:, :, :], stream[i * RING + s]).then_inc(unit_full[s], 16)
            for s in range(RING):
                sp.wait_ge(unit_full[s], 16 * n_rounds)
            if until is None:
                for part in range(2):
                    sp.wait_ge(x_updated, KC * (UPDATED["final2"]) + 4 * (part + 1))
                    sp.dma_start(out[:, 4 * part:4 * part + 4, :], x[:, 4 * part:4 * part + 4, CTX:])\
                        .then_inc(sem("stored"), 16)
                sp.wait_ge(sem("stored"), 32)
            else:
                sp.wait_ge(x_updated, KC * (3 * DEPTH + 1))
                sp.dma_start(out, x[:, :, CTX:]).then_inc(sem("stored"), 16)
                sp.wait_ge(sem("stored"), 16)

        @block.tensor
        def _(pe):
            class At:
                half, side = 0, 0

            def side_sum(at, rounds=0):
                full_wait(pe, at, rounds)
                which = 0 if ORDER[at][0] != "mod" else 1
                for kc in range(KC):
                    g = 32 * (kc % 4)
                    last = nc.tensor.matmul(bank[ROW_BANK][g:g + 32, 0:UNIT], cond[:, which, kc, :], raw[at % RING][:, kc, :],
                                            start=kc < 4, stop=kc >= 4)
                    if kc == 0:
                        last.then_inc(unit_begun, 1)
                last.then_inc(sem("side_sum"), 1)

            def side_turn(side):
                pe.wait_ge(sem("side_row"), side + 1)
                if later(side):
                    pe.wait_ge(sem("side_done"), side)
                for q in range(2):
                    last = nc.tensor.matmul(bank[TURN_BANK][:, 2 * q:2 * q + 2], side_row[:, q * P:(q + 1) * P],
                                            const("sum_rows"), start=True, stop=True)
                last.then_inc(sem("side_turned"), 1)

            def split_product(acc, half, operand, chunks, first_chunk=0, begins_unit=False, start=True, stop=True):
                pe.wait_ge(half_high, half + 1)
                buffer = At.half % 2
                hi, lo = operand
                for kc in range(chunks):
                    for n, v in enumerate((hi, lo)):
                        last = nc.tensor.matmul(acc, w_hi[:, buffer, kc, :], v(first_chunk + kc), start=start and kc == n == 0,
                                                stop=False)
                        if kc == 0 and n == 0:
                            last.then_inc(half_begun, 1)
                        if kc == 0 and n == 1 and begins_unit:
                            last.then_inc(unit_begun, 1)
                pe.wait_ge(half_ready, half + 1)
                for kc in range(chunks):
                    last = nc.tensor.matmul(acc, w_lo[:, buffer, kc, :], hi(first_chunk + kc), start=False,
                                            stop=stop and kc == chunks - 1)
                At.half += 1
                return last

            def joint_product(accs, operands, await_chunk, units=1):
                last = [None, None]
                for step in range(KC + 2):
                    for sub, kc in ((0, step), (1, step - 2)):
                        if not 0 <= kc < KC:
                            continue
                        if kc == 0:
                            pe.wait_ge(half_ready, At.half + sub + 1)
                        if sub == 0:
                            await_chunk("h_high", kc)
                        hi, lo = operands[sub]
                        for n, (w, v) in enumerate(((w_hi, hi), (w_lo, hi), (w_hi, lo))):
                            if sub == 0 and n == 2:
                                await_chunk("h_ready", kc)
                            last[sub] = nc.tensor.matmul(accs[sub], w[:, (At.half + sub) % 2, kc, :], v(kc), start=kc == n == 0,
                                                         stop=kc == KC - 1 and n == 2)
                            if kc == n == 0 and sub < units:
                                last[sub].then_inc(unit_begun, 1)
                            if sub == 1 and step == KC - 1 and n == 0:
                                last[sub].then_inc(half_begun, 1)
                At.half += 2
                return last

            def normed(t0):
                return (lambda kc: h_hi[:, kc, t0:]), (lambda kc: h_lo[:, kc, t0:])

            def norm_sum(name):
                n, t0 = NORM_AT[name], START[name]
                for k, part in enumerate((square_sum, squares[:, 2, :], squares[:, 3, :])):
                    if k == 0:
                        pe.wait_ge(sem("square_added"), (ADDED - 1) * (n + 1))
                    else:
                        pe.wait_ge(sem("square_ready"), KC * n + ADDED + k)
                    for tc in range((T - t0) // P):
                        last = nc.tensor.matmul(bank[SUM_BANK][:, tc:tc + 1], part[:, t0 + tc * P:t0 + (tc + 1) * P], ones[:, 0:1],
                                                start=k == tc == 0, stop=k == 2, skip_group_check=True)
                        if k == tc == 0 and joint(name):
                            last.then_inc(half_begun, 1)
                last.then_inc(sem("norm_summed"), 1)
                if name == "norm10":
                    pe.wait_ge(sem("side_done"), FIRST_SIDES)
                pe.wait_ge(sem("diag_ready"), diags_before(name) + (T - t0) // P)
                nc.tensor.matmul(bank[SPREAD_BANK][:, 0:T - t0], ones, norm_diag[:, 0:T - t0], start=True, stop=True)\
                    .then_inc(sem("rinv_spread"), 1)

            def swiglu(name, norm, norm_after):
                f, t0 = FFNS.index(name), START[norm]
                with_up, with_down = SWIGLU[name]

                def pair(p, j, at, half, side=None, rounds=0, await_chunk=None):
                    pe.wait_ge(sem("pair_moved"), p + (UP * f + 1))
                    full_wait(pe, at, rounds)
                    accs = [bank[PAIR_BANKS[j][gv]][:, 0:T - t0] for gv in range(2)]
                    if await_chunk:
                        _, last = joint_product(accs, [normed(t0)] * 2, await_chunk)
                    else:
                        for gv in range(2):
                            last = split_product(accs[gv], half + gv, normed(t0), KC, begins_unit=gv == 0)
                            if gv == 0 and side is not None:
                                side_turn(side)
                    last.then_inc(sem("pair_ready"), 1)

                def await_chunk(part, kc):
                    pe.wait_ge(sem(part), h_before(norm) + kc + 1)

                pair(0, 0, AT[f"up{name}", 0], At.half, await_chunk=await_chunk)
                half, side = At.half, At.side
                per_round = 2 if with_up else 1
                with pe.Fori(0, (UP - 1) // RING) as i:
                    for j in range(RING):
                        at = AT[f"up{name}", 1 + j]
                        if with_up:
                            side_sum(at - 1, i * per_round)
                        pair(i * RING + (1 + j), (1 + j) % RING, at, i * 2 * RING + (half + 2 * j),
                             i * RING + (side + j) if with_up else None, i * per_round)
                At.half = half + 2 * (UP - 1)
                At.side = side + with_up
                pe.wait_ge(sem("pair_moved"), UP * f + UP + 1)
                down(name, f"ffn{name}", UP * f, with_down, t0, norm_after)

            def down(name, update, hidden_before, sides, t0, norm_after):
                before = KC * BANKED.index(update)
                operand = (lambda kc: hidden_hi[:, kc, t0:]), (lambda kc: hidden_lo[:, kc, t0:])
                for j in range(4 * len(GROUPS)):
                    at = AT[f"down{name}", j]
                    g, pair_of_chunks = j % len(GROUPS), j // len(GROUPS)
                    if j < sides:
                        side_sum(at - 1)
                    full_wait(pe, at)
                    pe.wait_ge(sem("hidden_ready"), hidden_before + min(KC * (g + 1), FC) if j < len(GROUPS) else hidden_before + FC)
                    if j == 3 * len(GROUPS):
                        pe.wait_ge(x_updated, before_updates(update) + 2)
                    for sub in range(2):
                        c = 2 * pair_of_chunks + sub
                        last = split_product(bank[OUT_BANK[c]][:, 0:T - t0], At.half, operand, GROUPS[g], KC * g, sub == 0,
                                             g == 0, g == len(GROUPS) - 1)
                        if g == len(GROUPS) - 1:
                            last.then_inc(sem("acc_ready"), 1)
                        if sub == 0 and j < sides:
                            side_turn(At.side)
                            At.side += 1
                norm_sum(norm_after)

            def out_product(name, update, t0, norm_after, await_chunk=None):
                for j in range(4):
                    full_wait(pe, AT[name, j])
                    if j == 0 and await_chunk:
                        for last in joint_product([bank[OUT_BANK[sub]][:, 0:T - t0] for sub in range(2)], [normed(t0)] * 2, await_chunk):
                            last.then_inc(sem("acc_ready"), 1)
                        continue
                    if j == 3:
                        pe.wait_ge(x_updated, before_updates(update) + 2)
                    for sub in range(2):
                        split_product(bank[OUT_BANK[2 * j + sub]][:, 0:T - t0], At.half, normed(t0), KC, 0, sub == 0)\
                            .then_inc(sem("acc_ready"), 1)
                norm_sum(norm_after)

            def mla_and_conv(i):
                tag, t0 = f"mix{i}", CTX if i == DEPTH - 1 else 0

                def await_chunk(part, kc):
                    pe.wait_ge(sem(part), h_before(f"norm2{i}") + kc + 1)

                def exchange(r):
                    if r == 4:
                        pe.wait_ge(sem(f"roped{tag}"), 2)
                    if r:
                        pe.wait_ge(sem(f"query_moved{tag}"), 2 * r)
                    src = q_heads[0:QK, 8:9, CTX:] if r == 0 else q_heads[0:QK, 2 * r - 2:2 * r, CTX:]
                    width = LAT if r == 0 else 2 * LAT
                    nc.tensor.matmul(bank[ROPE_BANK[r]][0:QK, 0:width], const("perm", 0, QK, rows=QK), src, start=True, stop=True)\
                        .then_inc(sem(f"exchanged{tag}"), 1)

                for n in range(16):
                    if n % 2 == 0:
                        full_wait(pe, AT[f"in{i}", n // 2])
                    if n == 6:
                        pe.wait_ge(sem(f"latent_moved{tag}"), 4)
                    if n >= 8:
                        pe.wait_ge(sem(f"conv_moved{tag}"), n - 7)
                    start = 0 if n in (2, 3) else t0
                    if n < 2:
                        if n == 0:
                            for last in joint_product([bank[IN_BANK[m]][:, 0:T - t0] for m in range(2)], [normed(t0)] * 2, await_chunk):
                                last.then_inc(sem(f"latent_sum{tag}"), 1)
                        continue
                    split_product(bank[IN_BANK[n]][:, 0:T - start], At.half, normed(start), KC, 0, n % 2 == 0)\
                        .then_inc(sem(f"latent_sum{tag}" if n < 4 else f"conv_sum{tag}"), 1)
                    if n == 7:
                        exchange(0)
                        pe.wait_ge(sem(f"latent_square{tag}"), 3)
                        for c in range(2):
                            last = nc.tensor.matmul(bank[0][:, 0:T - t0], ones, squares[:, c, t0:], start=c == 0, stop=c == 1)
                        last.then_inc(sem(f"latent_norm_sum{tag}"), 1)
                        nc.tensor.matmul(bank[1][:, :], ones, squares[:, 2, :], start=True, stop=True)\
                            .then_inc(sem(f"latent_norm_sum{tag}"), 1)
                at_q, at_kv = AT[f"uq{i}", 0], AT[f"ukv{i}", 0]
                full_wait(pe, at_q)
                full_wait(pe, at_kv)
                flat = [raw[at % RING][:, :, :].rearrange("p a b -> p (a b)") for at in (at_q, at_kv)]
                w_q = flat[0][:, 0:2 * HEADS * QK].rearrange("p (k n) -> p k n", k=2)
                w_kv = flat[1][:, 0:HEADS * (NOPE + VD)].rearrange("p (h n) -> p h n", h=HEADS)
                pe.wait_ge(sem(f"latent_ready{tag}"), 3)
                for n in range(20):
                    acc = bank[IN_BANK[8 + n % 4]]
                    if n < 4:
                        pe.wait_ge(sem(f"conv_u{tag}"), n + 1)
                    elif n % 2 and n < 20:
                        pe.wait_ge(sem(f"key_moved{tag}"), (n - 4) // 2 + 1)
                    else:
                        pe.wait_ge(sem(f"query_moved{tag}"), (n - 4) // 2 + 1)
                    hd = n // 2
                    if n >= 16:
                        c = n - 16
                        for q in range(2):
                            last = nc.tensor.matmul(acc[:, q * LAT:(q + 1) * LAT], latent[:, 2, c * P:(c + 1) * P],
                                                    w_kv[:, 4 * q:4 * q + 4, NOPE:], start=True, stop=True, skip_group_check=True)
                            if c == q == 0:
                                last.then_inc(unit_begun, 1)
                    elif n % 2:
                        last = nc.tensor.matmul(acc[0:NOPE, :], w_kv[:, hd, 0:NOPE], latent[:, 2, :], start=True, stop=True)
                    else:
                        for c in range(2):
                            last = nc.tensor.matmul(acc[0:QK, 0:T - t0], w_q[:, c, hd * QK:(hd + 1) * QK],
                                                    latent[:, c, t0:], start=c == 0, stop=c == 1)
                            if n == c == 0:
                                last.then_inc(unit_begun, 1)
                    last.then_inc(sem(f"head_sum{tag}"), 1)
                    if n % 4 == 1 and n > 1:
                        exchange(n // 4)
                pe.wait_ge(sem(f"roped{tag}"), 4)
                pe.wait_ge(sem(f"key_rope{tag}"), 1)
                pe.wait_ge(sem(f"key_moved{tag}"), HEADS)
                pe.wait_ge(sem(f"query_moved{tag}"), HEADS + 4)
                units = attention_units(t0)
                for n in range(len(units) + 3):
                    if n < len(units):
                        hd, tc, keys = units[n]
                        if hd == HEADS - 2:
                            pe.wait_ge(sem(f"roped{tag}"), 5)
                        if n >= 3:
                            pe.wait_ge(sem(f"exp{tag}"), n - 2)
                        nc.tensor.matmul(bank[SCORE_BANKS[n % 3]][:, 0:keys], q_heads[0:QK, hd, tc * P:(tc + 1) * P],
                                         k_heads[0:QK, hd, 0:keys], start=True, stop=True).then_inc(sem(f"score{tag}"), 1)
                    m = n - 2
                    if 0 <= m < len(units):
                        keys = units[m][2]
                        pe.wait_ge(sem(f"prob{tag}"), m + 1)
                        if m >= 2:
                            pe.wait_ge(sem(f"prob_turned_moved{tag}"), m - 1)
                        for c in range(keys // P):
                            last = nc.tensor.transpose(bank[6 + m % 2][:, c * P:(c + 1) * P],
                                                       probs[:, m % 3, c * P:(c + 1) * P], ident)
                        last.then_inc(sem(f"prob_turned{tag}"), 1)
                    m = n - 3
                    if 0 <= m < len(units):
                        hd, tc, keys = units[m]
                        pe.wait_ge(sem(f"prob_turned_moved{tag}"), m + 1)
                        if m == 0:
                            pe.wait_ge(sem(f"roped{tag}"), 5)
                        if m >= 2:
                            pe.wait_ge(sem(f"attended{tag}"), m - 1)
                        for c in range(keys // P):
                            v0 = hd // 2 * P
                            last = nc.tensor.matmul(bank[m % 2][:, 0:P], values[:, c, v0:v0 + P],
                                                    probs_turned[:, m % 2, c * P:(c + 1) * P], start=c == 0,
                                                    stop=c == keys // P - 1)
                        last.then_inc(sem(f"attend_sum{tag}"), 1)
                pe.wait_ge(sem(f"attended{tag}"), len(units))
                pe.wait_ge(sem(f"conv_out{tag}"), 4)
                out_product(f"out{i}", tag, t0, f"norm3{i}")

            def projections():
                def await_chunk(part, kc):
                    pe.wait_ge(sem(part), h_before("norm_a") + kc + 1)

                full_wait(pe, AT["gate", 0])
                full_wait(pe, AT["in", 0])
                gate, first = joint_product([bank[6][:, :], bank[0][:, 0:LAT]], [normed(0), normed(CTX)], await_chunk, 2)
                gate.then_inc(sem("gate_sum"), 1)
                first.then_inc(sem("projection_sum"), 1)

                def turn(n):
                    m = V_HALVES.index(n)
                    pe.wait_ge(sem("projected"), n + 1)
                    if m >= 1:
                        pe.wait_ge(sem("value_moved"), m)
                    for c in range(4):
                        last = nc.tensor.transpose(bank[4][:, c * P:(c + 1) * P], squares[:, m % 2, c * P:(c + 1) * P], ident)
                    last.then_inc(sem("value_turned"), 1)

                for n, (name, c) in enumerate(HALVES_B):
                    if n == 0:
                        continue
                    if n % 2 == 0:
                        full_wait(pe, AT["in", n // 2])
                    if n >= 4:
                        pe.wait_ge(sem("projected"), n - 3)
                    start = 0 if name in WIDE else CTX
                    split_product(bank[n % 4][:, 0:T - start], At.half, normed(start), KC, 0, n % 2 == 0)\
                        .then_inc(sem("projection_sum"), 1)
                    if n - 1 in V_HALVES:
                        turn(n - 1)

            def hgrn():
                for n, stage in enumerate(HG_STAGES):
                    pe.wait_ge(sem("hg_scaled"), n + 1)
                    if stage != "diagonal":
                        pe.wait_ge(sem("hg_query_scaled"), n + 1)
                    q, k = hg_factor[n % N_FACTORS]
                    if stage in ("ctx0", "ctx1"):
                        if n == 0:
                            pe.wait_ge(sem("projected"), len(HALVES_B))
                        for hd in range(MH):
                            for c in range(2):
                                last = nc.tensor.matmul(bank[hd][:, c * LAT:(c + 1) * LAT], k[:, hd, c * P:(c + 1) * P], q[:, hd, :],
                                                        start=n == 0 and c == 0, stop=n == 1, skip_group_check=True)
                    else:
                        if n >= 4:
                            pe.wait_ge(sem("hg_placed"), n - 3)
                        for c in range(2):
                            t = 1 - c if stage == LEVELS else c
                            source = q_hg if stage == "diagonal" else q
                            for hd in range(MH):
                                last = nc.tensor.matmul(bank[4 + 2 * (n % 2) + c][:, hd * P:(hd + 1) * P], k[:, hd, c * P:(c + 1) * P],
                                                        source[:, hd, t * P:(t + 1) * P], start=True, stop=True)
                    last.then_inc(sem("hg_product"), 1)
                pe.wait_ge(sem("hg_placed"), len(HG_STAGES) - 2)
                pe.wait_ge(sem("value_moved"), len(V_HALVES))
                for hd in range(MH):
                    pe.wait_ge(sem("hg_ctx_moved"), hd + 1)
                    for c in range(4):
                        w = hg_ctx_scores[:, hd % 2, c * LAT:(c + 1) * LAT] if c < 2 else hg_scores[:, hd, c - 2, :]
                        last = nc.tensor.matmul(bank[4 + hd][:, 0:LAT], v_hg[:, c, hd * P:(hd + 1) * P], w, start=c == 0, stop=c == 3)
                    last.then_inc(sem("hg_out_sum"), 1)

            def mlstm():
                pe.wait_ge(sem("gate_rows"), 1)
                pe.wait_ge(sem("hg_ctx_moved"), MH)
                for d in range(2):
                    for c in range(4):
                        at = MH * (4 * d + c)
                        last = nc.tensor.matmul(bank[2][:, at:at + MH], u_rows[d][:, c * P:(c + 1) * P], const("ident", 0, MH, rows=MH),
                                                start=True, stop=True)
                last.then_inc(sem("u_turned"), 1)
                pe.wait_ge(sem("u_cols"), 1)
                pe.wait_ge(sem("conv_silu"), 2)
                pe.wait_ge(sem("hg_out_moved"), MH)

                def maxima(n):
                    hd, d = n // 2, n % 2
                    if n >= 2:
                        pe.wait_ge(sem("ml_decayed"), n - 1)
                    nc.tensor.matmul(bank[2 + d][:, 0:LAT], spread(hd, MH), m_rows[d], start=True, stop=True)\
                        .then_inc(sem("ml_max"), 1)

                def scores(hd):
                    if hd:
                        pe.wait_ge(sem("ml_weighted"), 2 * hd)
                    for c in range(4):
                        last = nc.tensor.matmul(bank[c // 2][:, c % 2 * LAT:(c % 2 + 1) * LAT], k_ml[:, hd, c * P:(c + 1) * P],
                                                q_ml[:, hd, :], start=c % 2 == 0, stop=c % 2 == 1, skip_group_check=True)
                    last.then_inc(sem("ml_score"), 1)

                maxima(0)
                maxima(1)
                scores(0)
                for n in range(2 * MH):
                    hd, d = n // 2, n % 2
                    pe.wait_ge(sem("ml_weighted"), n + 1)
                    if n + 2 < 2 * MH:
                        maxima(n + 2)
                    if d == 1 and hd + 1 < MH:
                        scores(hd + 1)
                    if n >= 2:
                        pe.wait_ge(sem("ml_num_moved"), n - 1)
                    for target in range(2):
                        for c in range(4):
                            a, b = (0, LAT) if c < 2 else lat_valid(d, c - 2)
                            w = ml_weight[d][:, c, a:b]
                            if target == 0:
                                last = nc.tensor.matmul(bank[4 + d][:, a:b], v_ml[:, c, hd * P:(hd + 1) * P], w,
                                                        start=c == 0, stop=c == 3, skip_group_check=True)
                            else:
                                last = nc.tensor.matmul(bank[6 + d][0:8, a:b], const("col_of", 8 * hd, 8), w,
                                                        start=c == hd == 0, stop=c == hd == 3, skip_group_check=True)
                    last.then_inc(sem("ml_num_sum"), 1)
                pe.wait_ge(sem("ml_den_ready"), 1)
                for hd in range(MH):
                    nc.tensor.matmul(bank[hd][:, :], spread(hd, MH), ml_den, start=True, stop=True)\
                        .then_inc(sem("ml_den_spread"), 1)

            def head_norms():
                for j in range(8):
                    pe.wait_ge(sem("out_square"), j + 1)
                    last = nc.tensor.matmul(bank[4][0:8, 0:LAT], const("col_of", 8 * j, 8), out_squares[:, j, :],
                                            start=j == 0, stop=j == 7)
                    if j == 0:
                        last.then_inc(half_begun, 1)
                last.then_inc(sem("out_norm_sum"), 1)
                pe.wait_ge(sem("out_rinv"), 1)
                for j in range(8):
                    nc.tensor.matmul(bank[HEAD_NORM_BANK[j // 2]][:, j % 2 * LAT:(j % 2 + 1) * LAT], spread(j, 8), out_rinv,
                                     start=True, stop=True, skip_group_check=True)\
                        .then_inc(sem("out_rinv_spread"), 1)

            def conv_ffn():
                def pair(p, j, at, rounds=0):
                    pe.wait_ge(sem("up_moved"), p + 1)
                    full_wait(pe, at, rounds)
                    for gv in range(2):
                        for kc in range(KC):
                            if gv == 0 and isinstance(p, int):
                                pe.wait_ge(sem("h_ready"), h_before("norm_b") + kc + 1)
                            last = nc.tensor.matmul(bank[PAIR_BANKS[j][gv]][:, 0:LAT], raw[at % RING][:, kc, gv * P:(gv + 1) * P],
                                                    h[:, kc, CTX:], start=kc == 0, stop=kc == KC - 1)
                            if gv == kc == 0:
                                last.then_inc(unit_begun, 1)
                    last.then_inc(sem("up_sum"), 1)

                pe.sem_inc(sem("up_moved"), 3)
                pair(0, 0, AT["up", 0])
                with pe.Fori(0, (UP - 1) // RING) as i:
                    for j in range(RING):
                        pair(i * RING + (1 + j), (1 + j) % RING, AT["up", 1 + j], i)
                pe.wait_ge(sem("up_moved"), UP + 3)
                down("", "ffn_b", UP * len(FFNS), 0, CTX, "final2")

            pe.wait_ge(loaded, 48)
            pe.sem_inc(sem("pair_moved"), 3)
            pe.wait_ge(sem("cond_ready"), 1)
            for j in range(FIRST_SIDES):
                if j:
                    pe.wait_ge(sem("side_row"), j)
                side_sum(j)
                if j:
                    side_turn(j - 1)
            side_turn(FIRST_SIDES - 1)
            At.side = FIRST_SIDES
            norm_sum("norm10")
            for i in range(DEPTH):
                swiglu(f"1{i}", f"norm1{i}", f"norm2{i}")
                mla_and_conv(i)
                swiglu(f"2{i}", f"norm3{i}", f"norm1{i + 1}" if i + 1 < DEPTH else "final1")
            if until is None:
                norm_sum("norm_a")
                projections()
                hgrn()
                mlstm()
                head_norms()
                out_product("out", "mix_b", CTX, "norm_b",
                            lambda part, kc: pe.wait_ge(sem("mixed_b" if part == "h_ready" else "out_high"), kc + 1))
                conv_ffn()

        @block.scalar
        def _(act):
            own = Chain(act, "scalar_own")

            class At:
                half, side = 0, 0

            def convert(at, sub, half=None, rounds=0, chunks=KC):
                half = At.half if half is None else half
                buffer = At.half % 2
                full_wait(act, at, rounds)
                if later(half):
                    act.wait_ge(half_begun, half)
                nc.scalar.activation(w_hi[:, buffer, 0:chunks, :], raw[at % RING][:, 0:chunks, sub * P:(sub + 1) * P], ACT.Copy)\
                    .then_inc(half_high, 1)
                At.half += 1

            def side(number):
                act.wait_ge(sem("side_sum"), number + 1)
                if later(number):
                    act.wait_ge(sem("side_turned"), number)
                nc.scalar.activation(side_row[:, :], bank[ROW_BANK][:, 0:UNIT], ACT.Copy).then_inc(sem("side_row"), 1)

            def square(name, kc):
                n, t0, u = NORM_AT[name], START[name], UPDATED[name]
                if u > 0:
                    act.wait_ge(x_updated, KC * (u - 1) + kc + 1)
                if kc >= 4:
                    act.wait_ge(sem("square_added"), (ADDED - 1) * n + max(1, kc - 4))
                nc.scalar.activation(squares[:, kc % 4, t0:], x[:, kc, t0:], ACT.Square).then_inc(sem("square_ready"), 1)

            def norm(name, squared=0, then=None):
                n, t0 = NORM_AT[name], START[name]
                nc.scalar.activation(small[:, 72:73], const("eps"), ACT.Sqrt)
                for kc in range(squared, KC):
                    square(name, kc)
                act.wait_ge(sem("norm_summed"), n + 1)
                nc.scalar.activation(norm_rms[:, 0:(T - t0) // P], bank[SUM_BANK][:, 0:(T - t0) // P], ACT.Sqrt, bias=const("eps"),
                                     scale=1.0 / D).then_inc(sem("rms_ready"), 1)
                if then is not None:
                    convert(*then)
                if not modulated(name, t0) or name == "norm_b":
                    return
                for kc in range(KC + 1):
                    if t0 == 0 and kc < KC:
                        act.wait_ge(sem("h_scaled"), h_before(name) + kc + 1)
                        s, b = modulation(name, kc, 1)
                        own.mark(nc.scalar.activation(squares[:, kc % 4, 0:CTX], squares[:, kc % 4, 0:CTX], ACT.Identity, bias=b, scale=s))
                    if kc > 0:
                        act.wait_ge(sem("h_lat_ready"), h_before(name) + kc)
                        own.wait(own.n - (1 if kc < KC and t0 == 0 else 0))
                        nc.scalar.activation(h_hi[:, kc - 1, t0:], squares[:, (kc - 1) % 4, t0:], ACT.Copy).then_inc(sem("h_high"), 1)

            def swiglu(name, norm_name, norm_after):
                f, t0 = FFNS.index(name), START[norm_name]
                with_up, with_down = SWIGLU[name]

                def silu(p, j):
                    act.wait_ge(sem("pair_ready"), p + (UP * f + 1))
                    nc.scalar.activation(squares[:, j, t0:], bank[PAIR_BANKS[j][0]][:, 0:T - t0], ACT.Silu).then_inc(sem("silu_ready"), 1)

                def high(p, j):
                    act.wait_ge(sem("pair_moved"), p + (UP * f + 4))
                    nc.scalar.activation(hidden_hi[:, p, t0:], squares[:, j, t0:], ACT.Copy).then_inc(sem("hidden_high"), 1)

                first = AT[f"up{name}", 0]
                per_unit = 2 if with_up else 1
                convert(first + per_unit, 0)
                half = At.half
                with act.Fori(0, (UP - 1) // RING) as i:
                    for j in range(RING):
                        at = first + per_unit * (1 + j)
                        if with_up:
                            side(i * RING + (At.side + j))
                        convert(at, 1, i * 2 * RING + (half + 2 * j), i * per_unit)
                        silu(i * RING + j, j)
                        convert(at + per_unit, 0, i * 2 * RING + (half + 2 * j + 1), i * per_unit)
                        high(i * RING + j, j)
                At.half = half + 2 * (UP - 1)
                At.side += with_up
                last = (UP - 1, (UP - 1) % RING)
                down(name, with_down, norm_after, lambda: silu(*last), lambda: high(*last))

            def down(name, sides, norm_after, *ahead):
                for n in range(2 * 4 * len(GROUPS)):
                    j, sub = n // 2, n % 2
                    if sub == 0 and j < sides:
                        side(At.side)
                        At.side += 1
                    if n + 1 < 2 * 4 * len(GROUPS):
                        at = AT[f"down{name}", (n + 1) // 2]
                        convert(at, (n + 1) % 2, chunks=GROUPS[(n + 1) // 2 % len(GROUPS)])
                    if n < len(ahead):
                        ahead[n]()
                    if n >= 7 and (n - 7) % (2 * len(GROUPS)) < 2:
                        square(norm_after, 2 * ((n - 7) // (2 * len(GROUPS))) + (n - 7) % (2 * len(GROUPS)))

            def out_product(name, norm_after, then=None):
                for n in range(8):
                    if n < 7 and (n or name != "out"):
                        convert(AT[name, (n + 1) // 2], (n + 1) % 2)
                    if n >= 2:
                        square(norm_after, n - 2)
                if then is not None:
                    convert(then, 0)

            def mla_and_conv(i):
                tag, t0 = f"mix{i}", CTX if i == DEPTH - 1 else 0
                for n in range(16):
                    if 0 < n < 15:
                        convert(AT[f"in{i}", (n + 1) // 2], (n + 1) % 2)
                    c = n - 1
                    if 0 <= c < 3:
                        first = t0 if c < 2 else 0
                        act.wait_ge(sem(f"latent_moved{tag}"), c + 1)
                        nc.scalar.activation(squares[:, c, first:], latent[:, c, first:], ACT.Square)\
                            .then_inc(sem(f"latent_square{tag}"), 1)
                    if 4 <= c < 12:
                        act.wait_ge(sem(f"conv_sum{tag}"), c - 3)
                        nc.scalar.activation(conv_in[:, c - 4, t0:], bank[IN_BANK[c]][:, 0:T - t0], ACT.Copy)\
                            .then_inc(sem(f"conv_moved{tag}"), 1)
                    if n == 9:
                        for j, width in ((0, QR), (1, KVR)):
                            first = t0 if j == 0 else 0
                            act.wait_ge(sem(f"latent_norm_sum{tag}"), j + 1)
                            nc.scalar.activation(latent_rms[:, j, first:], bank[j][:, 0:T - first], ACT.Sqrt, bias=const("eps"),
                                                 scale=1.0 / width).then_inc(sem(f"latent_rms{tag}"), 1)
                for n in list(range(0, 16, 2)) + list(range(16, 20)):
                    act.wait_ge(sem(f"head_sum{tag}"), n + 1)
                    acc = bank[IN_BANK[8 + n % 4]]
                    if n < 16:
                        nc.scalar.activation(q_heads[0:QK, n // 2, t0:], acc[0:QK, 0:T - t0], ACT.Copy)\
                            .then_inc(sem(f"query_moved{tag}"), 1)
                    else:
                        nc.scalar.activation(values[:, n - 16, :], acc[:, :], ACT.Copy).then_inc(sem(f"query_moved{tag}"), 1)
                convert(AT[f"out{i}", 0], 0)
                units = attention_units(t0)
                for n in range(len(units) + 2):
                    if n in CONV_STEPS[i]:
                        c = CONV_STEPS[i].index(n)
                        act.wait_ge(sem(f"conv_gated{tag}"), c + 1)
                        nc.scalar.activation(h_hi[:, 4 + c, t0:], squares[:, c, t0:], ACT.Copy).then_inc(sem(f"conv_high{tag}"), 1)
                    if n < len(units):
                        keys = units[n][2]
                        act.wait_ge(sem(f"negmax{tag}"), n + 1)
                        if n >= 3:
                            act.wait_ge(sem(f"prob_turned{tag}"), n - 2)
                        nc.scalar.activation(probs[:, n % 3, 0:keys], bank[SCORE_BANKS[n % 3]][:, 0:keys], ACT.Exp,
                                             bias=small[:, n % 4:n % 4 + 1], scale=SCALE,
                                             accum_out=small[:, 8 + n % 4:9 + n % 4]).then_inc(sem(f"exp{tag}"), 1)
                    m = n - 2
                    if m >= 0:
                        keys = units[m][2]
                        act.wait_ge(sem(f"prob_turned{tag}"), m + 1)
                        if m >= 2:
                            act.wait_ge(sem(f"attend_sum{tag}"), m - 1)
                        nc.scalar.activation(probs_turned[:, m % 2, 0:keys], bank[6 + m % 2][:, 0:keys], ACT.Copy)\
                            .then_inc(sem(f"prob_turned_moved{tag}"), 1)
                out_product(f"out{i}", f"norm3{i}", AT[f"up2{i}", 0])

            def gate_rows():
                act.wait_ge(sem("gate_abs"), 1)
                own.link(nc.scalar.activation(gate_tmp[0], gate_tmp[0], ACT.Exp, scale=-1.0))
                nc.scalar.activation(gate_tmp[0], gate_tmp[0], ACT.Ln, bias=const("ones", 0, 1)).then_inc(sem("gate_log"), 1)

            def move(n):
                name, c = HALVES_B[n]
                act.wait_ge(sem("projection_sum"), n + 1)
                acc = bank[n % 4]
                if name == "ml_q":
                    last = nc.scalar.activation(q_raw[:, c, :], acc[:, 0:LAT], ACT.Copy)
                elif name == "ml_k":
                    last = nc.scalar.activation(k_raw[:, c, :], acc[:, :], ACT.Copy)
                elif name in ("hg_zf", "hg_zb"):
                    d = int(name == "hg_zb")
                    own.mark(nc.scalar.activation(decay[d][:, c, :], acc[:, :], ACT.Sigmoid))
                    last = nc.scalar.activation(k_hg[d][:, c, :], acc[:, :], ACT.Sigmoid, scale=-1.0)
                elif name == "hg_q":
                    last = nc.scalar.activation(q_hg[:, c, :], acc[:, 0:LAT], ACT.Silu)
                elif name.endswith("_v"):
                    m = V_HALVES.index(n)
                    if m >= 2:
                        act.wait_ge(sem("value_turned"), m - 1)
                    last = nc.scalar.activation(squares[:, m % 2, :], acc[:, :], ACT.Copy)
                elif name == "ml_o":
                    last = nc.scalar.activation(o_gate[:, c, :], acc[:, 0:LAT], ACT.Sigmoid)
                else:
                    last = nc.scalar.activation(g_gate[:, c, :], acc[:, 0:LAT], ACT.Silu)
                last.then_inc(sem("projected"), 1)

            def projections():
                act.wait_ge(sem("bound_logits"), 1)
                for k in range(2):
                    own.link(nc.scalar.activation(bounds[:, k, :, :], small[:, 56:64].rearrange("p (d c) -> p d c", d=2), ACT.Sigmoid,
                                                  scale=-1.0 if k else 1.0))
                nc.scalar.activation(small[:, 33:34], bounds[:, 0, 0, 0:1], ACT.Copy).then_inc(sem("bounds"), 1)
                for n in range(len(HALVES_B) + 2):
                    if n + 1 < len(HALVES_B):
                        convert(AT["in", (n + 1) // 2], (n + 1) % 2)
                    if 1 <= n <= len(HALVES_B):
                        move(n - 1)
                    if n - 2 in V_HALVES:
                        m = V_HALVES.index(n - 2)
                        act.wait_ge(sem("value_turned"), m + 1)
                        target, scale = (v_ml, 1.0) if m < 4 else (v_hg, MSCALE)
                        nc.scalar.activation(target[:, :, m % 4 * P:(m % 4 + 1) * P], bank[4][:, :].rearrange("p (c f) -> p c f", c=4),
                                             ACT.Copy, scale=scale).then_inc(sem("value_moved"), 1)
                    if n == LOG_STEPS[-1] + 1:
                        gate_rows()
                    if n in LOG_STEPS:
                        own.wait(own.n)
                        d, pair = divmod(LOG_STEPS.index(n), 2)
                        for cc in (2 * pair, 2 * pair + 1):
                            nc.scalar.activation(decay[d][:, cc, :], decay[d][:, cc, :], ACT.Ln, bias=bounds[:, 0, d, cc:cc + 1],
                                                 scale=bounds[:, 1, d, cc:cc + 1]).then_inc(sem("log_decay"), 1)

            def hgrn():
                for n, stage in enumerate(HG_STAGES):
                    q, k = hg_factor[n % N_FACTORS]
                    if stage in ("ctx0", "ctx1"):
                        d = n
                        act.wait_ge(sem("projected"), len(HALVES_B))
                        act.wait_ge(sem("decay_summed"), 16)
                        own.mark(nc.scalar.activation(q, decay[d][:, :, CTX:], ACT.Exp))
                        for hd in range(MH):
                            total = decay[d][:, hd, CTX - 1:CTX] if d == 0 else decay[d][:, hd, 0:1]
                            last = nc.scalar.activation(k[:, hd, :], decay[d][:, hd, 0:CTX], ACT.Exp, bias=total, scale=-1.0)
                            if hd < MH - 1:
                                own.mark(last)
                        own.wait(own.n)
                        last.then_inc(sem("hg_exp"), 1)
                    elif stage != "diagonal":
                        act.wait_ge(sem("hg_differences"), n - 1)
                        nc.scalar.activation(hg_factors[n % N_FACTORS], hg_factors[n % N_FACTORS], ACT.Exp).then_inc(sem("hg_exp"), 1)
                for what, count in ((q_ml, 4), (k_ml, 8)):
                    act.wait_ge(sem("qk_conv"), count)
                    nc.scalar.activation(what, what, ACT.Silu).then_inc(sem("conv_silu"), 1)
                for hd in range(MH):
                    act.wait_ge(sem("hg_product"), 2)
                    if hd >= 2:
                        act.wait_ge(sem("hg_out_sum"), hd - 1)
                    nc.scalar.activation(hg_ctx_scores[:, hd % 2, :], bank[hd][:, :], ACT.Copy).then_inc(sem("hg_ctx_moved"), 1)
                for hd in range(MH):
                    act.wait_ge(sem("hg_out_sum"), hd + 1)
                    nc.scalar.activation(hg_out[:, hd, :], bank[4 + hd][:, 0:LAT], ACT.Copy).then_inc(sem("hg_out_moved"), 1)

            def mlstm():
                for n in range(2 * MH):
                    hd, d = n // 2, n % 2
                    act.wait_ge(sem("ml_masked"), n + 1)
                    open_chunk = (2, P, LAT) if d == 0 else (3, 0, P)
                    for c, a, b in ((0, 0, LAT), (1, 0, LAT), open_chunk):
                        u = u_cols[:, MH * (4 * d + c) + hd:MH * (4 * d + c) + hd + 1]
                        nc.scalar.activation(ml_decay[d][:, c, a:b], bank[2 + d][:, a:b], ACT.Exp, bias=u, scale=-1.0)\
                            .then_inc(sem("ml_open"), 1)
                    for c in range(2):
                        block_ = ml_decay[d][:, 2 + c, c * P:(c + 1) * P]
                        last = nc.scalar.activation(block_, block_, ACT.Exp)
                        if c == 0:
                            own.mark(last)
                    own.wait(own.n)
                    last.then_inc(sem("ml_decayed"), 1)
                    if n >= 1:
                        num_out(n - 1)
                num_out(2 * MH - 1)
                for d in range(2):
                    nc.scalar.activation(ml_floor[:, d * LAT:(d + 1) * LAT], floor_rows[d], ACT.Exp).then_inc(sem("ml_floor"), 1)

            def num_out(n):
                act.wait_ge(sem("ml_num_sum"), n + 1)
                nc.scalar.activation(ml_num[:, n // 2, n % 2 * LAT:(n % 2 + 1) * LAT], bank[4 + n % 2][:, 0:LAT], ACT.Copy)\
                    .then_inc(sem("ml_num_moved"), 1)

            def head_norms():
                convert(AT["out", 0], 0)
                for j in range(8):
                    if j < MH:
                        act.wait_ge(sem("ml_out"), j + 1)
                    source = ml_out[:, j, :] if j < MH else hg_out[:, j - MH, :]
                    nc.scalar.activation(out_squares[:, j, :], source, ACT.Square).then_inc(sem("out_square"), 1)
                act.wait_ge(sem("out_norm_sum"), 1)
                nc.scalar.activation(out_rms, bank[4][0:8, 0:LAT], ACT.Sqrt, bias=const("eps", rows=8), scale=1.0 / P)\
                    .then_inc(sem("out_rms"), 1)
                convert(AT["out", 0], 1)
                for j in range(8):
                    source = ml_out[:, j, :] if j < MH else hg_out[:, j - MH, :]
                    act.wait_ge(sem("out_gated"), j + 1)
                    nc.scalar.activation(h_hi[:, j, CTX:], source, ACT.Copy).then_inc(sem("out_high"), 1)
                out_product("out", "norm_b")

            def conv_ffn():
                def move(p, j, first=False):
                    act.wait_ge(sem("up_sum"), p + 1)
                    if not first:
                        act.wait_ge(sem("product_b"), p + 1)
                    for part in range(2):
                        source = bank[PAIR_BANKS[j][part]][:, 0:LAT]
                        own_copy = nc.scalar.activation(raw_b[j][part], source, ACT.Copy)
                        own_copy.then_inc(sem("up_copied"), 1)
                        centre = params[:, bass.ds(p + (PARAMS["ffn_conv"][0] + 4 * 2 * FC + part * FC), 1)]
                        last = nc.scalar.activation(acc_b[j][part], source, ACT.Copy, scale=centre)
                        if part == 0:
                            last.then_inc(sem("up_copied"), 1)
                    last.then_inc(sem("up_moved"), 1)

                def gate(p, j):
                    act.wait_ge(sem("tap"), p * N_TAPS + N_TAPS)
                    nc.scalar.activation(acc_b[j][0], acc_b[j][0], ACT.Silu).then_inc(sem("gate_b"), 1)

                def high(p, j):
                    act.wait_ge(sem("product_b"), p + 4)
                    nc.scalar.activation(hidden_hi[:, p, CTX:], product_b[j], ACT.Copy).then_inc(sem("hidden_high"), 1)

                move(0, 0, True)
                move(1, 1, True)
                gate(0, 0)
                move(2, 2, True)
                gate(1, 1)
                with act.Fori(0, (UP - 4) // RING) as i:
                    for j in range(RING):
                        high(i * RING + j, j)
                        move(i * RING + (3 + j), j)
                        gate(i * RING + (2 + j), (2 + j) % RING)
                high(UP - 4, 0)
                move(UP - 1, 0)
                convert(AT["down", 0], 0)
                gate(UP - 2, 2)
                high(UP - 3, 1)
                down("", 0, "final2", lambda: gate(UP - 1, 0), lambda: high(UP - 2, 2), lambda: high(UP - 1, 0))

            act.wait_ge(loaded, 48)
            act.wait_ge(sem("cond_zero"), 1)
            own.mark(nc.scalar.activation(cond[:, 0, :, 0:2], param("c1").rearrange("p (k c) -> p k c", c=2), ACT.Silu))
            last = nc.scalar.activation(cond[:, 1, :, 0:2], param("c2").rearrange("p (k c) -> p k c", c=2), ACT.Silu)
            own.wait(own.n)
            last.then_inc(sem("cond_ready"), 1)
            for j in range(FIRST_SIDES):
                side(j)
                square("norm10", j)
            At.side = FIRST_SIDES
            for i in range(DEPTH):
                if i == 0:
                    convert(AT["up10", 0], 0)
                norm(f"norm1{i}", ADDED if i else FIRST_SIDES, (AT[f"up1{i}", 0], 1))
                swiglu(f"1{i}", f"norm1{i}", f"norm2{i}")
                convert(AT[f"in{i}", 0], 0)
                norm(f"norm2{i}", ADDED, (AT[f"in{i}", 0], 1))
                mla_and_conv(i)
                norm(f"norm3{i}", ADDED, (AT[f"up2{i}", 0], 1))
                swiglu(f"2{i}", f"norm3{i}", f"norm1{i + 1}" if i + 1 < DEPTH else "final1")
                if i + 1 < DEPTH:
                    convert(AT[f"up1{i + 1}", 0], 0)
            norm("final1", ADDED)
            if until is None:
                convert(AT["gate", 0], 0)
                act.wait_ge(sem("ctx2_loaded"), 16)
                norm("norm_a", 0, (AT["in", 0], 0))
                projections()
                hgrn()
                mlstm()
                head_norms()
                norm("norm_b", ADDED)
                conv_ffn()
                norm("final2", ADDED)

        @block.vector
        def _(dve):
            own = Chain(dve, "vector_own")

            class At:
                half, side = 0, 0

            def convert(at, sub, half=None, chunks=KC):
                half = At.half if half is None else half
                buffer = At.half % 2
                dve.wait_ge(half_high, half + 1)
                nc.vector.tensor_tensor(w_lo[:, buffer, 0:chunks, :], raw[at % RING][:, 0:chunks, sub * P:(sub + 1) * P],
                                        w_hi[:, buffer, 0:chunks, :].bitcast(F32), ALU.subtract).then_inc(half_ready, 1)
                At.half += 1

            def side(number, which, unit):
                dve.wait_ge(sem("side_turned"), number + 1)
                first = PARAMS[("b_ada0", "b_ada1", "b_mod")[which]][0]
                nc.vector.tensor_tensor(mods[which][:, bass.ds(unit * 2, 2), :], bank[TURN_BANK][:, 0:4].rearrange("p (n c) -> p n c", c=2),
                                        params[:, bass.ds(unit * 2 + first, 2)].unsqueeze(2).broadcast_to([P, 2, 2]), ALU.add)\
                    .then_inc(sem("side_done"), 1)

            def side_static(number):
                name, unit = SIDE_UNITS[number]
                side(number, list(SIDES).index(name), unit)

            def factors(which, j, weight):
                dve.wait_ge(sem("side_done"), At.side)
                shift = KC * 3 * j
                own.link(nc.vector.scalar_tensor_tensor(scales[:, :, :], mods[which][:, shift + KC:shift + 2 * KC, :], 1.0,
                                                        param(*weight).unsqueeze(2).broadcast_to([P, KC, 2]), ALU.add, ALU.mult))

            def gate_factors(which, j, factor):
                dve.wait_ge(sem("side_done"), At.side)
                first = KC * (3 * j + 2)
                own.link(nc.vector.tensor_scalar(gates[:, :, :], mods[which][:, first:first + KC, :], factor, None, ALU.mult))

            def norm(name, then=None):
                n, t0 = NORM_AT[name], START[name]
                chunks = (T - t0) // P
                dve.wait_ge(sem("rms_ready"), n + 1)
                own.link(nc.vector.reciprocal(norm_rinv[:, 0:chunks], norm_rms[:, 0:chunks]))
                for tc in range(chunks):
                    nc.vector.tensor_scalar(norm_diag[:, tc * P:(tc + 1) * P], ident, norm_rinv[:, tc:tc + 1], None, ALU.mult)\
                        .then_inc(sem("diag_ready"), 1)
                if then is not None:
                    convert(*then)
                dve.wait_ge(sem("rinv_spread"), n + 1)
                factor = bank[SPREAD_BANK][:, 0:T - t0]
                if name.startswith("final"):
                    for kc in range(KC):
                        nc.vector.scalar_tensor_tensor(x[:, kc, t0:], x[:, kc, t0:], param(name, kc, 1), factor,
                                                       ALU.mult, ALU.mult).then_inc(x_updated, 1)
                    return
                split = name != "norm_b"
                before = h_before(name)
                for kc in range(KC + 2):
                    if kc < KC:
                        if split and kc >= 4:
                            dve.wait_ge(sem("h_ready"), before + kc - 3)
                        target = squares[:, kc % 4, t0:] if split else h[:, kc, t0:]
                        nc.vector.tensor_tensor(target, x[:, kc, t0:], factor, ALU.mult).then_inc(sem("h_scaled"), 1)
                    if 1 <= kc <= KC:
                        dve.wait_ge(sem("h_scaled"), before + kc)
                        s, b = modulation(name, kc - 1, 0)
                        target = squares[:, (kc - 1) % 4, CTX:] if split else h[:, kc - 1, CTX:]
                        nc.vector.tensor_scalar(target, target, s, b, ALU.mult, ALU.add)\
                            .then_inc(sem("h_lat_ready" if split else "h_ready"), 1)
                    if split and kc >= 2:
                        c = kc - 2
                        dve.wait_ge(sem("h_high"), before + c + 1)
                        dve.wait_ge(sem("h_lat_ready"), before + c + 1)
                        nc.vector.tensor_tensor(h_lo[:, c, t0:], squares[:, c % 4, t0:], h_hi[:, c, t0:].bitcast(F32), ALU.subtract)\
                            .then_inc(sem("h_ready"), 1)

            def swiglu(name, norm_name):
                f, t0 = FFNS.index(name), START[norm_name]
                with_up, with_down = SWIGLU[name]

                def product(p, j):
                    dve.wait_ge(sem("silu_ready"), p + (UP * f + 1))
                    nc.vector.tensor_tensor(squares[:, j, t0:], squares[:, j, t0:], bank[PAIR_BANKS[j][1]][:, 0:T - t0], ALU.mult)\
                        .then_inc(sem("pair_moved"), 1)

                def rest(p, j):
                    dve.wait_ge(sem("hidden_high"), p + (UP * f + 1))
                    nc.vector.tensor_tensor(hidden_lo[:, p, t0:], squares[:, j, t0:], hidden_hi[:, p, t0:].bitcast(F32), ALU.subtract)\
                        .then_inc(sem("hidden_ready"), 1)

                first = AT[f"up{name}", 0]
                per_unit = 2 if with_up else 1
                convert(first + per_unit, 0)
                half = At.half
                with dve.Fori(0, (UP - 1) // RING) as i:
                    for j in range(RING):
                        at = first + per_unit * (1 + j)
                        convert(at, 1, i * 2 * RING + (half + 2 * j))
                        product(i * RING + j, j)
                        if with_up:
                            tag, unit = SIDE_UNITS[At.side + j]
                            side(i * RING + (At.side + j), list(SIDES).index(tag), i * RING + (unit))
                        convert(at + per_unit, 0, i * 2 * RING + (half + 2 * j + 1))
                        rest(i * RING + j, j)
                At.half = half + 2 * (UP - 1)
                At.side += with_up
                last = (UP - 1, (UP - 1) % RING)
                return (lambda: product(*last)), (lambda: rest(*last))

            def update_chunk(name, kc, t0):
                dve.wait_ge(sem("acc_ready"), KC * BANKED.index(name) + kc + 1)
                acc = bank[OUT_BANK[kc]]
                for start, which in ((0, 1), (CTX, 0)):
                    if start >= t0:
                        last = nc.vector.scalar_tensor_tensor(x[:, kc, start:start + CTX], acc[:, start - t0:start - t0 + CTX],
                                                              gates[:, kc, which:which + 1], x[:, kc, start:start + CTX],
                                                              ALU.mult, ALU.add)
                last.then_inc(x_updated, 1)

            def down(name, update, sides, t0, which, j_gate, factor, ahead=()):
                for n in range(2 * 4 * len(GROUPS)):
                    j, sub = n // 2, n % 2
                    if n + 1 < 2 * 4 * len(GROUPS):
                        convert(AT[f"down{name}", (n + 1) // 2], (n + 1) % 2, chunks=GROUPS[(n + 1) // 2 % len(GROUPS)])
                    if n < len(ahead):
                        ahead[n]()
                    if sub == 0 and j < sides:
                        side_static(At.side)
                        At.side += 1
                    if n == 3:
                        gate_factors(which, j_gate, factor)
                    done = n - 1
                    if done >= 0 and done // 2 % len(GROUPS) == len(GROUPS) - 1:
                        update_chunk(update, 2 * (done // 2 // len(GROUPS)) + done % 2, t0)
                update_chunk(update, KC - 1, t0)

            def out_product(name, update, t0, then=None):
                for n in range(8):
                    if n < 7 and (n or name != "out"):
                        convert(AT[name, (n + 1) // 2], (n + 1) % 2)
                    if n:
                        update_chunk(update, n - 1, t0)
                update_chunk(update, 7, t0)
                if then is not None:
                    convert(then, 0)

            def mla_and_conv(i):
                tag, t0 = f"mix{i}", CTX if i == DEPTH - 1 else 0

                def latent_out(c):
                    first = t0 if c < 2 else 0
                    dve.wait_ge(sem(f"latent_sum{tag}"), c + 1)
                    target = latent[:, c, first:] if c < 3 else q_heads[:, HEADS, :]
                    nc.vector.tensor_copy(target, bank[c][:, 0:T - first]).then_inc(sem(f"latent_moved{tag}"), 1)

                def latent_norm(j):
                    first = t0 if j == 0 else 0
                    dve.wait_ge(sem(f"latent_rms{tag}"), j + 1)
                    own.link(nc.vector.reciprocal(latent_rinv[:, j, first:], latent_rms[:, j, first:]))
                    for c, w in ((0, param(f"q_norm{i}", 0, 1)), (1, param(f"q_norm{i}", 1, 1))) if j == 0 else \
                            ((2, param(f"kv_norm{i}")),):
                        nc.vector.scalar_tensor_tensor(latent[:, c, first:], latent[:, c, first:], w, latent_rinv[:, j, first:],
                                                       ALU.mult, ALU.mult).then_inc(sem(f"latent_ready{tag}"), 1)

                def rope(r):
                    R = slice(NOPE, QK)
                    dve.wait_ge(sem(f"exchanged{tag}"), r + 1)
                    n = 1 if r == 0 else 2
                    f = q_heads[R, HEADS:HEADS + 1, CTX:] if r == 0 else q_heads[R, 2 * r - 2:2 * r, CTX:]
                    cos = const("cos")[R].unsqueeze(1).broadcast_to([ROPE, n, LAT])
                    sin = const("sin")[R].unsqueeze(1).broadcast_to([ROPE, n, LAT])
                    turned = rope_tmp[R, 0:n * LAT].rearrange("p (n t) -> p n t", n=n)
                    own.mark(nc.vector.tensor_tensor(turned, bank[ROPE_BANK[r]][R, 0:n * LAT].rearrange("p (n t) -> p n t", n=n), sin, ALU.mult))
                    own.link(nc.vector.tensor_tensor(f, f, cos, ALU.mult))
                    nc.vector.tensor_tensor(f, f, turned, ALU.add).then_inc(sem(f"roped{tag}"), 1)
                    dve.wait_ge(sem(f"roped{tag}"), r + 1)

                def conv_product(c):
                    dve.wait_ge(sem(f"conv_sum{tag}"), 9 + c)
                    dve.wait_ge(sem(f"conv_moved{tag}"), 5 + c)
                    nc.vector.tensor_tensor(conv_in[:, 4 + c, t0:], conv_in[:, 4 + c, t0:], bank[IN_BANK[12 + c]][:, 0:T - t0], ALU.mult)\
                        .then_inc(sem(f"conv_u{tag}"), 1)

                for n in range(17):
                    if 0 < n < 15:
                        convert(AT[f"in{i}", (n + 1) // 2], (n + 1) % 2)
                    if 1 <= n <= 4:
                        latent_out(n - 1)
                    if n == 9:
                        rope(0)
                    if n in (10, 12):
                        latent_norm((n - 10) // 2)
                    if n >= 13:
                        conv_product(n - 13)

                for hd in range(HEADS):
                    dve.wait_ge(sem(f"head_sum{tag}"), 2 * hd + 2)
                    nc.vector.tensor_copy(k_heads[0:NOPE, hd, :], bank[IN_BANK[8 + (2 * hd + 1) % 4]][0:NOPE, :])\
                        .then_inc(sem(f"key_moved{tag}"), 1)
                    if hd % 2 == 0 and hd:
                        rope(hd // 2)
                rope(4)
                convert(AT[f"out{i}", 0], 0)
                units = attention_units(t0)
                for n in range(len(units) + 3):
                    if n < len(units):
                        keys = units[n][2]
                        dve.wait_ge(sem(f"score{tag}"), n + 1)
                        own.link(nc.vector.tensor_reduce(small[:, 24 + n % 4:25 + n % 4], bank[SCORE_BANKS[n % 3]][:, 0:keys],
                                                         axis=AX_X, op=ALU.max))
                        nc.vector.tensor_scalar(small[:, n % 4:n % 4 + 1], small[:, 24 + n % 4:25 + n % 4], -SCALE, None, ALU.mult)\
                            .then_inc(sem(f"negmax{tag}"), 1)
                    m = n - 1
                    if 0 <= m < len(units):
                        keys = units[m][2]
                        dve.wait_ge(sem(f"exp{tag}"), m + 1)
                        own.link(nc.vector.reciprocal(small[:, 16 + m % 4:17 + m % 4], small[:, 8 + m % 4:9 + m % 4]))
                        nc.vector.tensor_scalar(probs[:, m % 3, 0:keys], probs[:, m % 3, 0:keys], small[:, 16 + m % 4:17 + m % 4],
                                                None, ALU.mult).then_inc(sem(f"prob{tag}"), 1)
                    m = n - 3
                    if 0 <= m < len(units):
                        hd, tc, _ = units[m]
                        half = slice(VD * (hd % 2), VD * (hd % 2) + VD)
                        dve.wait_ge(sem(f"attend_sum{tag}"), m + 1)
                        high = h_hi[half, hd // 2, tc * P:(tc + 1) * P]
                        own.link(nc.vector.tensor_copy(high, bank[m % 2][half, 0:P]))
                        nc.vector.tensor_tensor(h_lo[half, hd // 2, tc * P:(tc + 1) * P], bank[m % 2][half, 0:P], high.bitcast(F32),
                                                ALU.subtract).then_inc(sem(f"attended{tag}"), 1)
                    if n in CONV_STEPS[i]:
                        c = CONV_STEPS[i].index(n)
                        dve.wait_ge(sem(f"conv_high{tag}"), c + 1)
                        nc.vector.tensor_tensor(h_lo[:, 4 + c, t0:], squares[:, c, t0:], h_hi[:, 4 + c, t0:].bitcast(F32), ALU.subtract)\
                            .then_inc(sem(f"conv_out{tag}"), 1)

            def bounds_of_decay():
                logits = param("lb").rearrange("p (d l c) -> p d l c", d=2, l=2)
                nc.vector.tensor_tensor(small[:, 56:64].rearrange("p (d c) -> p d c", d=2), logits[:, :, 0, :], logits[:, :, 1, :],
                                        ALU.subtract).then_inc(sem("bound_logits"), 1)

            def segments(a, backwards):
                v = a.rearrange("p (s t) -> p s t", s=2)
                return v[:, :, ::-1] if backwards else v

            def gate_rows(part):
                g, log_f, forward, backward = squares[:, 3, :], gate_tmp[0], gate_tmp[1], gate_tmp[2]
                sums = [forward[0:MH, :], backward[0:MH, :]]
                u_back = arena[0:MH, 43, :]
                maxima = [rms[0:MH, :], rinv[0:MH, :]]
                if part == 0:
                    dve.wait_ge(sem("qk_conv"), 8)
                    nc.vector.scalar_tensor_tensor(log_f, g, -1.0, g, ALU.mult, ALU.max).then_inc(sem("gate_abs"), 1)
                elif part == 1:
                    dve.wait_ge(sem("gate_log"), 1)
                    own.link(nc.vector.scalar_tensor_tensor(log_f, g, 0.0, log_f, ALU.min, ALU.subtract))
                elif part == 2:
                    own.mark(nc.vector.tensor_copy(sums[0], log_f[32:32 + MH, :]))
                    own.mark(nc.vector.tensor_copy(segments(sums[1], False), segments(log_f[96:96 + MH, :], True)))
                    own.link(nc.vector.tensor_copy(segments(u_back, False), segments(g[64:64 + MH, :], True)))
                elif part == 3:
                    for d in range(2):
                        own.link(nc.vector.tensor_tensor_scan(sums[d], sums[d], sums[d], 0.0, ALU.add, ALU.bypass))
                elif part == 4:
                    own.mark(nc.vector.tensor_tensor(u_rows[0], g[0:MH, :], sums[0], ALU.subtract))
                    own.link(nc.vector.tensor_tensor(u_back, u_back, sums[1], ALU.subtract))
                elif part == 5:
                    for d, u in enumerate((u_rows[0], u_back)):
                        own.link(nc.vector.tensor_tensor_scan(maxima[d], u, u, 0.0, ALU.max, ALU.bypass))
                elif part == 6:
                    for d in range(2):
                        own.link(nc.vector.scalar_tensor_tensor(sums[d][:, CTX:], maxima[d][:, CTX:], -1.0, sums[d][:, CTX:],
                                                                ALU.mult, ALU.subtract))
                else:
                    own.mark(nc.vector.tensor_copy(segments(u_rows[1], False), segments(u_back, True)))
                    for a, rows in ((maxima, m_rows), (sums, floor_rows)):
                        own.mark(nc.vector.tensor_copy(rows[0], a[0][:, CTX:]))
                        own.mark(nc.vector.tensor_copy(rows[1], a[1][:, CTX:][:, ::-1]))
                    own.wait(own.n)
                    nc.vector.memset(small[:, 39:40], 0.0).then_inc(sem("gate_rows"), 1)

            def qk_conv(group, c):
                dve.wait_ge(sem("projected"), 4 * group + c + 1)
                windows = [(q_raw[:, c, :], q_ml[:, c, :], ROWS, GRID)] if group == 0 else \
                    [(k_raw[:, c, CTX:], k_ml[:, c, CTX:], ROWS, GRID), (k_raw[:, c, 0:CTX], k_ml[:, c, 0:CTX], 1, CTX)]
                for source, target, rows, cols in windows:
                    source, target = (a.rearrange("p (r c) -> p r c", c=cols) for a in (source, target))
                    own.link(nc.vector.tensor_scalar(target, source, param("qk_conv", KC * 4 + 4 * group + c, 1), None, ALU.mult))
                    for tap, (ro, co), (ri, ci) in taps(rows, cols):
                        to = target[:, ro, co]
                        own.link(nc.vector.scalar_tensor_tensor(to, source[:, ri, ci], param("qk_conv", KC * tap + 4 * group + c, 1), to,
                                                                ALU.mult, ALU.add))
                dve.sem_inc(sem("qk_conv"), 1)

            def decay_sums(d, c):
                dve.wait_ge(sem("bounds"), 1)
                dve.wait_ge(sem("projected"), 16)
                own.mark(nc.vector.tensor_scalar(k_hg[d][:, c, :], k_hg[d][:, c, :], bounds[:, 1, d, c:c + 1], None, ALU.mult))
                dve.wait_ge(sem("log_decay"), 4 * d + c + 1)
                for s in range(2):
                    part = decay[d][:, c, s * CTX:(s + 1) * CTX]
                    part = part[:, ::-1] if d else part
                    nc.vector.tensor_tensor_scan(part, part, part, 0.0, ALU.add, ALU.bypass).then_inc(sem("decay_summed"), 1)

            def projections():
                dve.wait_ge(sem("gate_sum"), 1)
                own.link(nc.vector.tensor_scalar(squares[:, 3, :], bank[6][:, :], param("gate_b"), None, ALU.add))
                for n in range(len(HALVES_B) - 1):
                    convert(AT["in", (n + 1) // 2], (n + 1) % 2)
                    if 8 <= n < 16:
                        qk_conv((n - 8) // 4, n % 4)
                    if n == 18:
                        gate_rows(0)
                    if 20 <= n < 28:
                        decay_sums((n - 20) // 4, n % 4)
                    if 21 <= n < 28:
                        gate_rows(n - 20)

            def hgrn():
                dve.wait_ge(sem("decay_summed"), 16)
                dve.wait_ge(sem("qk_conv"), 8)
                own.wait(own.n)

                def blocks(a, size):
                    return a.rearrange("p h (n two b) -> p h n two b", two=2, b=size)

                def differences(n):
                    stage = HG_STAGES[n]
                    if n >= N_FACTORS:
                        dve.wait_ge(sem("hg_product"), n - N_FACTORS + 1)
                    if stage == "diagonal":
                        return
                    size = 1 << stage
                    q, k = (blocks(f, size) for f in hg_factor[n % N_FACTORS])
                    f, b = (blocks(decay[d][:, :, CTX:], size) for d in range(2))
                    shape = [P, MH, LAT // (2 * size), size]
                    last_left = f[:, :, :, 0, size - 1:size].broadcast_to(shape)
                    first_right = b[:, :, :, 1, 0:1].broadcast_to(shape)
                    last = None
                    for out_, a, c in ((q[:, :, :, 1, :], f[:, :, :, 1, :], last_left), (k[:, :, :, 0, :], last_left, f[:, :, :, 0, :]),
                                       (q[:, :, :, 0, :], b[:, :, :, 0, :], first_right), (k[:, :, :, 1, :], first_right, b[:, :, :, 1, :])):
                        if last is not None:
                            own.mark(last)
                        last = nc.vector.tensor_tensor(out_, a, c, ALU.subtract)
                    last.then_inc(sem("hg_differences"), 1)

                def scale(n):
                    stage = HG_STAGES[n]
                    q, k = hg_factor[n % N_FACTORS]
                    if stage == "diagonal":
                        nc.vector.tensor_tensor(k, k_hg[0][:, :, CTX:], k_hg[1][:, :, CTX:], ALU.add).then_inc(sem("hg_scaled"), 1)
                        return
                    dve.wait_ge(sem("hg_exp"), n + 1)
                    if stage in ("ctx0", "ctx1"):
                        last = nc.vector.tensor_tensor(k, k, k_hg[n][:, :, 0:CTX], ALU.mult)
                    else:
                        kb = blocks(k, 1 << stage)
                        for d in range(2):
                            source = blocks(k_hg[d][:, :, CTX:], 1 << stage)
                            last = nc.vector.tensor_tensor(kb[:, :, :, d, :], kb[:, :, :, d, :], source[:, :, :, d, :], ALU.mult)
                            if d == 0:
                                own.mark(last)
                    own.wait(own.n)
                    last.then_inc(sem("hg_scaled"), 1)

                def place(n):
                    stage = HG_STAGES[n]
                    dve.wait_ge(sem("hg_product"), n + 1)
                    for c in range(2):
                        scores = bank[4 + 2 * (n % 2) + c][:, :].rearrange("p (h t) -> p h t", h=MH)
                        if stage == LEVELS:
                            last = nc.vector.tensor_copy(hg_scores[:, :, c, (1 - c) * P:(2 - c) * P], scores)
                        else:
                            level = LEVELS if stage == "diagonal" else stage
                            mask = const("level", level * P, P).bitcast(U32).unsqueeze(1).broadcast_to([P, MH, P])
                            last = nc.vector.copy_predicated(hg_scores[:, :, c, c * P:(c + 1) * P], mask, scores)
                        if c == 0:
                            own.mark(last)
                    own.wait(own.n)
                    last.then_inc(sem("hg_placed"), 1)

                dve.wait_ge(sem("projected"), len(HALVES_B))
                own.link(nc.vector.memset(hg_scores, 0.0))
                scale(0)
                differences(2)
                scale(1)
                for n in range(3, len(HG_STAGES)):
                    differences(n)
                    scale(n - 1)
                    if n >= 4:
                        place(n - 2)
                place(len(HG_STAGES) - 2)
                scale(len(HG_STAGES) - 1)
                place(len(HG_STAGES) - 1)

            def mlstm():
                dve.wait_ge(sem("u_turned"), 1)
                nc.vector.tensor_copy(u_cols, bank[2][:, 0:2 * 4 * MH]).then_inc(sem("u_cols"), 1)
                dve.wait_ge(sem("u_cols"), 1)

                def mask(n):
                    hd, d = n // 2, n % 2
                    dve.wait_ge(sem("ml_max"), n + 1)
                    for c in range(2):
                        u = u_cols[:, MH * (4 * d + 2 + c) + hd:MH * (4 * d + 2 + c) + hd + 1]
                        last = nc.vector.scalar_tensor_tensor(ml_decay[d][:, 2 + c, c * P:(c + 1) * P], const("causal", d * P, P), u,
                                                              bank[2 + d][:, c * P:(c + 1) * P], ALU.add, ALU.subtract)
                        if c == 0:
                            own.mark(last)
                    own.wait(own.n)
                    last.then_inc(sem("ml_masked"), 1)

                def weigh(n):
                    hd, d = n // 2, n % 2
                    dve.wait_ge(sem("ml_score"), hd + 1)
                    dve.wait_ge(sem("ml_decayed"), n + 1)
                    if n >= 2:
                        dve.wait_ge(sem("ml_num_sum"), n - 1)
                    own.mark(nc.vector.scalar_tensor_tensor(ml_weight[d][:, 0:2, :], bank[0][:, :].rearrange("p (c t) -> p c t", c=2), MSCALE,
                                                            ml_decay[d][:, 0:2, :], ALU.mult, ALU.mult))
                    for c in range(2):
                        a, b = lat_valid(d, c)
                        last = nc.vector.scalar_tensor_tensor(ml_weight[d][:, 2 + c, a:b], bank[1][:, c * LAT + a:c * LAT + b], MSCALE,
                                                              ml_decay[d][:, 2 + c, a:b], ALU.mult, ALU.mult)
                        if c == 0:
                            own.mark(last)
                    own.wait(own.n)
                    last.then_inc(sem("ml_weighted"), 1)

                mask(0)
                for n in range(2 * MH):
                    if n + 1 < 2 * MH:
                        mask(n + 1)
                    weigh(n)
                dve.wait_ge(sem("ml_num_sum"), 2 * MH)
                for d in range(2):
                    own.mark(nc.vector.tensor_copy(ml_den[:, d * LAT:(d + 1) * LAT], bank[6 + d][0:MH, 0:LAT]))
                own.wait(own.n)
                own.link(nc.vector.scalar_tensor_tensor(ml_den, ml_den, -1.0, ml_den, ALU.mult, ALU.max))
                dve.wait_ge(sem("ml_floor"), 2)
                own.link(nc.vector.tensor_tensor(ml_den, ml_den, ml_floor, ALU.max))
                nc.vector.reciprocal(ml_den, ml_den).then_inc(sem("ml_den_ready"), 1)
                dve.wait_ge(sem("ml_num_moved"), 2 * MH)
                for hd in range(MH):
                    dve.wait_ge(sem("ml_den_spread"), hd + 1)
                    own.link(nc.vector.tensor_tensor(ml_num[:, hd, :], ml_num[:, hd, :], bank[hd][:, :], ALU.mult))
                    nc.vector.tensor_tensor(ml_out[:, hd, :], ml_num[:, hd, 0:LAT], ml_num[:, hd, LAT:], ALU.add).then_inc(sem("ml_out"), 1)

            def head_norms():
                convert(AT["out", 0], 0)
                dve.wait_ge(sem("out_rms"), 1)
                nc.vector.reciprocal(out_rinv, out_rms).then_inc(sem("out_rinv"), 1)
                convert(AT["out", 0], 1)
                for j in range(8):
                    source = ml_out[:, j, :] if j < MH else hg_out[:, j - MH, :]
                    gate = o_gate[:, j, :] if j < MH else g_gate[:, j - MH, :]
                    weight = param("ml_norm", j, 1) if j < MH else param("hg_norm", j - MH, 1)
                    dve.wait_ge(sem("out_rinv_spread"), 8 if j % 2 == 0 else j + 1)
                    own.link(nc.vector.scalar_tensor_tensor(source, source, weight, bank[HEAD_NORM_BANK[j // 2]][:, j % 2 * LAT:(j % 2 + 1) * LAT],
                                                            ALU.mult, ALU.mult))
                    nc.vector.tensor_tensor(source, source, gate, ALU.mult).then_inc(sem("out_gated"), 1)
                    if j:
                        out_rest(j - 1)
                out_rest(7)

            def out_rest(j):
                source = ml_out[:, j, :] if j < MH else hg_out[:, j - MH, :]
                dve.wait_ge(sem("out_high"), j + 1)
                nc.vector.tensor_tensor(h_lo[:, j, CTX:], source, h_hi[:, j, CTX:].bitcast(F32), ALU.subtract).then_inc(sem("mixed_b"), 1)

            def conv_ffn():
                def convolve(p, j):
                    k = 0
                    dve.wait_ge(sem("up_moved"), p + 4)
                    for tap, (ro, co), (ri, ci) in taps(ROWS, GRID):
                        for part in range(2):
                            source = raw_b[j][part].rearrange("p (r c) -> p r c", c=GRID)
                            acc = acc_b[j][part].rearrange("p (r c) -> p r c", c=GRID)
                            w = params[:, bass.ds(p + (PARAMS["ffn_conv"][0] + tap * 2 * FC + part * FC), 1)]
                            if k >= 2:
                                dve.wait_ge(sem("tap"), p * N_TAPS + (k - 1))
                            nc.vector.scalar_tensor_tensor(acc[:, ro, co], source[:, ri, ci], w, acc[:, ro, co], ALU.mult, ALU.add)\
                                .then_inc(sem("tap"), 1)
                            k += 1

                def product(p, j):
                    dve.wait_ge(sem("tap"), p * N_TAPS + N_TAPS)
                    dve.wait_ge(sem("gate_b"), p + 1)
                    dve.wait_ge(sem("hidden_ready"), p + (UP * len(FFNS) - 2))
                    nc.vector.tensor_tensor(product_b[j], acc_b[j][0], acc_b[j][1], ALU.mult).then_inc(sem("product_b"), 1)

                def rest(p, j):
                    dve.wait_ge(sem("product_b"), p + 4)
                    dve.wait_ge(sem("hidden_high"), p + (UP * len(FFNS) + 1))
                    nc.vector.tensor_tensor(hidden_lo[:, p, CTX:], product_b[j], hidden_hi[:, p, CTX:].bitcast(F32), ALU.subtract)\
                        .then_inc(sem("hidden_ready"), 1)

                dve.sem_inc(sem("product_b"), 3)
                convolve(0, 0)
                convolve(1, 1)
                product(0, 0)
                with dve.Fori(0, (UP - 4) // RING) as i:
                    for j in range(RING):
                        convolve(i * RING + (2 + j), (2 + j) % RING)
                        product(i * RING + (1 + j), (1 + j) % RING)
                        rest(i * RING + j, j)
                for p in range(UP - 4, UP - 2):
                    if p == UP - 3:
                        convert(AT["down", 0], 0)
                    convolve(p + 2, (p + 2) % RING)
                    product(p + 1, (p + 1) % RING)
                    rest(p, p % RING)
                return (lambda: product(UP - 1, 0)), (lambda: rest(UP - 2, 2)), (lambda: rest(UP - 1, 0))

            dve.wait_ge(loaded, 48)
            nc.vector.memset(cond[:, :, :, :], 0.0).then_inc(sem("cond_zero"), 1)
            for j in range(FIRST_SIDES):
                side_static(j)
            At.side = FIRST_SIDES
            for i in range(DEPTH):
                t0 = CTX if i == DEPTH - 1 else 0
                if i == 0:
                    convert(AT["up10", 0], 0)
                factors(i, 0, (f"norm{i}", 0, KC))
                norm(f"norm1{i}", (AT[f"up1{i}", 0], 1))
                down(f"1{i}", f"ffn1{i}", SWIGLU[f"1{i}"][1], 0, i, 0, 0.5, swiglu(f"1{i}", f"norm1{i}"))
                convert(AT[f"in{i}", 0], 0)
                factors(i, 1, (f"norm{i}", KC, KC))
                norm(f"norm2{i}", (AT[f"in{i}", 0], 1))
                mla_and_conv(i)
                gate_factors(i, 1, 1.0)
                out_product(f"out{i}", f"mix{i}", t0, AT[f"up2{i}", 0])
                factors(i, 2, (f"norm{i}", 2 * KC, KC))
                norm(f"norm3{i}", (AT[f"up2{i}", 0], 1))
                down(f"2{i}", f"ffn2{i}", SWIGLU[f"2{i}"][1], t0, i, 2, 0.5, swiglu(f"2{i}", f"norm3{i}"))
                if i + 1 < DEPTH:
                    convert(AT[f"up1{i + 1}", 0], 0)
            norm("final1")
            if until is None:
                convert(AT["gate", 0], 0)
                factors(2, 0, ("norm_a",))
                dve.wait_ge(sem("ctx2_loaded"), 16)
                norm("norm_a", (AT["in", 0], 0))
                bounds_of_decay()
                projections()
                hgrn()
                mlstm()
                head_norms()
                gate_factors(2, 0, 1.0)
                out_product("out", "mix_b", CTX)
                factors(2, 1, ("norm_b",))
                norm("norm_b")
                down("", "ffn_b", 0, CTX, 2, 1, 1.0, conv_ffn())
                norm("final2")

        @block.gpsimd
        def _(pool):
            own = Chain(pool, "gpsimd_own")

            def add_squares(name):
                n, t0 = NORM_AT[name], START[name]
                if n:
                    pool.wait_ge(sem("norm_summed"), n)
                for kc in range(1, ADDED):
                    pool.wait_ge(sem("square_ready"), KC * n + kc + 1)
                    if kc > 1:
                        pool.wait_ge(sem("square_added"), (ADDED - 1) * n + kc - 1)
                    first = squares[:, 0, t0:] if kc == 1 else square_sum[:, t0:]
                    nc.gpsimd.tensor_tensor(square_sum[:, t0:], first, squares[:, kc % 4, t0:], ALU.add).then_inc(sem("square_added"), 1)

            add_squares("norm10")
            for i in range(DEPTH):
                tag, t0 = f"mix{i}", CTX if i == DEPTH - 1 else 0
                add_squares(f"norm2{i}")
                if i == DEPTH - 1 and until is None:
                    pool.wait_ge(sem("h_ready"), h_before(f"norm2{i}") + KC)
                    pool.dma_start(x[:, :, 0:CTX], ctx2_in).then_inc(sem("ctx2_loaded"), 16)

                def conv(c):
                    segments = (T - t0) // CTX
                    u = conv_in[:, 4 + c, t0:].rearrange("p (s t) -> p s t", s=segments)
                    gb = conv_in[:, c, t0:].rearrange("p (s t) -> p s t", s=segments)
                    y = squares[:, c, t0:].rearrange("p (s t) -> p s t", s=segments)
                    term = arena[:, 43, t0:].rearrange("p (s t) -> p s t", s=segments)
                    w = lambda tap: param(f"conv{i}", 4 * tap + c, 1)
                    pool.wait_ge(sem(f"conv_u{tag}"), 4)
                    own.link(nc.gpsimd.tensor_scalar(y, u, w(1), None, ALU.mult))
                    for tap, to, source in ((0, slice(1, None), slice(0, -1)), (2, slice(0, -1), slice(1, None))):
                        own.link(nc.gpsimd.tensor_scalar(term, u, w(tap), None, ALU.mult))
                        own.link(nc.gpsimd.tensor_tensor(y[:, :, to], y[:, :, to], term[:, :, source], ALU.add))
                    nc.gpsimd.tensor_tensor(y, y, gb, ALU.mult).then_inc(sem(f"conv_gated{tag}"), 1)

                pool.wait_ge(sem(f"roped{tag}"), 1)
                nc.gpsimd.tensor_copy(k_heads[NOPE:QK, :, :], q_heads[NOPE:QK, HEADS, :].unsqueeze(1).broadcast_to([ROPE, HEADS, T]))\
                    .then_inc(sem(f"key_rope{tag}"), 1)
                pool.wait_ge(sem(f"key_rope{tag}"), 1)
                for c in range(4):
                    conv(c)
                add_squares(f"norm3{i}")
                add_squares(f"norm1{i + 1}" if i + 1 < DEPTH else "final1")
            if until is None:
                pool.wait_ge(sem("ctx2_loaded"), 16)
                add_squares("norm_a")
                for n in range(len(HG_STAGES) - 1):
                    pool.wait_ge(sem("hg_exp"), n + 1)
                    q = hg_factor[n % N_FACTORS][0]
                    nc.gpsimd.tensor_tensor(q, q, q_hg, ALU.mult).then_inc(sem("hg_query_scaled"), 1)
                add_squares("norm_b")
                add_squares("final2")




def columns(v):
    v = np.asarray(v)
    return v.reshape(-1, P).T


def lay_params(a):
    out = np.zeros((P, N_PARAMS), np.float32)

    def put(name, value, rows=P):
        first, width = PARAMS[name]
        out[0:rows, first:first + value.shape[1]] = value

    for i in range(DEPTH):
        put(f"norm{i}", columns(a["norm_w"][i].reshape(-1)))
        put(f"b_ada{i}", columns(a["b_ada"][i]))
        put(f"q_norm{i}", columns(a["q_norm_w"][i]))
        put(f"kv_norm{i}", columns(a["kv_norm_w"][i]))
        put(f"conv{i}", columns(a["conv_w"][i].reshape(-1)))
    put("final1", columns(a["final_norm_w"]))
    put("c1", np.stack([columns(a["c"][0]), columns(a["c_ctx"])], 2).reshape(P, -1))
    put("c2", np.stack([columns(a["c_2"][0]), columns(a["c_ctx_2"])], 2).reshape(P, -1))
    put("b_mod", columns(a["b_mod_2"][0]))
    put("norm_a", columns(a["norm1_w_2"][0]))
    put("norm_b", columns(a["norm2_w_2"][0]))
    gate_b = np.zeros((P, 1), np.float32)
    for j in range(4):
        gate_b[32 * j:32 * j + MH, 0] = a["mlstm_gate_b_2"][0, MH * j:MH * (j + 1)]
    put("gate_b", gate_b)
    put("qk_conv", columns(a["mlstm_conv_w_2"][0].reshape(-1)))
    put("ml_norm", columns(a["mlstm_norm_w_2"][0]))
    put("lb", columns(a["hgrn_lb_logits_2"].reshape(-1)))
    put("hg_norm", columns(a["hgrn_norm_w_2"][0]))
    put("ffn_conv", columns(a["ffn_conv_w_2"][0].reshape(-1)))
    put("final2", columns(a["final_norm_w_2"]))
    return out


def lay_consts():
    out = np.zeros((P, N_CONSTS), np.float32)

    def put(name, value, first_row=0):
        first, _ = CONSTS[name]
        out[first_row:first_row + value.shape[0], first:first + value.shape[1]] = value

    put("ident", np.eye(P, dtype=np.float32))
    put("ones", np.ones((P, P), np.float32))
    put("sum_rows", (np.arange(P)[:, None] % 32 == np.arange(2)[None, :]).astype(np.float32))
    put("eps", np.full((P, 1), EPS, np.float32))
    axis, half = ROPE // 2, ROPE // 4
    inv = np.float32(10000.0) ** (-np.arange(0, axis, 2, dtype=np.float32) / np.float32(axis))
    t = np.arange(LAT)
    angle = np.concatenate([np.outer(inv, (t // GRID).astype(np.float32))] * 2
                           + [np.outer(inv, (t % GRID).astype(np.float32))] * 2)
    put("cos", np.cos(angle), NOPE)
    put("sin", np.sin(angle), NOPE)
    perm = np.zeros((P, P), np.float32)
    for d in range(ROPE):
        low = d % axis < half
        perm[NOPE + (d + half if low else d - half), NOPE + d] = -1.0 if low else 1.0
    put("perm", perm)
    s, t = np.arange(P)[:, None], np.arange(P)[None, :]
    for j in range(LEVELS):
        put_at = (s >> (j + 1) == t >> (j + 1)) & (s >> j != t >> j)
        out[:, CONSTS["level"][0] + j * P:CONSTS["level"][0] + (j + 1) * P] = put_at
    out[:, CONSTS["level"][0] + LEVELS * P:CONSTS["level"][0] + (LEVELS + 1) * P] = s == t
    put("causal", np.concatenate([np.where(s <= t, 0.0, NEG), np.where(s >= t, 0.0, NEG)], 1).astype(np.float32))
    for j in range(8):
        out[:, CONSTS["col_of"][0] + 8 * j + j] = 1.0
    return out


def lay_stream(a):
    out = np.zeros((N_UNITS, P, KC, UNIT), np.float32)

    def rows(w):
        return w.reshape(-1, P, w.shape[1]).transpose(1, 0, 2)

    def by_columns(name, w):
        for j in range(w.shape[1] // UNIT):
            out[AT[name, j]] = rows(w[:, j * UNIT:(j + 1) * UNIT])

    def up(name, w):
        for j in range(UP):
            out[AT[name, j], :, :, 0:P] = rows(w[:, j * P:(j + 1) * P])
            out[AT[name, j], :, :, P:] = rows(w[:, FF + j * P:FF + (j + 1) * P])

    def down(name, w):
        for j in range(4 * len(GROUPS)):
            g, pair = j % len(GROUPS), j // len(GROUPS)
            out[AT[name, j], :, 0:GROUPS[g], :] = rows(w[g * KC * P:(g + 1) * KC * P, pair * UNIT:(pair + 1) * UNIT])

    for i in range(DEPTH):
        by_columns(f"ada{i}", a["w_ada"][i])
        for n in (1, 2):
            up(f"up{n}{i}", a[f"w_ffn{n}_in"][i])
            down(f"down{n}{i}", a[f"w_ffn{n}_out"][i])
        w = a["w_in"][i]
        w_in = np.zeros((D, 4 * P + 3 * CONV), np.float32)
        w_in[:, 0:QR + KVR] = w[:, 0:QR + KVR]
        w_in[:, QR + KVR + NOPE:QR + KVR + QK] = w[:, QR + KVR:QR + KVR + ROPE]
        w_in[:, 4 * P:] = w[:, QR + KVR + ROPE:]
        by_columns(f"in{i}", w_in)
        out[AT[f"uq{i}", 0]].reshape(P, -1)[:, 0:2 * HEADS * QK] = rows(a["w_uq"][i]).reshape(P, -1)
        out[AT[f"ukv{i}", 0]].reshape(P, -1)[:, 0:HEADS * (NOPE + VD)] = a["w_ukv"][i]
        by_columns(f"out{i}", a["w_out"][i])
    by_columns("mod", a["w_mod_2"][0])
    w, width = a["w_in_2"][0], MH * P
    hg = 4 * width + 4 * MH
    for j in range(4):
        out[AT["gate", 0], :, :, 32 * j:32 * j + MH] = rows(w[:, 4 * width + MH * j:4 * width + MH * (j + 1)])
    by_columns("in", np.concatenate([w[:, first(width, hg):first(width, hg) + width] for first in PROJECTIONS.values()], 1))
    by_columns("out", a["w_out_2"][0])
    up("up", a["w_up_2"][0])
    down("down", a["w_down_2"][0])
    return out


def feature_major(a):
    return np.ascontiguousarray(a.T.reshape(KC, P, -1).transpose(1, 0, 2))


def lay_out(a):
    return {
        "stream": lay_stream(a),
        "x_in": feature_major(np.concatenate([a["ctx"][0], a["x"][0]], 0)),
        "ctx2_in": feature_major(a["ctx_2"][0]),
        "params_in": lay_params(a),
        "consts_in": lay_consts(),
    }


def kernel(**inputs):
    import concourse.bacc as bacc
    from concourse.bass_utils import run_bass_kernel_spmd

    nc = bacc.Bacc("TRN2", target_bir_lowering=False, num_devices=1)
    arrays = lay_out({k: np.asarray(v) for k, v in inputs.items()})
    args = [nc.dram_tensor(n, v.shape, F32, kind="ExternalInput").ap() for n, v in arrays.items()]
    out = nc.dram_tensor("out", (P, KC, LAT), F32, kind="ExternalOutput").ap()
    build_program(nc, *args, out)
    result = run_bass_kernel_spmd(nc, [arrays], core_ids=[0])
    out = result.results[0]["out"]
    return np.ascontiguousarray(out.transpose(1, 0, 2).reshape(D, LAT).T)[None]
```
